# Optimizing a Trainium2 kernel written in Bass

```python
import jax, jax.numpy as jnp
from jax import lax
import numpy as np

D_MODEL = 1024
BATCH = 1
SEQ = 256
DEPTH = 2

CHUNK = 64
Q_BLOCK = 128

MLA_HEADS = 8
MLA_Q_LORA = 384
MLA_KV_LORA = 256
MLA_NOPE_DIM = 64
MLA_ROPE_DIM = 32
MLA_V_DIM = 64
ROPE_THETA = 10000.0

SWA_Q_HEADS = 8
SWA_KV_HEADS = 2
SWA_HEAD_DIM = 64
SWA_WINDOW = 128
SWA_WINDOW_CHUNKS = SWA_WINDOW // CHUNK

DENSE_FF = 2816
N_EXPERTS = 8
TOP_K = 2
EXPERT_FF = 3584
N_DENSE = (DEPTH + 1) // 2
N_MOE = DEPTH // 2

N_BRANCHES = 2
RMS_EPS = 1e-6
NEG_INF = -1e30

IN_SIZES = (
    MLA_Q_LORA,
    MLA_KV_LORA,
    MLA_ROPE_DIM,
    SWA_Q_HEADS * SWA_HEAD_DIM,
    SWA_KV_HEADS * SWA_HEAD_DIM,
    SWA_KV_HEADS * SWA_HEAD_DIM,
    N_BRANCHES * D_MODEL,
)
IN_COLS = sum(IN_SIZES)
IN_OFFSETS = [int(v) for v in np.cumsum(IN_SIZES)[:-1]]

kernel_name = "hybrid_mla_swa_sink_moe_streaming"

def rms_norm(x, g):
    xf = x.astype(jnp.float32)
    y = xf * lax.rsqrt(jnp.mean(xf * xf, axis=-1, keepdims=True) + RMS_EPS)
    return (y * g.astype(jnp.float32)).astype(x.dtype)

def rope_tables(seq_len):
    inv_freq = 1.0 / (ROPE_THETA ** (np.arange(0, MLA_ROPE_DIM, 2, dtype=np.float32) / MLA_ROPE_DIM))
    ang = np.arange(seq_len, dtype=np.float32)[:, None] * inv_freq[None, :]
    return jnp.asarray(np.cos(ang)), jnp.asarray(np.sin(ang))

def apply_rope(x, cos, sin):
    half = x.shape[-1] // 2
    x1, x2 = x[..., :half], x[..., half:]
    cos = cos.astype(x.dtype)
    sin = sin.astype(x.dtype)
    return jnp.concatenate([x1 * cos - x2 * sin, x1 * sin + x2 * cos], axis=-1)

def alibi_slopes(n_heads):
    return (2.0 ** (-8.0 * (np.arange(n_heads, dtype=np.float32) + 1.0) / n_heads)).astype(np.float32)

def mla_attention(q_lat, kv_lat, k_rope, g_qn, g_kvn, w_q_up, w_kv_up):
    B, S, _ = q_lat.shape
    cos, sin = rope_tables(S)
    q = (rms_norm(q_lat, g_qn) @ w_q_up).reshape(B, S, MLA_HEADS, MLA_NOPE_DIM + MLA_ROPE_DIM)
    q_nope = q[..., :MLA_NOPE_DIM]
    q_rope = apply_rope(q[..., MLA_NOPE_DIM:], cos[:, None, :], sin[:, None, :])
    kv = (rms_norm(kv_lat, g_kvn) @ w_kv_up).reshape(B, S, MLA_HEADS, MLA_NOPE_DIM + MLA_V_DIM)
    k_nope, v = kv[..., :MLA_NOPE_DIM], kv[..., MLA_NOPE_DIM:]
    k_rope = apply_rope(k_rope, cos, sin)
    scale = (MLA_NOPE_DIM + MLA_ROPE_DIM) ** -0.5
    outs = []
    for i in range(S // Q_BLOCK):
        qs, qe = i * Q_BLOCK, (i + 1) * Q_BLOCK
        s = (jnp.einsum('bqhd,bkhd->bhqk', q_nope[:, qs:qe], k_nope[:, :qe])
             + jnp.einsum('bqhr,bkr->bhqk', q_rope[:, qs:qe], k_rope[:, :qe]))
        s = s.astype(jnp.float32) * scale
        q_chunk = (qs + np.arange(Q_BLOCK)) // CHUNK
        k_chunk = np.arange(qe) // CHUNK
        mask = k_chunk[None, :] <= q_chunk[:, None]
        s = jnp.where(mask, s, NEG_INF)
        p = jax.nn.softmax(s, axis=-1).astype(v.dtype)
        outs.append(jnp.einsum('bhqk,bkhd->bqhd', p, v[:, :qe]))
    return jnp.concatenate(outs, axis=1).reshape(B, S, MLA_HEADS * MLA_V_DIM)

def shift_chunks(a, n):
    if n == 0:
        return a
    return jnp.concatenate([jnp.zeros_like(a[:, :n]), a[:, :-n]], axis=1)

def swa_attention(q, k, v, sinks):
    B, S, _ = q.shape
    NC = S // CHUNK
    W = SWA_WINDOW_CHUNKS
    G = SWA_Q_HEADS // SWA_KV_HEADS
    q = q.reshape(B, NC, CHUNK, SWA_KV_HEADS, G, SWA_HEAD_DIM)
    k = k.reshape(B, NC, CHUNK, SWA_KV_HEADS, SWA_HEAD_DIM)
    v = v.reshape(B, NC, CHUNK, SWA_KV_HEADS, SWA_HEAD_DIM)
    kb = jnp.concatenate([shift_chunks(k, W - 1 - w) for w in range(W)], axis=2)
    vb = jnp.concatenate([shift_chunks(v, W - 1 - w) for w in range(W)], axis=2)
    s = jnp.einsum('bcqkgd,bcjkd->bckgqj', q, kb).astype(jnp.float32) * (SWA_HEAD_DIM ** -0.5)
    qpos = np.arange(CHUNK)
    jpos = np.arange(W * CHUNK)
    dist = np.abs((W - 1) * CHUNK + qpos[:, None] - jpos[None, :]).astype(np.float32)
    slopes = alibi_slopes(SWA_Q_HEADS).reshape(SWA_KV_HEADS, G)
    s = s - slopes[:, :, None, None] * dist
    valid = (np.arange(NC)[:, None] - (W - 1) + jpos[None, :] // CHUNK) >= 0
    s = jnp.where(valid[None, :, None, None, None, :], s, NEG_INF)
    sink = sinks.astype(jnp.float32).reshape(SWA_KV_HEADS, G)[None, None, :, :, None, None]
    m = jnp.maximum(jnp.max(s, axis=-1, keepdims=True), sink)
    p = jnp.exp(s - m)
    p = (p / (jnp.sum(p, axis=-1, keepdims=True) + jnp.exp(sink - m))).astype(v.dtype)
    o = jnp.einsum('bckgqj,bcjkd->bcqkgd', p, vb)
    return o.reshape(B, S, SWA_Q_HEADS * SWA_HEAD_DIM)

def swiglu(h, w_gate, w_up, w_down):
    return (jax.nn.silu(h @ w_gate) * (h @ w_up)) @ w_down

def moe_swiglu(h, w_router, w_gate, w_up, w_down):
    logits = (h @ w_router).astype(jnp.float32)
    top_vals, top_idx = lax.top_k(logits, TOP_K)
    top_w = jax.nn.softmax(top_vals, axis=-1)
    combine = jnp.sum(jax.nn.one_hot(top_idx, N_EXPERTS, dtype=jnp.float32) * top_w[..., None], axis=-2)
    combine = combine.astype(h.dtype)
    y = jnp.zeros_like(h)
    for e in range(N_EXPERTS):
        y = y + combine[..., e:e + 1] * swiglu(h, w_gate[e], w_up[e], w_down[e])
    return y

def setup_inputs(seed: int = 0) -> dict:
    key = jax.random.key(seed)
    ks = jax.random.split(key, 32)
    f32 = jnp.float32

    def nrm(k, shape, fan_in):
        return jax.random.normal(k, shape, f32) * (fan_in ** -0.5)

    def gain(k, shape):
        return 1.0 + 0.1 * jax.random.normal(k, shape, f32)

    return {
        "x": jax.random.normal(ks[0], (BATCH, SEQ, D_MODEL), f32),
        "g_attn_norm": gain(ks[1], (DEPTH, D_MODEL)),
        "w_in": nrm(ks[2], (DEPTH, D_MODEL, IN_COLS), D_MODEL),
        "b_gate": 0.1 * jax.random.normal(ks[3], (DEPTH, N_BRANCHES * D_MODEL), f32),
        "g_q_norm": gain(ks[4], (DEPTH, MLA_Q_LORA)),
        "w_q_up": nrm(ks[5], (DEPTH, MLA_Q_LORA, MLA_HEADS * (MLA_NOPE_DIM + MLA_ROPE_DIM)), MLA_Q_LORA),
        "g_kv_norm": gain(ks[6], (DEPTH, MLA_KV_LORA)),
        "w_kv_up": nrm(ks[7], (DEPTH, MLA_KV_LORA, MLA_HEADS * (MLA_NOPE_DIM + MLA_V_DIM)), MLA_KV_LORA),
        "sinks": jax.random.normal(ks[8], (DEPTH, SWA_Q_HEADS), f32),
        "w_br_mla": nrm(ks[9], (DEPTH, MLA_HEADS * MLA_V_DIM, D_MODEL), MLA_HEADS * MLA_V_DIM),
        "w_br_swa": nrm(ks[10], (DEPTH, SWA_Q_HEADS * SWA_HEAD_DIM, D_MODEL), SWA_Q_HEADS * SWA_HEAD_DIM),
        "w_out": nrm(ks[11], (DEPTH, D_MODEL, D_MODEL), D_MODEL),
        "g_ffn_norm": gain(ks[12], (DEPTH, D_MODEL)),
        "dense_w_gate": nrm(ks[13], (N_DENSE, D_MODEL, DENSE_FF), D_MODEL),
        "dense_w_up": nrm(ks[14], (N_DENSE, D_MODEL, DENSE_FF), D_MODEL),
        "dense_w_down": nrm(ks[15], (N_DENSE, DENSE_FF, D_MODEL), DENSE_FF),
        "w_router": nrm(ks[16], (N_MOE, D_MODEL, N_EXPERTS), D_MODEL),
        "moe_w_gate": nrm(ks[17], (N_MOE, N_EXPERTS, D_MODEL, EXPERT_FF), D_MODEL),
        "moe_w_up": nrm(ks[18], (N_MOE, N_EXPERTS, D_MODEL, EXPERT_FF), D_MODEL),
        "moe_w_down": nrm(ks[19], (N_MOE, N_EXPERTS, EXPERT_FF, D_MODEL), EXPERT_FF),
        "g_final": gain(ks[20], (D_MODEL,)),
    }

def reference(x, g_attn_norm, w_in, b_gate, g_q_norm, w_q_up, g_kv_norm, w_kv_up, sinks,
              w_br_mla, w_br_swa, w_out, g_ffn_norm, dense_w_gate, dense_w_up, dense_w_down,
              w_router, moe_w_gate, moe_w_up, moe_w_down, g_final):
    for l in range(DEPTH):
        h = rms_norm(x, g_attn_norm[l])
        proj = h @ w_in[l]
        q_lat, kv_lat, k_rope, q_swa, k_swa, v_swa, gate_pre = jnp.split(proj, IN_OFFSETS, axis=-1)
        o_mla = mla_attention(q_lat, kv_lat, k_rope, g_q_norm[l], g_kv_norm[l], w_q_up[l], w_kv_up[l])
        o_swa = swa_attention(q_swa, k_swa, v_swa, sinks[l])
        gates = jax.nn.sigmoid((gate_pre + b_gate[l]).astype(jnp.float32)).astype(x.dtype)
        g_mla, g_swa = gates[..., :D_MODEL], gates[..., D_MODEL:]
        merged = g_mla * (o_mla @ w_br_mla[l]) + g_swa * (o_swa @ w_br_swa[l])
        x = x + merged @ w_out[l]
        h = rms_norm(x, g_ffn_norm[l])
        if l % 2 == 0:
            i = l // 2
            x = x + swiglu(h, dense_w_gate[i], dense_w_up[i], dense_w_down[i])
        else:
            i = l // 2
            x = x + moe_swiglu(h, w_router[i], moe_w_gate[i], moe_w_up[i], moe_w_down[i])
    return rms_norm(x, g_final)


_drawn_inputs = setup_inputs


def setup_inputs(seed=0):
    import zlib

    import numpy as np

    out = dict(_drawn_inputs(seed))
    spreads = {}
    factors = {'g_q_norm': 3.485, 'sinks': 2.873}
    for name, (base, spread) in spreads.items():
        noise = np.random.default_rng([zlib.crc32(name.encode()), seed]).standard_normal(out[name].shape)
        drawn = base * np.exp(spread * noise) if base else spread * noise
        out[name] = __import__('jax').numpy.asarray(drawn.astype(out[name].dtype))
    for name, factor in factors.items():
        out[name] = (out[name] * factor).astype(out[name].dtype)
    return out
```

```python
from contextlib import ExitStack

import concourse.bass as bass
from concourse import mybir

F32 = mybir.dt.float32
F32R = mybir.dt.float32r
I32 = mybir.dt.int32
ALU = mybir.AluOpType
ACT = mybir.ActivationFunctionType
AX = mybir.AxisListType.X

P = 128
D = 1024
SEQ = 256
NB = SEQ // P
KD = D // P
DEPTH = 2
CHUNK = 64
HEADS = 8
NOPE, ROPE, VD = 64, 32, 64
QK = NOPE + ROPE
HALF = ROPE // 2
Q_LORA, KV_LORA = 384, 256
KQ, KKV = Q_LORA // P, KV_LORA // P
SW_KV, SW_D = 2, 64
FF = 2816
NE = 8
EFF = 3584
EPS = 1e-6
MLA_SCALE = float(QK) ** -0.5
SWA_SCALE = float(SW_D) ** -0.5
SLOPES = [2.0 ** (-8.0 * (h + 1.0) / HEADS) for h in range(HEADS)]

C_KV = Q_LORA
C_KR = C_KV + KV_LORA
C_QS = C_KR + ROPE
C_KS = C_QS + HEADS * SW_D
C_VS = C_KS + SW_KV * SW_D
C_GATE = C_VS + SW_KV * SW_D
PROJ = [(0, 512), (512, 512), (1024, C_GATE - 1024)]

UNIT = 2048
R = 6
S = 3
N = 512

def group_at(j):
    return 0 if j == 0 else 4 + 6 * (j - 1)


def down_at(j, groups):
    return 8 + 6 * j if j < groups - 1 else 4 + 6 * (groups - 1)


EG = EFF // N
EU = 6 * EG
DG = -(-FF // N)
assert EU % R == 0 and EU % S == 0

K_COS = 0
K_SIN = K_COS + NB * HALF
K_MASK = K_SIN + NB * HALF
K_DIST = K_MASK + SEQ
K_IDENT = K_DIST + SEQ
K_BEFORE = K_IDENT + P
K_IOTA = K_BEFORE + P
K_LOWER = K_IOTA + SEQ
K_ALL = K_LOWER + NE * NE

G_LAYER = KD + KQ + KKV + KD
G_ATTN, G_Q, G_KV, G_FFN = 0, KD, KD + KQ, KD + KQ + KKV

FILLS = []
for kind in range(2):
    for b in range(NB):
        per = 4 // (b + 1)
        order = list(range(HEADS)) if kind == 0 else list(range(0, HEADS, 2)) + list(range(1, HEADS, 2))
        FILLS += [(kind, b, order[h:h + per]) for h in range(0, HEADS, per)]
NF = len(FILLS)
LAST = [max(f for f, x in enumerate(FILLS) if x[:2] == (kind, b)) for kind in range(2) for b in range(NB)]
QT_FILLS = 11


def trunk(nc, x, g_attn_norm, w_in, b_gate, g_q_norm, w_q_up, g_kv_norm, w_kv_up, sinks, w_br_mla,
          w_br_swa, w_out, g_ffn_norm, dense_w_gate, dense_w_up, dense_w_down, w_router, moe_w_gate,
          moe_w_up, moe_w_down, g_final, consts, out):
    units = []
    at = {}

    def rows(w, k0, kt, c0, n):
        units.append((w[k0 * P:(k0 + kt) * P, c0:c0 + n].rearrange("(k p) n -> p k n", p=P), kt, n))

    for l in range(DEPTH):
        at[l, "in"] = len(units)
        for c0, n in PROJ:
            rows(w_in[l], 0, 4, c0, n)
            rows(w_in[l], 4, 4, c0, n)
        at[l, "gate0"] = len(units)
        rows(w_in[l], 0, 4, C_GATE, N)
        rows(w_in[l], 4, 4, C_GATE, N)
        at[l, "q"] = len(units)
        for i in range(2):
            rows(w_q_up[l], 0, KQ, i * 4 * QK, 4 * QK)
        at[l, "kv"] = len(units)
        rows(w_kv_up[l], 0, KKV, 0, D)
        at[l, "gate"] = len(units)
        for g in range(1, 4):
            rows(w_in[l], 0, 4, C_GATE + g * N, N)
            rows(w_in[l], 4, 4, C_GATE + g * N, N)
        at[l, "br"] = len(units)
        for n in range(2):
            rows(w_br_mla[l], 0, 4, n * N, N)
            rows(w_br_swa[l], 0, 4, n * N, N)
        at[l, "out"] = len(units)
        for n in range(2):
            rows(w_out[l], 0, 4, n * N, N)
            rows(w_out[l], 4, 4, n * N, N)
        at[l, "ffn"] = len(units)
        if l == 0:
            def down(j):
                for k in range(4 * j, min(4 * j + 4, FF // P), 2):
                    rows(dense_w_down[0], k, 2, 0, D)

            for j in range(DG):
                n = min(N, FF - j * N)
                for w in (dense_w_gate, dense_w_up):
                    rows(w[0], 0, 4, j * N, n)
                    rows(w[0], 4, 4, j * N, n)
                if j:
                    down(j - 1)
            down(DG - 1)
    UM = len(units)
    assert UM == at[1, "ffn"]

    with ExitStack() as ctx:
        used = [(nc.sbuf_base + 31) // 32 * 32]

        def place(name, shape, dt, offset=None):
            size = 4
            for s in shape[1:]:
                size *= s
            if offset is None:
                offset = used[0]
                used[0] += (size + 31) // 32 * 32
            assert offset + size <= nc.sbuf_usable_end, (name, offset + size)
            return nc.alloc_sbuf_tensor_at(name, shape, dt, offset=offset)

        def sem(name):
            return ctx.enter_context(nc.semaphore(name))

        raw = place("raw", [P, R, UNIT], F32)
        whi = place("whi", [P, S, UNIT], F32R)
        wlo = place("wlo", [P, S, UNIT], F32R)
        xs = place("xs", [P, NB, D], F32)
        o_xn = used[0]
        xn = place("xn", [P, NB, D], F32)
        sqT = place("sqT", [P, 4, SEQ], F32, o_xn)
        skT = place("skT", [P, SW_KV, SEQ], F32, o_xn + 4096)
        kdup = place("kdup", [P, NB, SW_KV, 2, SW_D], F32, o_xn + 6144)
        hTh = place("hTh", [P, KD, SEQ], F32R)
        hTl = place("hTl", [P, KD, SEQ], F32R)
        o_o = used[0]
        oTh = place("oTh", [P, 2, 4, SEQ], F32R)
        oTl = place("oTl", [P, 2, 4, SEQ], F32R)
        latTh = place("latTh", [P, KQ + KKV, SEQ], F32R, o_o)
        latTl = place("latTl", [P, KQ + KKV, SEQ], F32R, o_o + 8192)
        sg = place("sg", [P, 2, N], F32, o_o)
        av = place("av", [P, 2, N], F32, o_o + 4096)
        aTh = place("aTh", [P, 2, 4, P], F32R, o_o + 8192)
        aTl = place("aTl", [P, 2, 4, P], F32R, o_o + 12288)
        o_pj = used[0]
        pj = place("pj", [P, NB, C_GATE], F32)
        mg = place("mg", [P, NB, D], F32, o_pj)
        o_g = used[0]
        gates = place("gates", [P, 4, NB, N], F32)
        qn = place("qn", [P, NB, HEADS, QK], F32, o_g + 4096)
        kn = place("kn", [P, NB, HEADS, QK], F32, o_g + 4096 + 6144)
        heTh = place("heTh", [P, KD, P], F32R, o_g)
        heTl = place("heTl", [P, KD, P], F32R, o_g + 4096)
        oe = place("oe", [P, D], F32, o_g + 8192)
        pick = place("pick", [P, NB, P], F32, o_g + 12288)
        cw = place("cw", [P, NB, P], F32, o_g + 13312)
        cwT = place("cwT", [P, SEQ], F32, o_g + 14336)
        gout = place("gout", [P, NB, D], F32, o_g)
        qT = place("qT", [P, HEADS, SEQ], F32)
        o_kT = used[0]
        kT = place("kT", [P, HEADS, SEQ], F32)
        gfin = place("gfin", [P, D], F32, o_kT)
        bg = place("bg", [P, 2, N], F32)
        o_sx = used[0]
        sx = place("sx", [P, 2, N], F32)
        rt = place("rt", [P, 4, NB * HEADS * HALF], F32, o_sx)
        pT = place("pT", [P, 2, N], F32)
        cst = place("cst", [P, K_ALL], F32)
        gcol = place("gcol", [P, DEPTH * G_LAYER], F32)
        sk = place("sk", [P, DEPTH, HEADS], F32)
        ones = place("ones", [P, P], F32)
        krt = place("krt", [P, 4, NB * HALF], F32)
        st = place("st", [P, 16], F32)
        eps = place("eps", [P, 1], F32)
        mx = place("mx", [P, 2, 4], F32)
        nm = place("nm", [P, 2, 4], F32)
        sink_d = place("sink_d", [P, 2, 4], F32)
        sink_e = place("sink_e", [P, 2, 4], F32)
        sums = place("sums", [P, 2, 4], F32)
        rsum = place("rsum", [P, 2, 4], F32)
        o_r = o_sx
        wr = place("wr", [P, KD, NE], F32, o_kT + 4096)
        wrh = place("wrh", [P, KD, NE], F32R, o_kT + 4096 + 256)
        wrl = place("wrl", [P, KD, NE], F32R, o_kT + 4096 + 512)
        lg = place("lg", [P, NB, NE], F32, o_r)
        above = place("above", [P, NB, NE, NE], F32, o_r + 64)
        ties = place("ties", [P, NB, NE, NE], F32, o_r + 576)
        rank = place("rank", [P, NB, NE], F32, o_r + 1088)
        mask = place("mask", [P, NB, NE], F32, o_r + 1152)
        lmax = place("lmax", [P, NB], F32, o_r + 1216)
        pe8 = place("pe8", [P, NB, NE], F32, o_r + 1248)
        psum8 = place("psum8", [P, NB], F32, o_r + 1312)
        comb = place("comb", [P, NB, NE], F32, o_r + 1344)
        pos = place("pos", [P, NB, NE], F32, o_r + 1408)
        most = place("most", [P, 1], F32, o_r + 1472)
        flag = place("flag", [P, 1], I32, o_r + 1504)
        posc = place("posc", [P, NB], F32, o_r + 1536)
        combc = place("combc", [P, NB], F32, o_r + 1568)
        grow = place("grow", [P, P], F32, o_r + 2048)

        A = [ctx.enter_context(nc.psum_tensor(f"A{i}", [P, N], F32)) for i in range(4)]
        T = [ctx.enter_context(nc.psum_tensor(f"T{i}", [P, N], F32)) for i in range(2)]
        DN = [ctx.enter_context(nc.psum_tensor(f"DN{i}", [P, N], F32)) for i in range(2)]

        ident = cst[:, K_IDENT:K_IDENT + P]
        before = cst[:, K_BEFORE:K_BEFORE + P]

        raw_landed = [sem(f"raw_landed{i}") for i in range(R)]
        hi_done = sem("hi_done")
        lo_done = sem("lo_done")
        unit_used = sem("unit_used")
        const_landed = sem("const_landed")
        gain_landed = sem("gain_landed")
        x_landed = sem("x_landed")
        sink_landed = sem("sink_landed")
        router_landed = sem("router_landed")
        gfin_landed = sem("gfin_landed")
        bg_landed = [[sem(f"bg_landed{l}_{i}") for i in range(4)] for l in range(DEPTH)]
        out_landed = sem("out_landed")
        ones_set = sem("ones_set")
        gain_T = sem("gain_T")
        gain_done = sem("gain_done")
        act_own = sem("act_own")
        dve_own = sem("dve_own")

        def layered(name):
            return [sem(f"{name}{l}") for l in range(DEPTH)]

        norm_root = [sem(f"norm_root{n}") for n in range(5)]
        norm_rows = [sem(f"norm_rows{n}") for n in range(5)]
        norm_T = [sem(f"norm_T{n}") for n in range(4)]
        norm_hi = [sem(f"norm_hi{n}") for n in range(4)]
        norm_lo = [sem(f"norm_lo{n}") for n in range(4)]
        proj_act, proj_dve = layered("proj_act"), layered("proj_dve")
        gate_added, gate_ready = layered("gate_added"), layered("gate_ready")
        lat_root, lat_rows = layered("lat_root"), layered("lat_rows")
        lat_T, lat_hi, lat_lo = layered("lat_T"), layered("lat_hi"), layered("lat_lo")
        up_act, up_dve = layered("up_act"), layered("up_dve")
        rope_done, kdup_done = layered("rope_done"), layered("kdup_done")
        qk_T, qk_act, qk_dve = layered("qk_T"), layered("qk_act"), layered("qk_dve")
        scored, masked, max_ready = layered("scored"), layered("masked"), layered("max_ready")
        exp_done, probs_ready = layered("exp_done"), layered("probs_ready")
        probs_T, probs_T_out = layered("probs_T"), layered("probs_T_out")
        pv_done, o_hi, o_lo = layered("pv_done"), layered("o_hi"), layered("o_lo")
        br_free, merged = layered("br_free"), layered("merged")
        mg_T, mg_hi, mg_lo = layered("mg_T"), layered("mg_hi"), layered("mg_lo")
        x_added = layered("x_added")
        silu_done, ff_ready = layered("silu_done"), layered("ff_ready")
        ff_T, ff_hi, ff_lo = layered("ff_T"), layered("ff_hi"), layered("ff_lo")
        down_done, down_added = sem("down_done"), sem("down_added")
        wr_hi, wr_lo = sem("wr_hi"), sem("wr_lo")
        logits_done, mask_ready, counted = sem("logits_done"), sem("mask_ready"), sem("counted")
        lmax_ready, lexp_done = sem("lmax_ready"), sem("lexp_done")
        routed, selected = sem("routed"), sem("selected")
        picked, gathered = sem("picked"), sem("gathered")
        he_hi, he_lo = sem("he_hi"), sem("he_lo")
        cw_T, cw_out = sem("cw_T"), sem("cw_out")
        oe_full, oe_act, oe_dve, scattered = sem("oe_full"), sem("oe_act"), sem("oe_dve"), sem("scattered")
        last_full, last_added = sem("last_full"), sem("last_added")

        X_DENSE = 4 + 4 * DG

        def times(e, per):
            return 0 if e is None else e * per

        def split_hi(act, u, e=None):
            n = UNIT if u >= UM else units[u][1] * units[u][2]
            act.wait_ge(raw_landed[u % R], 16 * (u // R + 1) + times(e, 16 * EU // R))
            if u >= S:
                act.wait_ge(unit_used, u - S + 1 + times(e, EU))
            nc.scalar.activation(whi[:, u % S, :n], raw[:, u % R, :n], ACT.Copy).then_inc(hi_done, 1)

        def split_lo(dve, u, e=None):
            n = UNIT if u >= UM else units[u][1] * units[u][2]
            dve.wait_ge(hi_done, u + 1 + times(e, EU))
            nc.vector.tensor_tensor(wlo[:, u % S, :n], raw[:, u % R, :n],
                                    whi[:, u % S, :n].bitcast(F32), ALU.subtract).then_inc(lo_done, 1)

        class Lead:

            def __init__(self, eng, split, first, last, e=None):
                self.eng, self.split, self.next, self.last, self.e = eng, split, first, last, e

            def to(self, u):
                while self.next < min(u, self.last):
                    self.split(self.eng, self.next, self.e)
                    self.next += 1

        def split_tile(u, kk, n, c0=0, width=None):
            a = kk * n + c0
            b = a + (n if width is None else width)
            return whi[:, u % S, a:b], wlo[:, u % S, a:b]

        def product(o, hi, lo, wh, wl, start, stop):
            nc.tensor.matmul(o, hi, wh, start=start, stop=False)
            nc.tensor.matmul(o, hi, wl, start=False, stop=False)
            return nc.tensor.matmul(o, lo, wh, start=False, stop=stop)

        def vm(b, n):
            return pj[:, b, n * 4 * VD:(n + 1) * 4 * VD].rearrange("p (h d) -> p h d", h=4)

        def qk_target(i):
            if i < 4:
                return qT[0:QK, 2 * i:2 * i + 2, :].rearrange("p h t -> p (h t)"), QK, N, 1.0
            if i < 8:
                return kT[0:QK, 2 * i - 8:2 * i - 6, :].rearrange("p h t -> p (h t)"), QK, N, 1.0
            if i < 10:
                return sqT[:, 2 * i - 16:2 * i - 14, :].rearrange("p h t -> p (h t)"), P, N, SWA_SCALE
            return skT[:].rearrange("p h t -> p (h t)"), P, N, 1.0

        block = ctx.enter_context(nc.Block())

        @block.sync
        def _(sp):
            sp.dma_start(xs[:], x[0].rearrange("(b p) d -> p b d", p=P)).then_inc(x_landed, 16)
            sp.dma_start(cst[:], consts).then_inc(const_landed, 16)
            for l in range(DEPTH):
                r = l * G_LAYER
                for g, k, o in ((g_attn_norm, KD, G_ATTN), (g_q_norm, KQ, G_Q), (g_kv_norm, KKV, G_KV),
                                (g_ffn_norm, KD, G_FFN)):
                    sp.dma_start(grow[r + o:r + o + k, :], g[l].rearrange("(k p) -> k p", p=P)
                                 ).then_inc(gain_landed, 16)
            sp.dma_start(sk[:], sinks.rearrange("(a l) h -> a l h", a=1).broadcast_to([P, DEPTH, HEADS])
                         ).then_inc(sink_landed, 16)

            def load(u, dst_u, src, kt, n, e=None):
                if u >= R:
                    sp.wait_ge(lo_done, u - R + 1 + times(e, EU))
                sp.dma_start(raw[:, dst_u, :kt * n].rearrange("p (k n) -> p k n", k=kt), src
                             ).then_inc(raw_landed[dst_u], 16)

            for u, (src, kt, n) in enumerate(units):
                load(u, u % R, src, kt, n)

            def expert_loads(base, e):
                gate = moe_w_gate[0, bass.ds(e, 1)].rearrange("a (k p) n -> p (a k) n", p=P)
                up = moe_w_up[0, bass.ds(e, 1)].rearrange("a (k p) n -> p (a k) n", p=P)
                dn = moe_w_down[0, bass.ds(e, 1)].rearrange("a (k p) n -> p (a k) n", p=P)
                i = 0

                def take(src, kt, n):
                    nonlocal i
                    load(base + i, (base + i) % R, src, kt, n, e)
                    i += 1

                for j in range(EG + 1):
                    if j < EG:
                        for w in (gate, up):
                            take(w[:, 0:4, j * N:(j + 1) * N], 4, N)
                            take(w[:, 4:8, j * N:(j + 1) * N], 4, N)
                    if j:
                        take(dn[:, 4 * j - 4:4 * j - 2, :], 2, D)
                        take(dn[:, 4 * j - 2:4 * j, :], 2, D)

            with sp.Fori(0, NE) as e:
                expert_loads(UM, e)
            sp.wait_ge(routed, 1)
            more = sp.value_load(flag[0:1, 0:1], min_val=0, max_val=1)
            with sp.If(more > 0):
                with sp.Fori(0, NE) as e:
                    expert_loads(UM + NE * EU, e)
            for b in range(NB):
                sp.wait_ge(norm_rows[4], b + 1)
                sp.dma_start(out[0, b * P:(b + 1) * P, :], gout[:, b, :]).then_inc(out_landed, 16)
            sp.wait_ge(out_landed, 16 * NB)

        @block.scalar
        def _(act):
            own = [0]

            def done(ins):
                own[0] += 1
                ins.then_inc(act_own, 1)
                return own[0]

            lead = Lead(act, split_hi, 0, UM)

            def bias_chunk(l, g):
                act.dma_start(bg[:, g % 2, :], b_gate[l:l + 1, g * N:(g + 1) * N].broadcast_to([P, N])
                              ).then_inc(bg_landed[l][g], 16)

            def root(n):
                for b in range(NB):
                    v = done(nc.scalar.activation(xn[:, b, :], xs[:, b, :], ACT.Square, accum_out=st[:, b:b + 1]))
                act.wait_ge(act_own, v)
                nc.scalar.activation(st[:, 2:4], st[:, 0:2], ACT.Sqrt, scale=1.0 / D, bias=eps[:]
                                     ).then_inc(norm_root[n], 1)

            def norm_high(n, gains):
                for i in range(4):
                    act.wait_ge(norm_T[n], i + 1)
                    for kk in range(2):
                        k = 2 * i + kk
                        nc.scalar.activation(hTh[:, k, :], T[i % 2][:, kk * SEQ:(kk + 1) * SEQ], ACT.Copy,
                                             scale=gcol[:, gains + k:gains + k + 1]).then_inc(norm_hi[n], 1)

            act.wait_ge(ones_set, 2)
            act.wait_ge(x_landed, 16)
            for l in range(DEPTH):
                if l:
                    lead.to(at[l, "in"] + 2)
                    act.wait_ge(x_added[0], X_DENSE)
                root(l)
                if l == 0:
                    act.wait_ge(gain_T, 1)
                    nc.scalar.activation(gcol[:], T[0][:, 0:DEPTH * G_LAYER], ACT.Copy).then_inc(gain_done, 1)
                    act.wait_ge(gain_done, 1)
                bias_chunk(l, 0)
                bias_chunk(l, 1)
                lead.to(at[l, "in"] + 2)
                norm_high(l, l * G_LAYER + G_ATTN)
                for g, (c0, n) in enumerate(PROJ):
                    u = at[l, "in"] + 2 * g + 1
                    lead.to(u + 3)
                    act.wait_ge(unit_used, u + 1)
                    nc.scalar.activation(pj[:, 0, c0:c0 + n], A[2 * (g % 2)][:, :n], ACT.Copy
                                         ).then_inc(proj_act[l], 1)
                act.wait_ge(proj_act[l], 3)
                act.wait_ge(proj_dve[l], 3)
                for b in range(NB):
                    done(nc.scalar.activation(xn[:, b, 0:Q_LORA], pj[:, b, 0:Q_LORA], ACT.Square,
                                              accum_out=st[:, 4 + b:5 + b]))
                    done(nc.scalar.activation(xn[:, b, Q_LORA:C_KR], pj[:, b, C_KV:C_KR], ACT.Square,
                                              accum_out=st[:, 6 + b:7 + b]))
                act.wait_ge(act_own, own[0])
                nc.scalar.activation(st[:, 8:10], st[:, 4:6], ACT.Sqrt, scale=1.0 / Q_LORA, bias=eps[:]
                                     ).then_inc(lat_root[l], 1)
                nc.scalar.activation(st[:, 10:12], st[:, 6:8], ACT.Sqrt, scale=1.0 / KV_LORA, bias=eps[:]
                                     ).then_inc(lat_root[l], 1)
                for r in range(2):
                    nc.scalar.activation(kdup[:, :, :, r, :],
                                         pj[:, :, C_KS:C_VS].rearrange("p b (k d) -> p b k d", k=SW_KV),
                                         ACT.Copy).then_inc(kdup_done[l], 1)
                lead.to(at[l, "gate0"] + 4)
                for i in range(3):
                    act.wait_ge(lat_T[l], i + 1)
                    for kk in range(2 if i < 2 else 1):
                        k = 2 * i + kk
                        c = l * G_LAYER + G_Q + k
                        nc.scalar.activation(latTh[:, k, :], T[i % 2][:, kk * SEQ:(kk + 1) * SEQ], ACT.Copy,
                                             scale=gcol[:, c:c + 1]).then_inc(lat_hi[l], 1)
                for i in range(2):
                    u = at[l, "q"] + i
                    lead.to(u + 3)
                    act.wait_ge(unit_used, u + 1)
                    nc.scalar.activation(qn[:, 0, 4 * i:4 * i + 4, :], [A, DN][i][0][:, :4 * QK], ACT.Copy
                                         ).then_inc(up_act[l], 1)
                lead.to(at[l, "kv"] + 3)
                act.wait_ge(unit_used, at[l, "kv"] + 1)
                for n in range(2):
                    kv = A[n][:].rearrange("p (h c) -> p h c", h=4)
                    nc.scalar.activation(kn[:, 0, 4 * n:4 * n + 4, 0:NOPE], kv[:, :, 0:NOPE], ACT.Copy
                                         ).then_inc(up_act[l], 1)
                    nc.scalar.activation(vm(0, n), kv[:, :, NOPE:], ACT.Copy).then_inc(up_act[l], 1)
                for i in range(0, QT_FILLS, 2):
                    act.wait_ge(qk_T[l], i + 1)
                    dst, p, w, scale = qk_target(i)
                    nc.scalar.activation(dst, T[0][0:p, 0:w], ACT.Copy, scale=scale).then_inc(qk_act[l], 1)

                def exps(f):
                    kind, b, heads = FILLS[f]
                    w = P * (b + 1)
                    act.wait_ge(max_ready[l], f + 1)
                    if kind:
                        done(nc.scalar.activation(sink_e[:, f % 2, :len(heads)], sink_d[:, f % 2, :len(heads)],
                                                  ACT.Exp))
                    for i in range(len(heads)):
                        s = sx[:, f % 2, i * w:(i + 1) * w]
                        nc.scalar.activation(s, s, ACT.Exp, bias=nm[:, f % 2, i:i + 1],
                                             scale=1.0 if kind else MLA_SCALE,
                                             accum_out=sums[:, f % 2, i:i + 1]).then_inc(exp_done[l], 1)

                def probs_out(f):
                    act.wait_ge(probs_T[l], f + 1)
                    if f >= 2:
                        act.wait_ge(pv_done[l], f - 1)
                    nc.scalar.activation(pT[:, f % 2, :], T[f % 2][:], ACT.Copy).then_inc(probs_T_out[l], 1)

                def o_high(i):
                    kind, b = i // NB, i % NB
                    act.wait_ge(pv_done[l], LAST[i] + 1)
                    nc.scalar.activation(oTh[:, kind, :, b * P:(b + 1) * P],
                                         DN[b][:].rearrange("p (j t) -> p j t", j=4), ACT.Copy
                                         ).then_inc(o_hi[l], 1)

                for f in range(NF):
                    lead.to(at[l, "gate"] + min(f, 5) + 3)
                    exps(f)
                    if f:
                        probs_out(f - 1)
                    if f - 2 in LAST:
                        o_high(LAST.index(f - 2))
                    if f == 0:
                        act.wait_ge(gate_added[l], 2)
                        bias_chunk(l, 2)
                    if f == 3:
                        act.wait_ge(gate_added[l], 4)
                        bias_chunk(l, 3)
                probs_out(NF - 1)
                o_high(3)
                act.wait_ge(gate_added[l], 8)
                for n in range(2):
                    for b in range(NB):
                        for h in range(2):
                            g = gates[:, 2 * h + n, b, :]
                            nc.scalar.activation(g, g, ACT.Sigmoid).then_inc(gate_ready[l], 1)
                lead.to(at[l, "br"] + 4 + 2)
                for i in range(4):
                    act.wait_ge(mg_T[l], i + 1)
                    nc.scalar.activation(hTh[:, 2 * i:2 * i + 2, :], T[i % 2][:].rearrange("p (k t) -> p k t", k=2),
                                         ACT.Copy).then_inc(mg_hi[l], 1)
                lead.to(at[l, "ffn"] + 2)
                act.wait_ge(x_added[l], 4)
                root(2 + l)
                norm_high(2 + l, l * G_LAYER + G_FFN)
                if l == 0:
                    u0 = at[0, "ffn"]
                    for j in range(DG + 1):
                        n = min(N, FF - j * N)
                        u = u0 + group_at(j)
                        lead.to(u + (4 if j < DG else 2))
                        if j < DG:
                            act.wait_ge(unit_used, u + 2)
                            for b in range(NB):
                                if j:
                                    act.wait_ge(ff_ready[0], NB * (j - 1) + b + 1)
                                nc.scalar.activation(sg[:, b, :n], A[b][:, :n], ACT.Silu
                                                     ).then_inc(silu_done[0], 1)
                        if j:
                            m = min(N, FF - (j - 1) * N)
                            for b in range(NB):
                                q = NB * (j - 1) + b
                                act.wait_ge(ff_T[0], q + 1)
                                nc.scalar.activation(aTh[:, b, :m // P, :], T[b][:, :m].rearrange("p (k t) -> p k t", t=P),
                                                     ACT.Copy).then_inc(ff_hi[0], 1)

            act.wait_ge(router_landed, 16)
            nc.scalar.activation(wrh[:], wr[:], ACT.Copy).then_inc(wr_hi, 1)
            act.wait_ge(lmax_ready, 1)
            for b in range(NB):
                nc.scalar.activation(pe8[:, b, :], lg[:, b, :], ACT.Exp, bias=lmax[:, b:b + 1]
                                     ).then_inc(lexp_done, 1)

            def tokens_high(i, n, e):
                act.wait_ge(gathered, 2 * n + i + 1 + e * 2)
                for kk in range(4):
                    k = 4 * i + kk
                    c = G_LAYER + G_FFN + k
                    nc.scalar.activation(heTh[:, k, :], T[i][:, kk * P:(kk + 1) * P], ACT.Copy,
                                         scale=gcol[:, c:c + 1]).then_inc(he_hi, 1)

            def expert(base, n, e, following):
                ahead = Lead(act, split_hi, base, base + EU + (S if following else 0), e)
                ahead.next += S
                for j in range(EG + 1):
                    u = base + group_at(j)
                    ahead.to(u + (4 if j < EG else 2))
                    if j < EG:
                        act.wait_ge(unit_used, u + 2 + e * EU)
                        if j >= 2:
                            act.wait_ge(ff_ready[1], EG * n + j - 1 + e * EG)
                        nc.scalar.activation(sg[:, j % 2, :], A[j % 2][:], ACT.Silu).then_inc(silu_done[1], 1)
                    if j == 0:
                        act.wait_ge(cw_T, n + 1 + e)
                        nc.scalar.activation(cwT[:], T[0][:, :SEQ], ACT.Copy).then_inc(cw_out, 1)
                    else:
                        act.wait_ge(ff_T[1], EG * n + j + e * EG)
                        nc.scalar.activation(aTh[:, (j - 1) % 2], T[(j - 1) % 2][:].rearrange("p (k t) -> p k t", k=4),
                                             ACT.Copy).then_inc(ff_hi[1], 1)
                    if following and j >= EG - 1:
                        if j < EG:
                            ahead.to(u + 6)
                        tokens_high(j - EG + 1, n + 1, e)
                ahead.to(base + EU + S)
                act.wait_ge(unit_used, base + EU + e * EU)
                nc.scalar.activation(oe[:, 0:N], DN[0][:], ACT.Copy).then_inc(oe_act, 1)

            def head(base, n, e):
                Lead(act, split_hi, base, base + S, e).to(base + S)
                for i in range(2):
                    tokens_high(i, n, e)

            head(UM, 0, 0)
            with act.Fori(0, NE - 1) as e:
                expert(UM, 0, e, True)
            expert(UM + (NE - 1) * EU, NE - 1, 0, False)
            act.wait_ge(routed, 1)
            more = act.value_load(flag[0:1, 0:1], min_val=0, max_val=1)
            with act.If(more > 0):
                with act.Fori(0, NE) as e:
                    head(UM + NE * EU, NE, e)
                    expert(UM + NE * EU, NE, e, False)
            act.wait_ge(scattered, 1)
            root(4)

        @block.vector
        def _(dve):
            own = [0]
            base_own = [0]

            def done(ins):
                own[0] += 1
                ins.then_inc(dve_own, 1)
                return own[0]

            def settle():
                dve.wait_ge(dve_own, own[0])

            lead = Lead(dve, split_lo, 0, UM)

            def norm_rows_of(n):
                dve.wait_ge(norm_root[n], 1)
                done(nc.vector.reciprocal(st[:, 12:14], st[:, 2:4]))
                settle()
                for b in range(NB):
                    nc.vector.tensor_scalar(xn[:, b, :], xs[:, b, :], st[:, 12 + b:13 + b], None, ALU.mult
                                            ).then_inc(norm_rows[n], 1)

            def norm_low(n, gains):
                for i in range(4):
                    dve.wait_ge(norm_hi[n], 2 * i + 2)
                    for kk in range(2):
                        k = 2 * i + kk
                        nc.vector.scalar_tensor_tensor(
                            hTl[:, k, :], T[i % 2][:, kk * SEQ:(kk + 1) * SEQ], gcol[:, gains + k:gains + k + 1],
                            hTh[:, k, :].bitcast(F32), ALU.mult, ALU.subtract).then_inc(norm_lo[n], 1)

            nc.vector.memset(ones[:], 1.0).then_inc(ones_set, 1)
            nc.vector.memset(eps[:], EPS).then_inc(ones_set, 1)
            for l in range(DEPTH):
                norm_rows_of(l)
                if l == 0:
                    dve.wait_ge(gain_done, 1)
                lead.to(at[l, "in"] + 2)
                norm_low(l, l * G_LAYER + G_ATTN)
                for g, (c0, n) in enumerate(PROJ):
                    u = at[l, "in"] + 2 * g + 1
                    lead.to(u + 3)
                    dve.wait_ge(unit_used, u + 1)
                    nc.vector.tensor_copy(pj[:, 1, c0:c0 + n], A[2 * (g % 2) + 1][:, :n]).then_inc(proj_dve[l], 1)
                dve.wait_ge(proj_act[l], 3)
                dve.wait_ge(proj_dve[l], 3)

                def rope(x1, x2, cos, sin, t, o1, o2, outs):
                    done(nc.vector.tensor_tensor(t[0], x1, cos, ALU.mult))
                    done(nc.vector.tensor_tensor(t[1], x2, sin, ALU.mult))
                    done(nc.vector.tensor_tensor(t[2], x1, sin, ALU.mult))
                    done(nc.vector.tensor_tensor(t[3], x2, cos, ALU.mult))
                    settle()
                    nc.vector.tensor_tensor(o1, outs(t[0]), outs(t[1]), ALU.subtract).then_inc(rope_done[l], 1)
                    nc.vector.tensor_tensor(o2, outs(t[2]), outs(t[3]), ALU.add).then_inc(rope_done[l], 1)

                cos = cst[:, K_COS:K_SIN].rearrange("p (b r) -> p b r", b=NB)
                sin = cst[:, K_SIN:K_MASK].rearrange("p (b r) -> p b r", b=NB)
                kr = pj[:, :, C_KR:C_QS]
                tk = [krt[:, i].rearrange("p (b r) -> p b r", b=NB) for i in range(4)]

                def heads_of(a):
                    return a.unsqueeze(2).broadcast_to([P, NB, HEADS, HALF])

                rope(kr[:, :, :HALF], kr[:, :, HALF:], cos, sin, tk, kn[:, :, :, NOPE:NOPE + HALF],
                     kn[:, :, :, NOPE + HALF:], heads_of)
                dve.wait_ge(lat_root[l], 2)
                done(nc.vector.reciprocal(st[:, 4:8], st[:, 8:12]))
                settle()
                for b in range(NB):
                    nc.vector.tensor_scalar(pj[:, b, 0:Q_LORA], pj[:, b, 0:Q_LORA], st[:, 4 + b:5 + b], None,
                                            ALU.mult).then_inc(lat_rows[l], 1)
                    nc.vector.tensor_scalar(pj[:, b, C_KV:C_KR], pj[:, b, C_KV:C_KR], st[:, 6 + b:7 + b], None,
                                            ALU.mult).then_inc(lat_rows[l], 1)

                def gate_add(g):
                    u = at[l, "gate0"] + 1 if g == 0 else at[l, "gate"] + 2 * g - 1
                    dve.wait_ge(unit_used, u + 1)
                    dve.wait_ge(bg_landed[l][g], 16)
                    for b in range(NB):
                        nc.vector.tensor_tensor(gates[:, g, b, :], A[2 + b][:], bg[:, g % 2, :],
                                                ALU.add).then_inc(gate_added[l], 1)

                lead.to(at[l, "gate0"] + 4)
                for i in range(3):
                    dve.wait_ge(lat_hi[l], min(2 * i + 2, KQ + KKV))
                    for kk in range(2 if i < 2 else 1):
                        k = 2 * i + kk
                        c = l * G_LAYER + G_Q + k
                        nc.vector.scalar_tensor_tensor(
                            latTl[:, k, :], T[i % 2][:, kk * SEQ:(kk + 1) * SEQ], gcol[:, c:c + 1],
                            latTh[:, k, :].bitcast(F32), ALU.mult, ALU.subtract).then_inc(lat_lo[l], 1)
                gate_add(0)
                for i in range(2):
                    u = at[l, "q"] + i
                    lead.to(u + 3)
                    dve.wait_ge(unit_used, u + 1)
                    nc.vector.tensor_copy(qn[:, 1, 4 * i:4 * i + 4, :], [A, DN][i][1][:, :4 * QK].rearrange(
                        "p (h c) -> p h c", h=4)).then_inc(up_dve[l], 1)
                dve.wait_ge(up_act[l], 2)
                dve.wait_ge(up_dve[l], 2)
                tq = [rt[:, i].rearrange("p (b h r) -> p b h r", b=NB, h=HEADS) for i in range(4)]
                x1, x2 = qn[:, :, :, NOPE:NOPE + HALF], qn[:, :, :, NOPE + HALF:]
                rope(x1, x2, heads_of(cos), heads_of(sin), tq, x1, x2, lambda a: a)
                lead.to(at[l, "kv"] + 3)
                dve.wait_ge(unit_used, at[l, "kv"] + 1)
                for n in range(2):
                    kv = A[2 + n][:].rearrange("p (h c) -> p h c", h=4)
                    nc.vector.tensor_copy(kn[:, 1, 4 * n:4 * n + 4, 0:NOPE], kv[:, :, 0:NOPE]
                                          ).then_inc(up_dve[l], 1)
                    nc.vector.tensor_copy(vm(1, n), kv[:, :, NOPE:]).then_inc(up_dve[l], 1)
                for i in range(1, QT_FILLS, 2):
                    dve.wait_ge(qk_T[l], i + 1)
                    dst, p, w, scale = qk_target(i)
                    nc.vector.tensor_scalar(dst, T[1][0:p, 0:w], scale, None, ALU.mult).then_inc(qk_dve[l], 1)

                def mask_max(f):
                    kind, b, heads = FILLS[f]
                    nh, w, off = len(heads), P * (b + 1), P * (1 - b)
                    dve.wait_ge(scored[l], f + 1)
                    if f >= 2:
                        dve.wait_ge(probs_T[l], f - 1)
                    s = sx[:, f % 2, :].rearrange("p (h k) -> p h k", h=nh)
                    sc = A[f % 2][:].rearrange("p (h k) -> p h k", h=nh)
                    m, neg = mx[:, f % 2, :nh], nm[:, f % 2, :nh]
                    if kind == 0:
                        tab = cst[:, K_MASK + off:K_MASK + SEQ]
                        nc.vector.tensor_tensor(s, sc, tab.unsqueeze(1).broadcast_to([P, nh, w]), ALU.add
                                                ).then_inc(masked[l], 1)
                        dve.wait_ge(masked[l], f + 1)
                    else:
                        tab = cst[:, K_DIST + off:K_DIST + SEQ]
                        for i, h in enumerate(heads):
                            last = nc.vector.scalar_tensor_tensor(s[:, i], tab, -SLOPES[h], sc[:, i], ALU.mult, ALU.add)
                            if i < nh - 1:
                                done(last)
                        last.then_inc(masked[l], 1)
                        dve.wait_ge(masked[l], f + 1)
                        settle()
                    done(nc.vector.tensor_reduce(m, s, AX, ALU.max))
                    settle()
                    if kind:
                        sink = sk[:, l, heads[0]:heads[-1] + 1:2]
                        done(nc.vector.tensor_tensor(m, m, sink, ALU.max))
                        settle()
                        done(nc.vector.tensor_tensor(sink_d[:, f % 2, :nh], sink, m, ALU.subtract))
                        settle()
                    nc.vector.tensor_scalar(neg, m, -1.0 if kind else -MLA_SCALE, None, ALU.mult
                                            ).then_inc(max_ready[l], 1)

                EXPS = [sum(len(x[2]) for x in FILLS[:f + 1]) for f in range(NF)]

                def normalise(f):
                    kind, b, heads = FILLS[f]
                    nh, w = len(heads), P * (b + 1)
                    s = sx[:, f % 2, :].rearrange("p (h k) -> p h k", h=nh)
                    sm, r = sums[:, f % 2, :nh], rsum[:, f % 2, :nh]
                    dve.wait_ge(exp_done[l], EXPS[f])
                    if kind:
                        done(nc.vector.tensor_tensor(sm, sm, sink_e[:, f % 2, :nh], ALU.add))
                        settle()
                    done(nc.vector.reciprocal(r, sm))
                    settle()
                    nc.vector.tensor_tensor(s, s, r.unsqueeze(2).broadcast_to([P, nh, w]), ALU.mult
                                            ).then_inc(probs_ready[l], 1)

                def o_low(i):
                    kind, b = i // NB, i % NB
                    dve.wait_ge(o_hi[l], i + 1)
                    o = slice(b * P, (b + 1) * P)
                    nc.vector.tensor_tensor(oTl[:, kind, :, o], DN[b][:].rearrange("p (j t) -> p j t", j=4),
                                            oTh[:, kind, :, o].bitcast(F32), ALU.subtract).then_inc(o_lo[l], 1)

                dve.wait_ge(sink_landed, 16)
                mask_max(0)
                for f in range(NF):
                    lead.to(at[l, "gate"] + min(f, 5) + 3)
                    if f + 1 < NF:
                        mask_max(f + 1)
                    normalise(f)
                    if f in (2, 4, 6):
                        gate_add(f // 2)
                    if f - 3 in LAST:
                        o_low(LAST.index(f - 3))
                for i in range(4):
                    if LAST[i] + 3 >= NF:
                        o_low(i)
                for n in range(2):
                    u = at[l, "br"] + 2 * n + 1
                    lead.to(u + 3)
                    dve.wait_ge(unit_used, u + 1)
                    dve.wait_ge(gate_ready[l], 4 * n + 4)
                    c = slice(n * N, (n + 1) * N)
                    for b in range(NB):
                        g1, g2 = gates[:, n, b, :], gates[:, 2 + n, b, :]
                        nc.vector.tensor_tensor(mg[:, b, c], A[b][:], g1, ALU.mult).then_inc(br_free[l], 1)
                        nc.vector.tensor_tensor(g2, A[2 + b][:], g2, ALU.mult).then_inc(br_free[l], 1)
                    dve.wait_ge(br_free[l], 4 * n + 4)
                    for b in range(NB):
                        nc.vector.tensor_tensor(mg[:, b, c], mg[:, b, c], gates[:, 2 + n, b, :], ALU.add).then_inc(merged[l], 1)
                for i in range(4):
                    dve.wait_ge(mg_hi[l], i + 1)
                    nc.vector.tensor_tensor(hTl[:, 2 * i:2 * i + 2, :], T[i % 2][:].rearrange("p (k t) -> p k t", k=2),
                                            hTh[:, 2 * i:2 * i + 2, :].bitcast(F32), ALU.subtract
                                            ).then_inc(mg_lo[l], 1)
                for n in range(2):
                    u = at[l, "out"] + 2 * n + 1
                    lead.to(u + 3)
                    dve.wait_ge(unit_used, u + 1)
                    for b in range(NB):
                        c = xs[:, b, n * N:(n + 1) * N]
                        nc.vector.tensor_tensor(c, [DN, A][n][b][:], c, ALU.add).then_inc(x_added[l], 1)
                norm_rows_of(2 + l)
                norm_low(2 + l, l * G_LAYER + G_FFN)
                if l == 0:
                    u0 = at[0, "ffn"]
                    for j in range(DG + 1):
                        n = min(N, FF - j * N)
                        u = u0 + group_at(j)
                        lead.to(u + (4 if j < DG else 2))
                        if j:
                            m = min(N, FF - (j - 1) * N)
                            for b in range(NB):
                                dve.wait_ge(ff_hi[0], NB * (j - 1) + b + 1)
                                nc.vector.tensor_tensor(aTl[:, b, :m // P, :], T[b][:, :m].rearrange("p (k t) -> p k t", t=P),
                                                        aTh[:, b, :m // P, :].bitcast(F32), ALU.subtract
                                                        ).then_inc(ff_lo[0], 1)
                        if j < DG:
                            lead.to(u + 6)
                            dve.wait_ge(unit_used, u + 4)
                            for b in range(NB):
                                dve.wait_ge(silu_done[0], NB * j + b + 1)
                                if j:
                                    dve.wait_ge(ff_T[0], NB * j)
                                nc.vector.tensor_tensor(av[:, b, :n], A[2 + b][:, :n], sg[:, b, :n], ALU.mult
                                                        ).then_inc(ff_ready[0], 1)
                        if j:
                            lead.to(u0 + down_at(j - 1, DG) + (2 if j < DG else 1) + 2)
                            for b in range(NB):
                                for h in range(2):
                                    i = 4 * (j - 1) + 2 * b + h
                                    if b and h:
                                        dve.wait_ge(unit_used, u0 + down_at(j - 1, DG) + m // SEQ)
                                    else:
                                        dve.wait_ge(down_done, 3 * (j - 1) + 2 * b + h + 1)
                                    c = xs[:, b, h * N:(h + 1) * N]
                                    if j > 1:
                                        dve.wait_ge(x_added[0], i + 1)
                                    nc.vector.tensor_tensor(c, [DN, T][b][h][:], c, ALU.add).then_inc(x_added[0], 1)
                    dve.wait_ge(x_added[0], X_DENSE)

            dve.wait_ge(wr_hi, 1)
            nc.vector.tensor_tensor(wrl[:], wr[:], wrh[:].bitcast(F32), ALU.subtract).then_inc(wr_lo, 1)
            dve.wait_ge(logits_done, 1)
            done(nc.vector.tensor_copy(lg[:], A[0][:, :NB * NE].rearrange("p (b e) -> p b e", b=NB)))
            settle()
            done(nc.vector.tensor_reduce(lmax[:], lg[:], AX, ALU.max))
            settle()
            nc.vector.tensor_scalar(lmax[:], lmax[:], -1.0, None, ALU.mult).then_inc(lmax_ready, 1)
            for b in range(NB):
                other = lg[:, b].unsqueeze(1).broadcast_to([P, NE, NE])
                this = lg[:, b].unsqueeze(2).broadcast_to([P, NE, NE])
                done(nc.vector.tensor_tensor(above[:, b], other, this, ALU.is_gt))
                done(nc.vector.tensor_tensor(ties[:, b], other, this, ALU.is_equal))
            settle()
            lower = cst[:, K_LOWER:K_ALL].rearrange("p (e f) -> p e f", e=NE)
            for b in range(NB):
                done(nc.vector.tensor_tensor(ties[:, b], ties[:, b], lower, ALU.mult))
            settle()
            done(nc.vector.tensor_tensor(above[:], above[:], ties[:], ALU.add))
            settle()
            done(nc.vector.tensor_reduce(rank[:], above[:], AX, ALU.add))
            settle()
            nc.vector.tensor_scalar(mask[:], rank[:], 2.0, None, ALU.is_lt).then_inc(mask_ready, 1)
            dve.wait_ge(mask_ready, 1)
            dve.wait_ge(lexp_done, NB)
            done(nc.vector.tensor_tensor(pe8[:], pe8[:], mask[:], ALU.mult))
            settle()
            done(nc.vector.tensor_reduce(psum8[:], pe8[:], AX, ALU.add))
            settle()
            done(nc.vector.reciprocal(psum8[:], psum8[:]))
            settle()
            done(nc.vector.tensor_tensor(comb[:], pe8[:], psum8[:].unsqueeze(2).broadcast_to([P, NB, NE]), ALU.mult))
            dve.wait_ge(counted, 1)
            cnt = A[1][:, :NB * NE].rearrange("p (b e) -> p b e", b=NB)
            done(nc.vector.scalar_tensor_tensor(pos[:], cnt, 1.0, mask[:], ALU.add, ALU.mult))
            done(nc.vector.tensor_reduce(most[:], A[1][:, NB * NE:NB * NE + NE], AX, ALU.max))
            settle()
            done(nc.vector.tensor_scalar(pos[:], pos[:], -1.0, None, ALU.add))
            nc.vector.tensor_scalar(flag[:], most[:], float(P), None, ALU.is_gt).then_inc(routed, 1)
            settle()

            def select(turn, n, e, col):
                nc.vector.tensor_copy(posc[:], pos[:, :, bass.ds(col, 1)].rearrange("p b a -> p (b a)")
                                      ).then_inc(selected, 1)
                nc.vector.tensor_copy(combc[:], comb[:, :, bass.ds(col, 1)].rearrange("p b a -> p (b a)")
                                      ).then_inc(selected, 1)
                dve.wait_ge(selected, 2 * n + 2 + e * 2)
                rank_of = cst[:, K_IOTA + turn * P:K_IOTA + (turn + 1) * P]
                for b in range(NB):
                    nc.vector.tensor_scalar(pick[:, b], rank_of, posc[:, b:b + 1], None, ALU.is_equal
                                            ).then_inc(picked, 1)
                    nc.vector.tensor_scalar(cw[:, b], rank_of, posc[:, b:b + 1], combc[:, b:b + 1], ALU.is_equal,
                                            ALU.mult).then_inc(picked, 1)

            def tokens_low(i, n, e):
                dve.wait_ge(he_hi, 8 * n + 4 * i + 4 + e * 8)
                for kk in range(4):
                    k = 4 * i + kk
                    c = G_LAYER + G_FFN + k
                    nc.vector.scalar_tensor_tensor(
                        heTl[:, k, :], T[i][:, kk * P:(kk + 1) * P], gcol[:, c:c + 1],
                        heTh[:, k, :].bitcast(F32), ALU.mult, ALU.subtract).then_inc(he_lo, 1)

            def add_spread(b, full, value, added):
                for h in range(2):
                    dve.wait_ge(full, value + h)
                    c = xs[:, b, h * N:(h + 1) * N]
                    nc.vector.tensor_tensor(c, DN[h][:], c, ALU.add).then_inc(added, 1)

            def expert(base, n, e, following):
                ahead = Lead(dve, split_lo, base, base + EU + (S if following else 0), e)
                ahead.next += S
                for j in range(EG + 1):
                    u = base + group_at(j)
                    ahead.to(u + (4 if j < EG else 2))
                    if j == 0:
                        add_spread(0, oe_full, 4 * n + 1 + e * 4, x_added[1])
                    if j:
                        dve.wait_ge(ff_hi[1], EG * n + j + e * EG)
                        nc.vector.tensor_tensor(aTl[:, (j - 1) % 2], T[(j - 1) % 2][:].rearrange("p (k t) -> p k t", k=4),
                                                aTh[:, (j - 1) % 2].bitcast(F32), ALU.subtract).then_inc(ff_lo[1], 1)
                    if following and j == EG - 2:
                        select(0, n + 1, e, e + 1)
                    if j < EG:
                        ahead.to(u + 6)
                        dve.wait_ge(unit_used, u + 4 + e * EU)
                        dve.wait_ge(silu_done[1], EG * n + j + 1 + e * EG)
                        nc.vector.tensor_tensor(av[:, j % 2], A[2 + j % 2][:], sg[:, j % 2], ALU.mult
                                                ).then_inc(ff_ready[1], 1)
                    if j == 0:
                        add_spread(1, oe_full, 4 * n + 3 + e * 4, x_added[1])
                    if following and j >= EG - 1:
                        tokens_low(j - EG + 1, n + 1, e)
                ahead.to(base + EU + S)
                dve.wait_ge(unit_used, base + EU + e * EU)
                nc.vector.tensor_copy(oe[:, N:], DN[1][:]).then_inc(oe_dve, 1)

            def head(turn, base, n, e):
                select(turn, n, e, e)
                Lead(dve, split_lo, base, base + S, e).to(base + S)
                for i in range(2):
                    tokens_low(i, n, e)

            nc.vector.memset(oe[:], 0.0).then_inc(oe_act, 1)
            nc.vector.memset(cwT[:], 0.0).then_inc(oe_dve, 1)
            head(0, UM, 0, 0)
            with dve.Fori(0, NE - 1) as e:
                expert(UM, 0, e, True)
            expert(UM + (NE - 1) * EU, NE - 1, 0, False)
            more = dve.value_load(flag[0:1, 0:1], min_val=0, max_val=1)
            with dve.If(more > 0):
                with dve.Fori(0, NE) as e:
                    head(1, UM + NE * EU, NE, e)
                    expert(UM + NE * EU, NE, e, False)
            for b in range(NB):
                add_spread(b, last_full, 2 * b + 1, last_added)
            dve.wait_ge(last_added, 2 * NB)
            nc.vector.tensor_copy(st[:, 14:15], eps[:]).then_inc(scattered, 1)
            dve.wait_ge(norm_root[4], 1)
            nc.vector.reciprocal(st[:, 12:14], st[:, 2:4]).then_inc(lmax_ready, 1)
            dve.wait_ge(lmax_ready, 2)
            dve.wait_ge(gfin_landed, 16)
            for b in range(NB):
                nc.vector.scalar_tensor_tensor(gout[:, b, :], xs[:, b, :], st[:, 12 + b:13 + b], gfin[:],
                                               ALU.mult, ALU.mult).then_inc(norm_rows[4], 1)

        @block.tensor
        def _(pe):
            def turn_norm(n, waits):
                pe.wait_ge(norm_rows[n], NB)
                for s, v in waits:
                    pe.wait_ge(s, v)
                for i in range(4):
                    if i >= 2:
                        pe.wait_ge(norm_lo[n], 2 * i - 2)
                    for kk in range(2):
                        for b in range(NB):
                            k = 2 * i + kk
                            last = nc.tensor.transpose(T[i % 2][:, (kk * NB + b) * P:(kk * NB + b + 1) * P],
                                                       xn[:, b, k * P:(k + 1) * P], ident)
                    last.then_inc(norm_T[n], 1)

            def columns(u, kt0, kt, total, n, hi, lo, banks):
                pe.wait_ge(lo_done, u + 1)
                for b in range(NB):
                    for kk in range(kt):
                        k = kt0 + kk
                        wh, wl = split_tile(u, kk, n)
                        last = product(banks[b][:, :n], hi[:, k, b * P:(b + 1) * P], lo[:, k, b * P:(b + 1) * P],
                                       wh, wl, k == 0, k == total - 1)
                last.then_inc(unit_used, 1)

            pe.wait_ge(const_landed, 16)
            pe.wait_ge(gain_landed, 16 * 8)
            nc.tensor.transpose(T[0][:, 0:DEPTH * G_LAYER], grow[0:DEPTH * G_LAYER, :],
                                ident[0:DEPTH * G_LAYER, 0:DEPTH * G_LAYER]).then_inc(gain_T, 1)
            for l in range(DEPTH):
                turn_norm(l, [(gain_done, 1)] if l == 0 else [(x_added[0], X_DENSE)])
                pe.wait_ge(norm_lo[l], KD)
                for g, (c0, n) in enumerate(PROJ):
                    u = at[l, "in"] + 2 * g
                    if g == 2:
                        pe.wait_ge(proj_act[l], 1)
                        pe.wait_ge(proj_dve[l], 1)
                    for h in range(2):
                        columns(u + h, 4 * h, 4, KD, n, hTh, hTl, A[2 * (g % 2):])
                pe.wait_ge(proj_act[l], 2)
                pe.wait_ge(proj_dve[l], 2)
                for h in range(2):
                    columns(at[l, "gate0"] + h, 4 * h, 4, KD, N, hTh, hTl, A[2:])
                pe.wait_ge(lat_rows[l], 4)
                for i in range(3):
                    if i == 2:
                        pe.wait_ge(lat_lo[l], 2)
                    for kk in range(2 if i < 2 else 1):
                        k = 2 * i + kk
                        for b in range(NB):
                            last = nc.tensor.transpose(T[i % 2][:, (kk * NB + b) * P:(kk * NB + b + 1) * P],
                                                       pj[:, b, k * P:(k + 1) * P], ident)
                    last.then_inc(lat_T[l], 1)
                pe.wait_ge(lat_lo[l], 3)
                pe.wait_ge(proj_act[l], 3)
                pe.wait_ge(proj_dve[l], 3)
                for i in range(2):
                    columns(at[l, "q"] + i, 0, KQ, KQ, 4 * QK, latTh, latTl, [A, DN][i])
                u = at[l, "kv"]
                pe.wait_ge(lo_done, u + 1)
                pe.wait_ge(lat_lo[l], KQ + KKV)
                pe.wait_ge(up_act[l], 1)
                pe.wait_ge(up_dve[l], 1)
                pe.wait_ge(gate_added[l], 2)
                for b in range(NB):
                    for n in range(2):
                        for k in range(KKV):
                            wh, wl = split_tile(u, k, D, n * N, N)
                            last = product(A[2 * b + n][:], latTh[:, KQ + k, b * P:(b + 1) * P],
                                           latTl[:, KQ + k, b * P:(b + 1) * P], wh, wl, k == 0, k == KKV - 1)
                last.then_inc(unit_used, 1)
                for i in range(QT_FILLS):
                    bank = T[i % 2]
                    if i == 0:
                        pe.wait_ge(rope_done[l], 4)
                    if i == 4:
                        pe.wait_ge(up_act[l], 6)
                        pe.wait_ge(up_dve[l], 6)
                    if i == 10:
                        pe.wait_ge(kdup_done[l], 2)
                    if i >= 2:
                        pe.wait_ge([qk_act, qk_dve][i % 2][l], i // 2)
                    for s in range(2):
                        for b in range(NB):
                            o = (s * NB + b) * P
                            if i < 8:
                                src = (qn if i < 4 else kn)[:, b, 2 * (i % 4) + s, :]
                                last = nc.tensor.transpose(bank[0:QK, o:o + P], src, ident)
                            else:
                                if i < 10:
                                    c = C_QS + (2 * (i - 8) + s) * P
                                    src = pj[:, b, c:c + P]
                                else:
                                    src = kdup[:, b, s].rearrange("p r d -> p (r d)")
                                last = nc.tensor.transpose(bank[:, o:o + P], src, ident)
                    last.then_inc(qk_T[l], 1)

                def scores(f):
                    kind, b, heads = FILLS[f]
                    w = P * (b + 1)
                    if f >= 2:
                        pe.wait_ge(masked[l], f - 1)
                    for i, h in enumerate(heads):
                        o = A[f % 2][:, i * w:(i + 1) * w]
                        q = slice(b * P, (b + 1) * P)
                        if kind == 0:
                            last = nc.tensor.matmul(o, qT[0:QK, h, q], kT[0:QK, h, 0:w], start=True, stop=True)
                        else:
                            r = slice(SW_D * (h % 2), SW_D * (h % 2) + SW_D)
                            last = nc.tensor.matmul(o, sqT[r, h // 2, q], skT[r, h // 4, 0:w], start=True, stop=True)
                    last.then_inc(scored[l], 1)

                def turn_probs(f):
                    kind, b, heads = FILLS[f]
                    pe.wait_ge(probs_ready[l], f + 1)
                    if f >= 2:
                        pe.wait_ge(probs_T_out[l], f - 1)
                    for i in range(4):
                        last = nc.tensor.transpose(T[f % 2][:, i * P:(i + 1) * P], sx[:, f % 2, i * P:(i + 1) * P],
                                                   ident)
                    last.then_inc(probs_T[l], 1)

                def values(f):
                    kind, b, heads = FILLS[f]
                    pe.wait_ge(probs_T_out[l], f + 1)
                    if kind and heads[0] == 0:
                        pe.wait_ge(o_lo[l], b + 1)
                    for i, h in enumerate(heads):
                        r = slice(VD * (h % 2), VD * (h % 2) + VD)
                        o = DN[b][r, (h // 2) * P:(h // 2 + 1) * P]
                        for kb in range(b + 1):
                            v = pj[:, kb, h * VD:(h + 1) * VD] if kind == 0 else \
                                pj[:, kb, C_VS + SW_D * (h // 4):C_VS + SW_D * (h // 4) + SW_D]
                            c = (i * (b + 1) + kb) * P
                            last = nc.tensor.matmul(o, v, pT[:, f % 2, c:c + P], start=kb == 0, stop=kb == b)
                    last.then_inc(pv_done[l], 1)

                pe.wait_ge(qk_act[l], QT_FILLS - QT_FILLS // 2)
                pe.wait_ge(qk_dve[l], QT_FILLS // 2)
                scores(0)
                scores(1)
                for f in range(NF):
                    if f < 6:
                        if f % 2 == 0:
                            if f:
                                pe.wait_ge(gate_added[l], f + 2)
                            else:
                                pe.wait_ge(up_dve[l], 6)
                        columns(at[l, "gate"] + f, 4 * (f % 2), 4, KD, N, hTh, hTl, A[2:])
                    turn_probs(f)
                    if f + 2 < NF:
                        scores(f + 2)
                    if f:
                        values(f - 1)
                values(NF - 1)
                pe.wait_ge(o_lo[l], 4)
                pe.wait_ge(masked[l], NF)
                pe.wait_ge(gate_added[l], 8)
                for n in range(2):
                    if n:
                        pe.wait_ge(br_free[l], 4)
                    for kind in range(2):
                        columns(at[l, "br"] + 2 * n + kind, 0, 4, 4, N, oTh[:, kind], oTl[:, kind], A[2 * kind:])
                for i in range(4):
                    pe.wait_ge(merged[l], NB * (1 + i // 2))
                    if i >= 2:
                        pe.wait_ge(mg_lo[l], i - 1)
                    for kk in range(2):
                        for b in range(NB):
                            k = 2 * i + kk
                            last = nc.tensor.transpose(T[i % 2][:, (kk * NB + b) * P:(kk * NB + b + 1) * P],
                                                       mg[:, b, k * P:(k + 1) * P], ident)
                    last.then_inc(mg_T[l], 1)
                for n in range(2):
                    for h in range(2):
                        pe.wait_ge(mg_lo[l], 2 * h + 2)
                        columns(at[l, "out"] + 2 * n + h, 4 * h, 4, KD, N, hTh, hTl, [DN, A][n])
                turn_norm(2 + l, [(mg_lo[l], 4)])
                pe.wait_ge(norm_lo[2 + l], KD)
                if l == 0:
                    u0 = at[0, "ffn"]
                    pe.wait_ge(x_added[0], 4)
                    for j in range(DG + 1):
                        n = min(N, FF - j * N)
                        u = u0 + group_at(j)
                        if j < DG:
                            if j:
                                pe.wait_ge(silu_done[0], NB * j)
                            for h in range(2):
                                columns(u + h, 4 * h, 4, KD, n, hTh, hTl, A)
                        if j:
                            m = min(N, FF - (j - 1) * N)
                            if j > 1:
                                pe.wait_ge(x_added[0], 4 + 4 * (j - 1))
                            for b in range(NB):
                                pe.wait_ge(ff_ready[0], NB * (j - 1) + b + 1)
                                for k in range(m // P):
                                    last = nc.tensor.transpose(T[b][:, k * P:(k + 1) * P], av[:, b, k * P:(k + 1) * P],
                                                               ident)
                                last.then_inc(ff_T[0], 1)
                        if j < DG:
                            if j:
                                pe.wait_ge(ff_ready[0], NB * j)
                            for h in range(2):
                                columns(u + 2 + h, 4 * h, 4, KD, n, hTh, hTl, A[2:])
                        if j:
                            pe.wait_ge(ff_lo[0], NB * j)
                            ud = u0 + down_at(j - 1, DG)
                            kt = m // P
                            for b in range(NB):
                                for k in range(kt):
                                    if b == 0 and k % 2 == 0:
                                        pe.wait_ge(lo_done, ud + k // 2 + 1)
                                    for h in range(2):
                                        wh, wl = split_tile(ud + k // 2, k % 2, D, h * N, N)
                                        last = product([DN, T][b][h][:], aTh[:, b, k, :], aTl[:, b, k, :], wh, wl,
                                                       k == 0, k == kt - 1)
                                        if b == 1 and h == 1 and k % 2 == 1:
                                            last.then_inc(unit_used, 1)
                                        elif k == kt - 1:
                                            last.then_inc(down_done, 1)

            pe.wait_ge(x_added[1], 4)
            pe.wait_ge(wr_lo, 1)
            for b in range(NB):
                for k in range(KD):
                    last = product(A[0][:, b * NE:(b + 1) * NE], hTh[:, k, b * P:(b + 1) * P],
                                   hTl[:, k, b * P:(b + 1) * P], wrh[:, k, :], wrl[:, k, :], k == 0, k == KD - 1)
            last.then_inc(logits_done, 1)
            pe.wait_ge(mask_ready, 1)
            nc.tensor.matmul(A[1][:, 0:NE], before, mask[:, 0, :], start=True, stop=True)
            nc.tensor.matmul(A[1][:, NE:2 * NE], ones[:], mask[:, 0, :], start=True, stop=False)
            nc.tensor.matmul(A[1][:, NE:2 * NE], before, mask[:, 1, :], start=False, stop=True)
            nc.tensor.matmul(A[1][:, 2 * NE:3 * NE], ones[:], mask[:, 0, :], start=True, stop=False)
            nc.tensor.matmul(A[1][:, 2 * NE:3 * NE], ones[:], mask[:, 1, :], start=False, stop=True
                             ).then_inc(counted, 1)
            pe.wait_ge(routed, 1)

            def gather(i, n, e):
                pe.wait_ge(picked, 4 * n + 4 + e * 4)
                for kk in range(4):
                    k = 4 * i + kk
                    for b in range(NB):
                        last = nc.tensor.matmul(T[i][:, kk * P:(kk + 1) * P], xn[:, b, k * P:(k + 1) * P],
                                                pick[:, b], start=b == 0, stop=b == NB - 1)
                last.then_inc(gathered, 1)

            def spread(b, full):
                for h in range(2):
                    nc.tensor.matmul(DN[h][:], cwT[:, b * P:(b + 1) * P], oe[:, h * N:(h + 1) * N],
                                     start=True, stop=True).then_inc(full, 1)

            def expert(base, n, e, following):
                def products(u, h, bank):
                    pe.wait_ge(lo_done, u + 1 + e * EU)
                    for kk in range(4):
                        k = 4 * h + kk
                        wh, wl = split_tile(u, kk, N)
                        last = product(bank[:], heTh[:, k, :], heTl[:, k, :], wh, wl, k == 0, k == KD - 1)
                    last.then_inc(unit_used, 1)

                pe.wait_ge(he_lo, 8 * n + 8 + e * 8)
                for j in range(EG + 1):
                    u = base + group_at(j)
                    if j < EG:
                        if j >= 2:
                            pe.wait_ge(silu_done[1], EG * n + j - 1 + e * EG)
                        for h in range(2):
                            products(u + h, h, A[j % 2])
                    if j == 0:
                        pe.wait_ge(oe_act, n + 1 + e)
                        pe.wait_ge(oe_dve, n + 1 + e)
                        spread(0, oe_full)
                    else:
                        q = (j - 1) % 2
                        pe.wait_ge(ff_ready[1], EG * n + j + e * EG)
                        if j == 1:
                            pe.wait_ge(cw_out, n + 1 + e)
                        if j > 2:
                            pe.wait_ge(ff_lo[1], EG * n + j - 2 + e * EG)
                        if following and j == EG:
                            pe.wait_ge(he_lo, 8 * n + 12 + e * 8)
                        for k in range(4):
                            last = nc.tensor.transpose(T[q][:, k * P:(k + 1) * P], av[:, q, k * P:(k + 1) * P], ident)
                        last.then_inc(ff_T[1], 1)
                    if following and j == EG:
                        gather(1, n + 1, e)
                    if j < EG:
                        if j >= 2:
                            pe.wait_ge(ff_ready[1], EG * n + j - 1 + e * EG)
                        for h in range(2):
                            products(u + 2 + h, h, A[2 + j % 2])
                    if j == 0:
                        pe.wait_ge(x_added[1], 4 + 4 * n + 2 + e * 4)
                        spread(1, oe_full)
                        for b in range(NB):
                            last = nc.tensor.transpose(T[0][:, b * P:(b + 1) * P], cw[:, b], ident)
                        last.then_inc(cw_T, 1)
                    if following and j == EG - 1:
                        pe.wait_ge(ff_lo[1], EG * n + EG - 2 + e * EG)
                        gather(0, n + 1, e)
                    if j:
                        if j == 1:
                            pe.wait_ge(x_added[1], 4 + 4 * n + 4 + e * 4)
                        pe.wait_ge(ff_lo[1], EG * n + j + e * EG)
                        ud = base + down_at(j - 1, EG)
                        for i in range(2):
                            pe.wait_ge(lo_done, ud + i + 1 + e * EU)
                            for kk in range(2):
                                k = 2 * i + kk
                                for h in range(2):
                                    wh, wl = split_tile(ud + i, kk, D, h * N, N)
                                    last = product(DN[h][:], aTh[:, q, k, :], aTl[:, q, k, :], wh, wl,
                                                   j == 1 and k == 0, j == EG and k == 3)
                            last.then_inc(unit_used, 1)

            def head(n, e):
                for i in range(2):
                    gather(i, n, e)

            def output_out(n, e):
                pe.wait_ge(oe_act, n + 1 + e)
                pe.wait_ge(oe_dve, n + 1 + e)

            pe.wait_ge(oe_act, 1)
            pe.wait_ge(oe_dve, 1)
            head(0, 0)
            with pe.Fori(0, NE - 1) as e:
                expert(UM, 0, e, True)
            expert(UM + (NE - 1) * EU, NE - 1, 0, False)
            output_out(NE, 0)
            more = pe.value_load(flag[0:1, 0:1], min_val=0, max_val=1)
            with pe.If(more > 0):
                with pe.Fori(0, NE) as e:
                    head(NE, e)
                    expert(UM + NE * EU, NE, e, False)
                    output_out(NE + 1, e)
            for b in range(NB):
                if b:
                    pe.wait_ge(last_added, 2)
                spread(b, last_full)

        @block.gpsimd
        def _(pool):
            pool.wait_ge(o_lo[1], 4)
            pool.dma_start(wr[:], w_router[0].rearrange("(k p) e -> p k e", p=P)).then_inc(router_landed, 16)
            pool.dma_start(gfin[:], g_final.rearrange("(a d) -> a d", a=1).broadcast_to([P, D])
                           ).then_inc(gfin_landed, 16)
            pool.wait_ge(gfin_landed, 16)


_INS = ["x", "g_attn_norm", "w_in", "b_gate", "g_q_norm", "w_q_up", "g_kv_norm", "w_kv_up", "sinks", "w_br_mla",
        "w_br_swa", "w_out", "g_ffn_norm", "dense_w_gate", "dense_w_up", "dense_w_down", "w_router",
        "moe_w_gate", "moe_w_up", "moe_w_down", "g_final"]


def shape_constants():
    import numpy as np

    c = np.zeros((P, K_ALL), np.float32)
    inv = 1.0 / (10000.0 ** (np.arange(0, ROPE, 2, dtype=np.float32) / ROPE))
    ang = np.arange(SEQ, dtype=np.float32)[:, None] * inv[None, :]
    for b in range(NB):
        c[:, K_COS + b * HALF:K_COS + (b + 1) * HALF] = np.cos(ang[b * P:(b + 1) * P])
        c[:, K_SIN + b * HALF:K_SIN + (b + 1) * HALF] = np.sin(ang[b * P:(b + 1) * P])
    q, k = np.arange(P, SEQ)[:, None], np.arange(SEQ)[None, :]
    ahead = k // CHUNK > q // CHUNK
    c[:, K_MASK:K_DIST] = np.where(ahead, -1e30, 0.0)
    outside = ahead | (k // CHUNK < q // CHUNK - 1)
    c[:, K_DIST:K_IDENT] = np.where(outside, 1e33, np.abs(q - k))
    c[:, K_IDENT:K_BEFORE] = np.eye(P)
    c[:, K_BEFORE:K_IOTA] = np.triu(np.ones((P, P)), 1)
    c[:, K_IOTA:K_LOWER] = np.arange(SEQ)[None, :]
    c[:, K_LOWER:K_ALL] = np.tril(np.ones((NE, NE)), -1).reshape(1, -1)
    return c


def kernel(**inputs):
    import numpy as np
    import concourse.bacc as bacc
    from concourse.bass_utils import run_bass_kernel_spmd

    nc = bacc.Bacc("TRN2", target_bir_lowering=False, num_devices=1)
    arrays, args = {}, []
    for name in _INS:
        a = np.ascontiguousarray(inputs[name])
        arrays[f"in_{name}"] = a
        args.append(nc.dram_tensor(f"in_{name}", a.shape, F32, kind="ExternalInput").ap())
    arrays["shape_constants"] = shape_constants()
    args.append(nc.dram_tensor("shape_constants", (P, K_ALL), F32, kind="ExternalInput").ap())
    args.append(nc.dram_tensor("out", (1, SEQ, D), F32, kind="ExternalOutput").ap())
    trunk(nc, *args)
    r = run_bass_kernel_spmd(nc, [arrays], core_ids=[0])
    return r.results[0]["out"]
```

```python
from contextlib import ExitStack

import concourse.bass as bass
from concourse import mybir

F32 = mybir.dt.float32
F32R = mybir.dt.float32r
I32 = mybir.dt.int32
ALU = mybir.AluOpType
ACT = mybir.ActivationFunctionType
AX = mybir.AxisListType.X

P = 128
D = 1024
SEQ = 256
NB = SEQ // P
KD = D // P
DEPTH = 2
CHUNK = 64
HEADS = 8
NOPE, ROPE, VD = 64, 32, 64
QK = NOPE + ROPE
HALF = ROPE // 2
Q_LORA, KV_LORA = 384, 256
KQ, KKV = Q_LORA // P, KV_LORA // P
SW_KV, SW_D = 2, 64
FF = 2816
NE = 8
EFF = 3584
EPS = 1e-6
MLA_SCALE = float(QK) ** -0.5
SWA_SCALE = float(SW_D) ** -0.5
SLOPES = [2.0 ** (-8.0 * (h + 1.0) / HEADS) for h in range(HEADS)]

C_KV = Q_LORA
C_KR = C_KV + KV_LORA
C_QS = C_KR + ROPE
C_KS = C_QS + HEADS * SW_D
C_VS = C_KS + SW_KV * SW_D
C_GATE = C_VS + SW_KV * SW_D
PROJ = [(0, 512), (512, 512), (1024, C_GATE - 1024)]

UNIT = 2048
R = 6
S = 3
N = 512

def group_at(j):
    return 0 if j == 0 else 4 + 6 * (j - 1)


def down_at(j, groups):
    return 8 + 6 * j if j < groups - 1 else 4 + 6 * (groups - 1)


EG = EFF // N
EU = 6 * EG
DG = -(-FF // N)
assert EU % R == 0 and EU % S == 0

K_COS = 0
K_SIN = K_COS + NB * HALF
K_DIST = K_SIN + NB * HALF
K_IDENT = K_DIST + SEQ
K_BEFORE = K_IDENT + P
K_IOTA = K_BEFORE + P
K_LOWER = K_IOTA + SEQ
K_ALL = K_LOWER + NE * NE

G_LAYER = KD + KQ + KKV + KD
G_ATTN, G_Q, G_KV, G_FFN = 0, KD, KD + KQ, KD + KQ + KKV

FILLS = []
for kind in range(2):
    for b in range(NB):
        per = 4 // (b + 1)
        order = list(range(HEADS)) if kind == 0 else list(range(0, HEADS, 2)) + list(range(1, HEADS, 2))
        FILLS += [(kind, b, order[h:h + per]) for h in range(0, HEADS, per)]
NF = len(FILLS)
LAST = [max(f for f, x in enumerate(FILLS) if x[:2] == (kind, b)) for kind in range(2) for b in range(NB)]
MLA_FILLS = sum(x[0] == 0 for x in FILLS)
EXPS = [sum(len(x[2]) for x in FILLS[:f + 1]) for f in range(NF)]
AUG = QK + NB
QT_FILLS = 8


def trunk(nc, x, g_attn_norm, w_in, b_gate, g_q_norm, w_q_up, g_kv_norm, w_kv_up, sinks, w_br_mla,
          w_br_swa, w_out, g_ffn_norm, dense_w_gate, dense_w_up, dense_w_down, w_router, moe_w_gate,
          moe_w_up, moe_w_down, g_final, consts, mask_rows, out):
    units = []
    at = {}

    def rows(w, k0, kt, c0, n):
        units.append((w[k0 * P:(k0 + kt) * P, c0:c0 + n].rearrange("(k p) n -> p k n", p=P), kt, n))

    for l in range(DEPTH):
        at[l, "in"] = len(units)
        for c0, n in PROJ:
            rows(w_in[l], 0, 4, c0, n)
            rows(w_in[l], 4, 4, c0, n)
        at[l, "gate0"] = len(units)
        rows(w_in[l], 0, 4, C_GATE, N)
        rows(w_in[l], 4, 4, C_GATE, N)
        at[l, "q"] = len(units)
        for i in range(2):
            rows(w_q_up[l], 0, KQ, i * 4 * QK, 4 * QK)
        at[l, "kv"] = len(units)
        rows(w_kv_up[l], 0, KKV, 0, D)
        at[l, "gate"] = len(units)
        for g in range(1, 4):
            rows(w_in[l], 0, 4, C_GATE + g * N, N)
            rows(w_in[l], 4, 4, C_GATE + g * N, N)
        at[l, "br"] = len(units)
        for w in (w_br_mla, w_br_swa):
            for n in range(2):
                rows(w[l], 0, 4, n * N, N)
        at[l, "out"] = len(units)
        for h in range(2):
            for n in range(2):
                rows(w_out[l], 4 * h, 4, n * N, N)
        at[l, "ffn"] = len(units)
        if l == 0:
            def down(j):
                for k in range(4 * j, min(4 * j + 4, FF // P), 2):
                    rows(dense_w_down[0], k, 2, 0, D)

            for j in range(DG):
                n = min(N, FF - j * N)
                for w in (dense_w_gate, dense_w_up):
                    rows(w[0], 0, 4, j * N, n)
                    rows(w[0], 4, 4, j * N, n)
                if j:
                    down(j - 1)
            down(DG - 1)
    UM = len(units)
    assert UM == at[1, "ffn"]

    with ExitStack() as ctx:
        used = [(nc.sbuf_base + 31) // 32 * 32]

        def place(name, shape, dt, offset=None):
            size = 4
            for s in shape[1:]:
                size *= s
            if offset is None:
                offset = used[0]
                used[0] += (size + 31) // 32 * 32
            assert offset + size <= nc.sbuf_usable_end, (name, offset + size)
            return nc.alloc_sbuf_tensor_at(name, shape, dt, offset=offset)

        def sem(name):
            return ctx.enter_context(nc.semaphore(name))

        raw = place("raw", [P, R, UNIT], F32)
        whi = place("whi", [P, S, UNIT], F32R)
        wlo = place("wlo", [P, S, UNIT], F32R)
        xs = place("xs", [P, NB, D], F32)
        o_xn = used[0]
        xn = place("xn", [P, NB, D], F32)
        sqT = place("sqT", [P, 4, SEQ], F32, o_xn)
        skT = place("skT", [P, SW_KV, SEQ], F32, o_xn + 4096)
        kdup = place("kdup", [P, NB, SW_KV, 2, SW_D], F32, o_xn + 6144)
        hTh = place("hTh", [P, KD, SEQ], F32R)
        hTl = place("hTl", [P, KD, SEQ], F32R)
        o_o = used[0]
        oTh = place("oTh", [P, 2, 4, SEQ], F32R)
        oTl = place("oTl", [P, 2, 4, SEQ], F32R)
        latTh = place("latTh", [P, KQ + KKV, SEQ], F32R, o_o)
        latTl = place("latTl", [P, KQ + KKV, SEQ], F32R, o_o + 8192)
        sg = place("sg", [P, 2, N], F32, o_o)
        av = place("av", [P, 2, N], F32, o_o + 4096)
        aTh = place("aTh", [P, 2, 4, P], F32R, o_o + 8192)
        aTl = place("aTl", [P, 2, 4, P], F32R, o_o + 12288)
        o_pj = used[0]
        pj = place("pj", [P, NB, C_GATE], F32)
        mg = place("mg", [P, NB, D], F32, o_pj)
        o_g = used[0]
        gates = place("gates", [P, 4, NB, N], F32)
        qn = place("qn", [P, NB, HEADS, QK], F32, o_g + 4096)
        kn = place("kn", [P, NB, HEADS, QK], F32, o_g + 4096 + 6144)
        heTh = place("heTh", [P, KD, P], F32R, o_g)
        heTl = place("heTl", [P, KD, P], F32R, o_g + 4096)
        oe = place("oe", [P, D], F32, o_g + 8192)
        pick = place("pick", [P, NB, P], F32, o_g + 12288)
        cw = place("cw", [P, NB, P], F32, o_g + 13312)
        cwT = place("cwT", [P, SEQ], F32, o_g + 14336)
        gout = place("gout", [P, NB, D], F32, o_g)
        qT = place("qT", [P, HEADS, SEQ], F32)
        o_kT = used[0]
        kT = place("kT", [P, HEADS, SEQ], F32)
        gfin = place("gfin", [P, D], F32, o_kT)
        bg = place("bg", [P, 2, N], F32)
        o_sx = used[0]
        sx = place("sx", [P, 2, N], F32)
        rt = place("rt", [P, 4, NB * HEADS * HALF], F32, o_sx)
        pT = place("pT", [P, 2, N], F32)
        cst = place("cst", [P, K_ALL], F32)
        gcol = place("gcol", [P, DEPTH * G_LAYER], F32)
        sk = place("sk", [P, DEPTH, HEADS], F32)
        sk_neg = place("sk_neg", [P, DEPTH, HEADS], F32)
        ones = place("ones", [P, P], F32)
        krt = place("krt", [P, 4, NB * HALF], F32)
        st = place("st", [P, 16], F32)
        eps = place("eps", [P, 1], F32)
        nm = place("nm", [P, 2, 4], F32)
        sink_d = place("sink_d", [P, 2, 4], F32)
        sink_e = place("sink_e", [P, 2, 4], F32)
        sums = place("sums", [P, 2, 4], F32)
        rsum = place("rsum", [P, 2, 4], F32)
        o_r = o_sx
        wr = place("wr", [P, KD, NE], F32, o_kT + 4096)
        wrh = place("wrh", [P, KD, NE], F32R, o_kT + 4096 + 256)
        wrl = place("wrl", [P, KD, NE], F32R, o_kT + 4096 + 512)
        lg = place("lg", [P, NB, NE], F32, o_r)
        above = place("above", [P, NB, NE, NE], F32, o_r + 64)
        ties = place("ties", [P, NB, NE, NE], F32, o_r + 576)
        rank = place("rank", [P, NB, NE], F32, o_r + 1088)
        mask = place("mask", [P, NB, NE], F32, o_r + 1152)
        lmax = place("lmax", [P, NB], F32, o_r + 1216)
        pe8 = place("pe8", [P, NB, NE], F32, o_r + 1248)
        psum8 = place("psum8", [P, NB], F32, o_r + 1312)
        comb = place("comb", [P, NB, NE], F32, o_r + 1344)
        pos = place("pos", [P, NB, NE], F32, o_r + 1408)
        most = place("most", [P, 1], F32, o_r + 1472)
        flag = place("flag", [P, 1], I32, o_r + 1504)
        posc = place("posc", [P, NB], F32, o_r + 1536)
        combc = place("combc", [P, NB], F32, o_r + 1568)
        grow = place("grow", [P, P], F32, o_r + 2048)

        A = [ctx.enter_context(nc.psum_tensor(f"A{i}", [P, N], F32)) for i in range(4)]
        T = [ctx.enter_context(nc.psum_tensor(f"T{i}", [P, N], F32)) for i in range(2)]
        DN = [ctx.enter_context(nc.psum_tensor(f"DN{i}", [P, N], F32)) for i in range(2)]

        TB = T + DN
        ident = cst[:, K_IDENT:K_IDENT + P]
        before = cst[:, K_BEFORE:K_BEFORE + P]

        raw_landed = [sem(f"raw_landed{i}") for i in range(R)]
        hi_done = sem("hi_done")
        lo_done = sem("lo_done")
        unit_used = sem("unit_used")
        const_landed = sem("const_landed")
        gain_landed = sem("gain_landed")
        x_landed = sem("x_landed")
        sink_landed = sem("sink_landed")
        rows_landed = sem("rows_landed")
        sink_negated = sem("sink_negated")
        router_landed = sem("router_landed")
        gfin_landed = sem("gfin_landed")
        bg_landed = [[sem(f"bg_landed{l}_{i}") for i in range(4)] for l in range(DEPTH)]
        out_landed = sem("out_landed")
        ones_set = sem("ones_set")
        gain_T = sem("gain_T")
        gain_done = sem("gain_done")
        act_own = sem("act_own")
        dve_own = sem("dve_own")

        def layered(name):
            return [sem(f"{name}{l}") for l in range(DEPTH)]

        norm_root = [sem(f"norm_root{n}") for n in range(5)]
        norm_inv = [sem(f"norm_inv{n}") for n in range(5)]
        rows_ready = sem("rows_ready")
        norm_T = [sem(f"norm_T{n}") for n in range(4)]
        norm_hi = [sem(f"norm_hi{n}") for n in range(4)]
        norm_lo = [sem(f"norm_lo{n}") for n in range(4)]
        proj_act, proj_dve = layered("proj_act"), layered("proj_dve")
        gate_added, gate_ready = layered("gate_added"), layered("gate_ready")
        lat_root, lat_inv = layered("lat_root"), layered("lat_inv")
        win_T, win_act, win_dve = layered("win_T"), layered("win_act"), layered("win_dve")
        lat_T, lat_hi, lat_lo = layered("lat_T"), layered("lat_hi"), layered("lat_lo")
        up_act, up_dve = layered("up_act"), layered("up_dve")
        rope_done, kdup_done = layered("rope_done"), layered("kdup_done")
        qk_T, qk_act, qk_dve = layered("qk_T"), layered("qk_act"), layered("qk_dve")
        scored, masked, max_ready = layered("scored"), layered("masked"), layered("max_ready")
        exp_done, probs_ready = layered("exp_done"), layered("probs_ready")
        probs_T, probs_T_out = layered("probs_T"), layered("probs_T_out")
        pv_done, o_hi, o_lo = layered("pv_done"), layered("o_hi"), layered("o_lo")
        gated, merged = layered("gated"), layered("merged")
        mg_T, mg_hi, mg_lo = layered("mg_T"), layered("mg_hi"), layered("mg_lo")
        x_added = layered("x_added")
        silu_done, ff_ready = layered("silu_done"), layered("ff_ready")
        ff_T, ff_hi, ff_lo = layered("ff_T"), layered("ff_hi"), layered("ff_lo")
        down_done, down_added = sem("down_done"), sem("down_added")
        wr_hi, wr_lo = sem("wr_hi"), sem("wr_lo")
        logits_done, mask_ready, counted = sem("logits_done"), sem("mask_ready"), sem("counted")
        lmax_ready, lexp_done = sem("lmax_ready"), sem("lexp_done")
        routed, selected = sem("routed"), sem("selected")
        picked, gathered = sem("picked"), sem("gathered")
        he_hi, he_lo = sem("he_hi"), sem("he_lo")
        cw_T, cw_out = sem("cw_T"), sem("cw_out")
        oe_full, oe_act, oe_dve, scattered = sem("oe_full"), sem("oe_act"), sem("oe_dve"), sem("scattered")
        last_full, last_added = sem("last_full"), sem("last_added")

        X_DENSE = 4 + 4 * DG

        def times(e, per):
            return 0 if e is None else e * per

        def split_hi(act, u, e=None):
            n = UNIT if u >= UM else units[u][1] * units[u][2]
            act.wait_ge(raw_landed[u % R], 16 * (u // R + 1) + times(e, 16 * EU // R))
            if u >= S:
                act.wait_ge(unit_used, u - S + 1 + times(e, EU))
            nc.scalar.activation(whi[:, u % S, :n], raw[:, u % R, :n], ACT.Copy).then_inc(hi_done, 1)

        def split_lo(dve, u, e=None):
            n = UNIT if u >= UM else units[u][1] * units[u][2]
            dve.wait_ge(hi_done, u + 1 + times(e, EU))
            nc.vector.tensor_tensor(wlo[:, u % S, :n], raw[:, u % R, :n],
                                    whi[:, u % S, :n].bitcast(F32), ALU.subtract).then_inc(lo_done, 1)

        class Lead:

            def __init__(self, eng, split, first, last, e=None):
                self.eng, self.split, self.next, self.last, self.e = eng, split, first, last, e

            def to(self, u):
                while self.next < min(u, self.last):
                    self.split(self.eng, self.next, self.e)
                    self.next += 1

        def split_tile(u, kk, n, c0=0, width=None):
            a = kk * n + c0
            b = a + (n if width is None else width)
            return whi[:, u % S, a:b], wlo[:, u % S, a:b]

        def product(o, hi, lo, wh, wl, start, stop):
            nc.tensor.matmul(o, hi, wh, start=start, stop=False)
            nc.tensor.matmul(o, hi, wl, start=False, stop=False)
            return nc.tensor.matmul(o, lo, wh, start=False, stop=stop)

        def vm(b, n):
            return pj[:, b, n * 4 * VD:(n + 1) * 4 * VD].rearrange("p (h d) -> p h d", h=4)

        def qk_target(i):
            if i < 4:
                return qT[0:QK, 2 * i:2 * i + 2, :].rearrange("p h t -> p (h t)"), QK, N, MLA_SCALE
            return kT[0:QK, 2 * i - 8:2 * i - 6, :].rearrange("p h t -> p (h t)"), QK, N, 1.0

        BR = [[A[:2], A[2:]], [DN, T]]
        MB = A[:2] + T
        OUT = [DN, A[2:]]

        def down_order(j):
            if j < DG:
                return [(b, h, [DN, T][b][h]) for b in range(NB) for h in range(2)]
            return [(b, h, A[2 * b + h]) for h in range(2) for b in range(NB)]

        block = ctx.enter_context(nc.Block())

        @block.sync
        def _(sp):
            sp.dma_start(xs[:], x[0].rearrange("(b p) d -> p b d", p=P)).then_inc(x_landed, 16)
            sp.dma_start(cst[:], consts).then_inc(const_landed, 16)
            for l in range(DEPTH):
                r = l * G_LAYER
                for g, k, o in ((g_attn_norm, KD, G_ATTN), (g_q_norm, KQ, G_Q), (g_kv_norm, KKV, G_KV),
                                (g_ffn_norm, KD, G_FFN)):
                    sp.dma_start(grow[r + o:r + o + k, :], g[l].rearrange("(k p) -> k p", p=P)
                                 ).then_inc(gain_landed, 16)
            for src, dst in enumerate((qT, kT)):
                sp.dma_start(dst[QK:AUG], mask_rows[:, src:src + 1, :].broadcast_to([NB, HEADS, SEQ])
                             ).then_inc(rows_landed, 16)
            sp.dma_start(sk[:], sinks.rearrange("(a l) h -> a l h", a=1).broadcast_to([P, DEPTH, HEADS])
                         ).then_inc(sink_landed, 16)

            def load(u, dst_u, src, kt, n, e=None):
                if u >= R:
                    sp.wait_ge(lo_done, u - R + 1 + times(e, EU))
                sp.dma_start(raw[:, dst_u, :kt * n].rearrange("p (k n) -> p k n", k=kt), src
                             ).then_inc(raw_landed[dst_u], 16)

            for u, (src, kt, n) in enumerate(units):
                load(u, u % R, src, kt, n)

            def expert_loads(base, e):
                gate = moe_w_gate[0, bass.ds(e, 1)].rearrange("a (k p) n -> p (a k) n", p=P)
                up = moe_w_up[0, bass.ds(e, 1)].rearrange("a (k p) n -> p (a k) n", p=P)
                dn = moe_w_down[0, bass.ds(e, 1)].rearrange("a (k p) n -> p (a k) n", p=P)
                i = 0

                def take(src, kt, n):
                    nonlocal i
                    load(base + i, (base + i) % R, src, kt, n, e)
                    i += 1

                for j in range(EG + 1):
                    if j < EG:
                        for w in (gate, up):
                            take(w[:, 0:4, j * N:(j + 1) * N], 4, N)
                            take(w[:, 4:8, j * N:(j + 1) * N], 4, N)
                    if j:
                        take(dn[:, 4 * j - 4:4 * j - 2, :], 2, D)
                        take(dn[:, 4 * j - 2:4 * j, :], 2, D)

            with sp.Fori(0, NE) as e:
                expert_loads(UM, e)
            sp.wait_ge(routed, 1)
            more = sp.value_load(flag[0:1, 0:1], min_val=0, max_val=1)
            with sp.If(more > 0):
                with sp.Fori(0, NE) as e:
                    expert_loads(UM + NE * EU, e)
            for b in range(NB):
                sp.wait_ge(rows_ready, NB + b + 1)
                sp.dma_start(out[0, b * P:(b + 1) * P, :], gout[:, b, :]).then_inc(out_landed, 16)
            sp.wait_ge(out_landed, 16 * NB)

        @block.scalar
        def _(act):
            own = [0]

            def done(ins):
                own[0] += 1
                ins.then_inc(act_own, 1)
                return own[0]

            lead = Lead(act, split_hi, 0, UM)

            def bias_chunk(l, g):
                act.dma_start(bg[:, g % 2, :], b_gate[l:l + 1, g * N:(g + 1) * N].broadcast_to([P, N])
                              ).then_inc(bg_landed[l][g], 16)

            def root(n):
                for b in range(NB):
                    v = done(nc.scalar.activation(xn[:, b, :], xs[:, b, :], ACT.Square, accum_out=st[:, b:b + 1]))
                act.wait_ge(act_own, v)
                nc.scalar.activation(st[:, 2:4], st[:, 0:2], ACT.Sqrt, scale=1.0 / D, bias=eps[:]
                                     ).then_inc(norm_root[n], 1)

            def norm_high(n, gains):
                for i in range(4):
                    act.wait_ge(norm_T[n], i + 1)
                    for kk in range(2):
                        k = 2 * i + kk
                        nc.scalar.activation(hTh[:, k, :], TB[i][:, kk * SEQ:(kk + 1) * SEQ], ACT.Copy,
                                             scale=gcol[:, gains + k:gains + k + 1]).then_inc(norm_hi[n], 1)

            act.wait_ge(ones_set, 2)
            act.wait_ge(x_landed, 16)
            for l in range(DEPTH):
                if l == 0:
                    act.wait_ge(gain_T, 1)
                    nc.scalar.activation(gcol[:], T[0][:, 0:DEPTH * G_LAYER], ACT.Copy).then_inc(gain_done, 1)
                    act.wait_ge(gain_done, 1)
                bias_chunk(l, 0)
                bias_chunk(l, 1)
                lead.to(at[l, "in"] + 2)
                norm_high(l, l * G_LAYER + G_ATTN)
                root(l)
                for g, (c0, n) in enumerate(PROJ):
                    u = at[l, "in"] + 2 * g + 1
                    lead.to(u + 3)
                    act.wait_ge(unit_used, u + 1)
                    act.wait_ge(norm_inv[l], 1)
                    nc.scalar.activation(pj[:, 0, c0:c0 + n], A[2 * (g % 2)][:, :n], ACT.Copy,
                                         scale=st[:, 12:13]).then_inc(proj_act[l], 1)
                for i in range(3):
                    act.wait_ge(lat_T[l], i + 1)
                    for kk in range(2 if i < 2 else 1):
                        k = 2 * i + kk
                        c = l * G_LAYER + G_Q + k
                        nc.scalar.activation(latTh[:, k, :], TB[i][:, kk * SEQ:(kk + 1) * SEQ], ACT.Copy,
                                             scale=gcol[:, c:c + 1]).then_inc(lat_hi[l], 1)
                act.wait_ge(proj_act[l], 3)
                act.wait_ge(proj_dve[l], 3)
                for b in range(NB):
                    done(nc.scalar.activation(xn[:, b, 0:Q_LORA], pj[:, b, 0:Q_LORA], ACT.Square,
                                              accum_out=st[:, 4 + b:5 + b]))
                    done(nc.scalar.activation(xn[:, b, Q_LORA:C_KR], pj[:, b, C_KV:C_KR], ACT.Square,
                                              accum_out=st[:, 6 + b:7 + b]))
                act.wait_ge(act_own, own[0])
                nc.scalar.activation(st[:, 8:10], st[:, 4:6], ACT.Sqrt, scale=1.0 / Q_LORA, bias=eps[:]
                                     ).then_inc(lat_root[l], 1)
                nc.scalar.activation(st[:, 10:12], st[:, 6:8], ACT.Sqrt, scale=1.0 / KV_LORA, bias=eps[:]
                                     ).then_inc(lat_root[l], 1)
                for r in range(2):
                    nc.scalar.activation(kdup[:, :, :, r, :],
                                         pj[:, :, C_KS:C_VS].rearrange("p b (k d) -> p b k d", k=SW_KV),
                                         ACT.Copy).then_inc(kdup_done[l], 1)
                lead.to(at[l, "gate0"] + 4)
                act.wait_ge(win_T[l], 1)
                nc.scalar.activation(sqT[:, 0:2, :].rearrange("p h t -> p (h t)"), T[0][:], ACT.Copy,
                                     scale=SWA_SCALE).then_inc(win_act[l], 1)
                act.wait_ge(win_T[l], 3)
                nc.scalar.activation(skT[:].rearrange("p h t -> p (h t)"), DN[1][:], ACT.Copy
                                     ).then_inc(win_act[l], 1)
                act.wait_ge(lat_inv[l], 1)
                for i in range(2):
                    u = at[l, "q"] + i
                    lead.to(u + 3)
                    act.wait_ge(unit_used, u + 1)
                    nc.scalar.activation(qn[:, 0, 4 * i:4 * i + 4, :], [A, DN][i][0][:, :4 * QK], ACT.Copy,
                                         scale=st[:, 4:5]).then_inc(up_act[l], 1)
                lead.to(at[l, "kv"] + 3)
                act.wait_ge(unit_used, at[l, "kv"] + 1)
                for n in range(2):
                    kv = A[n][:].rearrange("p (h c) -> p h c", h=4)
                    nc.scalar.activation(kn[:, 0, 4 * n:4 * n + 4, 0:NOPE], kv[:, :, 0:NOPE], ACT.Copy,
                                         scale=st[:, 6:7]).then_inc(up_act[l], 1)
                    nc.scalar.activation(vm(0, n), kv[:, :, NOPE:], ACT.Copy, scale=st[:, 6:7]
                                         ).then_inc(up_act[l], 1)
                for i in range(0, QT_FILLS, 2):
                    act.wait_ge(qk_T[l], i + 1)
                    dst, p, w, scale = qk_target(i)
                    nc.scalar.activation(dst, T[0][0:p, 0:w], ACT.Copy, scale=scale).then_inc(qk_act[l], 1)

                def exps(f):
                    kind, b, heads = FILLS[f]
                    w = P * (b + 1)
                    act.wait_ge(max_ready[l], f + 1)
                    if f >= 2 and kind == 0:
                        act.wait_ge(probs_T[l], f - 1)
                    if kind:
                        done(nc.scalar.activation(sink_e[:, f % 2, :len(heads)], sink_d[:, f % 2, :len(heads)],
                                                  ACT.Exp))
                    for i in range(len(heads)):
                        s = sx[:, f % 2, i * w:(i + 1) * w]
                        scores = s if kind else A[f % 2][:, i * w:(i + 1) * w]
                        nc.scalar.activation(s, scores, ACT.Exp, bias=nm[:, f % 2, i:i + 1],
                                             accum_out=sums[:, f % 2, i:i + 1]).then_inc(exp_done[l], 1)

                def probs_out(f):
                    act.wait_ge(probs_T[l], f + 1)
                    if f >= 2:
                        act.wait_ge(pv_done[l], f - 1)
                    nc.scalar.activation(pT[:, f % 2, :], T[f % 2][:], ACT.Copy).then_inc(probs_T_out[l], 1)

                def o_high(i):
                    kind, b = i // NB, i % NB
                    act.wait_ge(pv_done[l], LAST[i] + 1)
                    nc.scalar.activation(oTh[:, kind, :, b * P:(b + 1) * P],
                                         DN[b][:].rearrange("p (j t) -> p j t", j=4), ACT.Copy
                                         ).then_inc(o_hi[l], 1)

                for f in range(NF):
                    lead.to(at[l, "gate"] + f // 2 + 3)
                    exps(f)
                    if f:
                        probs_out(f - 1)
                    if f - 2 in LAST:
                        o_high(LAST.index(f - 2))
                    if f == 0:
                        act.wait_ge(gate_added[l], 2)
                        bias_chunk(l, 2)
                    if f == 4:
                        act.wait_ge(gate_added[l], 4)
                        bias_chunk(l, 3)
                lead.to(at[l, "br"] + 3)
                probs_out(NF - 1)
                o_high(3)
                for n in range(2):
                    act.wait_ge(gate_added[l], 6 + 2 * n)
                    for b in range(NB):
                        for h in range(2):
                            g = gates[:, 2 * h + n, b, :]
                            nc.scalar.activation(g, g, ACT.Sigmoid).then_inc(gate_ready[l], 1)
                for i in range(4):
                    lead.to(at[l, "out"] + (2 if i < 2 else 3))
                    act.wait_ge(mg_T[l], i + 1)
                    nc.scalar.activation(hTh[:, 2 * i:2 * i + 2, :], MB[i][:].rearrange("p (k t) -> p k t", k=2),
                                         ACT.Copy).then_inc(mg_hi[l], 1)
                lead.to(at[l, "ffn"] + 2)
                norm_high(2 + l, l * G_LAYER + G_FFN)
                root(2 + l)
                if l == 0:
                    lead.to(at[0, "ffn"] + 4)
                    act.wait_ge(norm_inv[2], 1)
                if l == 0:
                    u0 = at[0, "ffn"]
                    for j in range(DG + 1):
                        n = min(N, FF - j * N)
                        u = u0 + group_at(j)
                        lead.to(u + (4 if j < DG else 2))
                        if j < DG:
                            act.wait_ge(unit_used, u + 2)
                            for b in range(NB):
                                if j:
                                    act.wait_ge(ff_ready[0], NB * (j - 1) + b + 1)
                                nc.scalar.activation(sg[:, b, :n], A[b][:, :n], ACT.Silu, scale=st[:, 12 + b:13 + b]
                                                     ).then_inc(silu_done[0], 1)
                        if j:
                            m = min(N, FF - (j - 1) * N)
                            for b in range(NB):
                                q = NB * (j - 1) + b
                                act.wait_ge(ff_T[0], q + 1)
                                nc.scalar.activation(aTh[:, b, :m // P, :], T[b][:, :m].rearrange("p (k t) -> p k t", t=P),
                                                     ACT.Copy).then_inc(ff_hi[0], 1)

            act.wait_ge(router_landed, 16)
            nc.scalar.activation(wrh[:], wr[:], ACT.Copy).then_inc(wr_hi, 1)
            act.wait_ge(lmax_ready, 1)
            for b in range(NB):
                nc.scalar.activation(pe8[:, b, :], lg[:, b, :], ACT.Exp, bias=lmax[:, b:b + 1]
                                     ).then_inc(lexp_done, 1)

            def tokens_high(i, n, e):
                act.wait_ge(gathered, 2 * n + i + 1 + e * 2)
                for kk in range(4):
                    k = 4 * i + kk
                    c = G_LAYER + G_FFN + k
                    nc.scalar.activation(heTh[:, k, :], T[i][:, kk * P:(kk + 1) * P], ACT.Copy,
                                         scale=gcol[:, c:c + 1]).then_inc(he_hi, 1)

            def expert(base, n, e, following):
                ahead = Lead(act, split_hi, base, base + EU + (S if following else 0), e)
                ahead.next += S
                for j in range(EG + 1):
                    u = base + group_at(j)
                    ahead.to(u + (4 if j < EG else 2))
                    if j < EG:
                        act.wait_ge(unit_used, u + 2 + e * EU)
                        if j >= 2:
                            act.wait_ge(ff_ready[1], EG * n + j - 1 + e * EG)
                        nc.scalar.activation(sg[:, j % 2, :], A[j % 2][:], ACT.Silu).then_inc(silu_done[1], 1)
                    ahead.to(u + (5 if j < EG else 2))
                    if j:
                        act.wait_ge(ff_T[1], EG * n + j + e * EG)
                        nc.scalar.activation(aTh[:, (j - 1) % 2], T[(j - 1) % 2][:].rearrange("p (k t) -> p k t", k=4),
                                             ACT.Copy).then_inc(ff_hi[1], 1)
                    if j == 1:
                        act.wait_ge(cw_T, n + 1 + e)
                        nc.scalar.activation(cwT[:], T[1][:, :SEQ], ACT.Copy).then_inc(cw_out, 1)
                    if following and j >= EG - 1:
                        if j < EG:
                            ahead.to(u + 6)
                        tokens_high(j - EG + 1, n + 1, e)
                ahead.to(base + EU + S)
                act.wait_ge(unit_used, base + EU + e * EU)
                nc.scalar.activation(oe[:, 0:N], DN[0][:], ACT.Copy).then_inc(oe_act, 1)

            def head(base, n, e):
                Lead(act, split_hi, base, base + S, e).to(base + S)
                for i in range(2):
                    tokens_high(i, n, e)

            head(UM, 0, 0)
            with act.Fori(0, NE - 1) as e:
                expert(UM, 0, e, True)
            expert(UM + (NE - 1) * EU, NE - 1, 0, False)
            act.wait_ge(routed, 1)
            more = act.value_load(flag[0:1, 0:1], min_val=0, max_val=1)
            with act.If(more > 0):
                with act.Fori(0, NE) as e:
                    head(UM + NE * EU, NE, e)
                    expert(UM + NE * EU, NE, e, False)
            act.wait_ge(scattered, 1)
            root(4)

        @block.vector
        def _(dve):
            own = [0]
            base_own = [0]

            def done(ins):
                own[0] += 1
                ins.then_inc(dve_own, 1)
                return own[0]

            def settle():
                dve.wait_ge(dve_own, own[0])

            lead = Lead(dve, split_lo, 0, UM)

            def invert(n):
                dve.wait_ge(norm_root[n], 1)
                nc.vector.reciprocal(st[:, 12:14], st[:, 2:4]).then_inc(norm_inv[n], 1)
                dve.wait_ge(norm_inv[n], 1)

            def norm_low(n, gains):
                for i in range(4):
                    dve.wait_ge(norm_hi[n], 2 * i + 2)
                    for kk in range(2):
                        k = 2 * i + kk
                        nc.vector.scalar_tensor_tensor(
                            hTl[:, k, :], TB[i][:, kk * SEQ:(kk + 1) * SEQ], gcol[:, gains + k:gains + k + 1],
                            hTh[:, k, :].bitcast(F32), ALU.mult, ALU.subtract).then_inc(norm_lo[n], 1)

            nc.vector.memset(ones[:], 1.0).then_inc(ones_set, 1)
            nc.vector.memset(eps[:], EPS).then_inc(ones_set, 1)
            for l in range(DEPTH):
                if l == 0:
                    dve.wait_ge(gain_done, 1)
                lead.to(at[l, "in"] + 2)
                norm_low(l, l * G_LAYER + G_ATTN)
                invert(l)
                for g, (c0, n) in enumerate(PROJ):
                    u = at[l, "in"] + 2 * g + 1
                    lead.to(u + 3)
                    dve.wait_ge(unit_used, u + 1)
                    nc.vector.tensor_scalar(pj[:, 1, c0:c0 + n], A[2 * (g % 2) + 1][:, :n], st[:, 13:14], None,
                                            ALU.mult).then_inc(proj_dve[l], 1)
                for i in range(3):
                    dve.wait_ge(lat_hi[l], min(2 * i + 2, KQ + KKV))
                    for kk in range(2 if i < 2 else 1):
                        k = 2 * i + kk
                        c = l * G_LAYER + G_Q + k
                        nc.vector.scalar_tensor_tensor(
                            latTl[:, k, :], TB[i][:, kk * SEQ:(kk + 1) * SEQ], gcol[:, c:c + 1],
                            latTh[:, k, :].bitcast(F32), ALU.mult, ALU.subtract).then_inc(lat_lo[l], 1)
                dve.wait_ge(proj_act[l], 3)
                dve.wait_ge(proj_dve[l], 3)

                def rope(x1, x2, cos, sin, t, o1, o2, outs):
                    done(nc.vector.tensor_tensor(t[0], x1, cos, ALU.mult))
                    done(nc.vector.tensor_tensor(t[1], x2, sin, ALU.mult))
                    done(nc.vector.tensor_tensor(t[2], x1, sin, ALU.mult))
                    done(nc.vector.tensor_tensor(t[3], x2, cos, ALU.mult))
                    settle()
                    nc.vector.tensor_tensor(o1, outs(t[0]), outs(t[1]), ALU.subtract).then_inc(rope_done[l], 1)
                    nc.vector.tensor_tensor(o2, outs(t[2]), outs(t[3]), ALU.add).then_inc(rope_done[l], 1)

                cos = cst[:, K_COS:K_SIN].rearrange("p (b r) -> p b r", b=NB)
                sin = cst[:, K_SIN:K_DIST].rearrange("p (b r) -> p b r", b=NB)
                kr = pj[:, :, C_KR:C_QS]
                tk = [krt[:, i].rearrange("p (b r) -> p b r", b=NB) for i in range(4)]

                def heads_of(a):
                    return a.unsqueeze(2).broadcast_to([P, NB, HEADS, HALF])

                rope(kr[:, :, :HALF], kr[:, :, HALF:], cos, sin, tk, kn[:, :, :, NOPE:NOPE + HALF],
                     kn[:, :, :, NOPE + HALF:], heads_of)
                dve.wait_ge(lat_root[l], 2)
                nc.vector.reciprocal(st[:, 4:8], st[:, 8:12]).then_inc(lat_inv[l], 1)
                dve.wait_ge(lat_inv[l], 1)

                def gate_add(g):
                    u = at[l, "gate0"] + 1 if g == 0 else at[l, "gate"] + 2 * g - 1
                    dve.wait_ge(unit_used, u + 1)
                    dve.wait_ge(bg_landed[l][g], 16)
                    for b in range(NB):
                        nc.vector.scalar_tensor_tensor(gates[:, g, b, :], A[2 + b][:], st[:, 12 + b:13 + b],
                                                       bg[:, g % 2, :], ALU.mult, ALU.add
                                                       ).then_inc(gate_added[l], 1)

                lead.to(at[l, "gate0"] + 4)
                gate_add(0)
                dve.wait_ge(win_T[l], 2)
                nc.vector.tensor_scalar(sqT[:, 2:4, :].rearrange("p h t -> p (h t)"), T[1][:], SWA_SCALE, None,
                                        ALU.mult).then_inc(win_dve[l], 1)
                for i in range(2):
                    u = at[l, "q"] + i
                    lead.to(u + 3)
                    dve.wait_ge(unit_used, u + 1)
                    nc.vector.tensor_scalar(qn[:, 1, 4 * i:4 * i + 4, :], [A, DN][i][1][:, :4 * QK].rearrange(
                        "p (h c) -> p h c", h=4), st[:, 5:6], None, ALU.mult).then_inc(up_dve[l], 1)
                dve.wait_ge(up_act[l], 2)
                dve.wait_ge(up_dve[l], 2)
                tq = [rt[:, i].rearrange("p (b h r) -> p b h r", b=NB, h=HEADS) for i in range(4)]
                x1, x2 = qn[:, :, :, NOPE:NOPE + HALF], qn[:, :, :, NOPE + HALF:]
                rope(x1, x2, heads_of(cos), heads_of(sin), tq, x1, x2, lambda a: a)
                lead.to(at[l, "kv"] + 3)
                dve.wait_ge(unit_used, at[l, "kv"] + 1)
                for n in range(2):
                    kv = A[2 + n][:].rearrange("p (h c) -> p h c", h=4)
                    nc.vector.tensor_scalar(kn[:, 1, 4 * n:4 * n + 4, 0:NOPE], kv[:, :, 0:NOPE], st[:, 7:8], None,
                                            ALU.mult).then_inc(up_dve[l], 1)
                    nc.vector.tensor_scalar(vm(1, n), kv[:, :, NOPE:], st[:, 7:8], None, ALU.mult
                                            ).then_inc(up_dve[l], 1)
                for i in range(1, QT_FILLS, 2):
                    dve.wait_ge(qk_T[l], i + 1)
                    dst, p, w, scale = qk_target(i)
                    nc.vector.tensor_scalar(dst, T[1][0:p, 0:w], scale, None, ALU.mult).then_inc(qk_dve[l], 1)

                def mask_max(f):
                    kind, b, heads = FILLS[f]
                    nh, w, off = len(heads), P * (b + 1), P * (1 - b)
                    dve.wait_ge(scored[l], f + 1)
                    s = sx[:, f % 2, :].rearrange("p (h k) -> p h k", h=nh)
                    sc = A[f % 2][:].rearrange("p (h k) -> p h k", h=nh)
                    neg = nm[:, f % 2, :nh]
                    if kind == 0:
                        nc.vector.tensor_reduce(neg, sc, AX, ALU.max, negate=True).then_inc(max_ready[l], 1)
                    else:
                        dve.wait_ge(probs_T[l], f - 1)
                        tab = cst[:, K_DIST + off:K_DIST + SEQ]
                        for i, h in enumerate(heads):
                            last = nc.vector.scalar_tensor_tensor(s[:, i], tab, -SLOPES[h], sc[:, i], ALU.mult, ALU.add)
                            if i < nh - 1:
                                done(last)
                        last.then_inc(masked[l], 1)
                        dve.wait_ge(masked[l], f + 1 - MLA_FILLS)
                        settle()
                        done(nc.vector.tensor_reduce(neg, s, AX, ALU.max, negate=True))
                        settle()
                        sink = slice(heads[0], heads[-1] + 1, 2)
                        done(nc.vector.tensor_tensor(neg, neg, sk_neg[:, l, sink], ALU.min))
                        settle()
                        nc.vector.tensor_tensor(sink_d[:, f % 2, :nh], sk[:, l, sink], neg, ALU.add
                                                ).then_inc(max_ready[l], 1)

                def normalise(f):
                    kind, b, heads = FILLS[f]
                    nh, w = len(heads), P * (b + 1)
                    s = sx[:, f % 2, :].rearrange("p (h k) -> p h k", h=nh)
                    sm, r = sums[:, f % 2, :nh], rsum[:, f % 2, :nh]
                    dve.wait_ge(exp_done[l], EXPS[f])
                    if kind:
                        done(nc.vector.tensor_tensor(sm, sm, sink_e[:, f % 2, :nh], ALU.add))
                        settle()
                    done(nc.vector.reciprocal(r, sm))
                    settle()
                    nc.vector.tensor_tensor(s, s, r.unsqueeze(2).broadcast_to([P, nh, w]), ALU.mult
                                            ).then_inc(probs_ready[l], 1)

                def o_low(i):
                    kind, b = i // NB, i % NB
                    dve.wait_ge(o_hi[l], i + 1)
                    o = slice(b * P, (b + 1) * P)
                    nc.vector.tensor_tensor(oTl[:, kind, :, o], DN[b][:].rearrange("p (j t) -> p j t", j=4),
                                            oTh[:, kind, :, o].bitcast(F32), ALU.subtract).then_inc(o_lo[l], 1)

                if l == 0:
                    dve.wait_ge(sink_landed, 16)
                    nc.vector.tensor_scalar(sk_neg[:], sk[:], -1.0, None, ALU.mult).then_inc(sink_negated, 1)
                    dve.wait_ge(sink_negated, 1)
                mask_max(0)
                for f in range(NF):
                    lead.to(at[l, "gate"] + f // 2 + 3)
                    if f + 1 < NF:
                        mask_max(f + 1)
                    normalise(f)
                    if f in (2, 6, 10):
                        gate_add((f + 2) // 4)
                    if f - 3 in LAST:
                        o_low(LAST.index(f - 3))
                lead.to(at[l, "br"] + 3)
                for i in range(4):
                    if LAST[i] + 3 >= NF:
                        o_low(i)
                for kind in range(2):
                    for n in range(2):
                        u = at[l, "br"] + 2 * kind + n
                        lead.to(u + 3)
                        dve.wait_ge(unit_used, u + 1)
                        dve.wait_ge(gate_ready[l], 4 * n + 4)
                        c = slice(n * N, (n + 1) * N)
                        for b in range(NB):
                            g = gates[:, 2 * kind + n, b, :]
                            nc.vector.tensor_tensor(g if kind else mg[:, b, c], BR[kind][n][b][:], g, ALU.mult
                                                    ).then_inc(gated[l], 1)
                        if kind:
                            dve.wait_ge(gated[l], 4 + 2 * (n + 1))
                            for b in range(NB):
                                nc.vector.tensor_tensor(mg[:, b, c], mg[:, b, c], gates[:, 2 + n, b, :], ALU.add
                                                        ).then_inc(merged[l], 1)
                for n in range(2):
                    for i in range(2 * n, 2 * n + 2):
                        lead.to(at[l, "out"] + (2 if i < 2 else 3))
                        dve.wait_ge(mg_hi[l], i + 1)
                        nc.vector.tensor_tensor(hTl[:, 2 * i:2 * i + 2, :],
                                                MB[i][:].rearrange("p (k t) -> p k t", k=2),
                                                hTh[:, 2 * i:2 * i + 2, :].bitcast(F32), ALU.subtract
                                                ).then_inc(mg_lo[l], 1)
                for n in range(2):
                    u = at[l, "out"] + 2 + n
                    lead.to(u + 3)
                    dve.wait_ge(unit_used, u + 1)
                    for b in range(NB):
                        c = xs[:, b, n * N:(n + 1) * N]
                        nc.vector.tensor_tensor(c, OUT[n][b][:], c, ALU.add).then_inc(x_added[l], 1)
                norm_low(2 + l, l * G_LAYER + G_FFN)
                invert(2 + l)
                if l == 0:
                    u0 = at[0, "ffn"]
                    for j in range(DG + 1):
                        n = min(N, FF - j * N)
                        u = u0 + group_at(j)
                        lead.to(u + (4 if j < DG else 2))
                        if j:
                            m = min(N, FF - (j - 1) * N)
                            for b in range(NB):
                                dve.wait_ge(ff_hi[0], NB * (j - 1) + b + 1)
                                nc.vector.tensor_tensor(aTl[:, b, :m // P, :], T[b][:, :m].rearrange("p (k t) -> p k t", t=P),
                                                        aTh[:, b, :m // P, :].bitcast(F32), ALU.subtract
                                                        ).then_inc(ff_lo[0], 1)
                        if j < DG:
                            lead.to(u + 6)
                            dve.wait_ge(unit_used, u + 4)
                            for b in range(NB):
                                dve.wait_ge(silu_done[0], NB * j + b + 1)
                                if j:
                                    dve.wait_ge(ff_T[0], NB * j)
                                nc.vector.scalar_tensor_tensor(av[:, b, :n], A[2 + b][:, :n], st[:, 12 + b:13 + b],
                                                               sg[:, b, :n], ALU.mult, ALU.mult
                                                               ).then_inc(ff_ready[0], 1)
                        if j:
                            lead.to(u0 + down_at(j - 1, DG) + (2 if j < DG else 1) + 2)
                            for i, (b, h, bank) in enumerate(down_order(j)):
                                if i == 3:
                                    dve.wait_ge(unit_used, u0 + down_at(j - 1, DG) + m // SEQ)
                                else:
                                    dve.wait_ge(down_done, 3 * (j - 1) + i + 1)
                                c = xs[:, b, h * N:(h + 1) * N]
                                dve.wait_ge(x_added[0], 4 * j)
                                nc.vector.tensor_tensor(c, bank[:], c, ALU.add).then_inc(x_added[0], 1)
                    dve.wait_ge(x_added[0], X_DENSE)

            dve.wait_ge(wr_hi, 1)
            nc.vector.tensor_tensor(wrl[:], wr[:], wrh[:].bitcast(F32), ALU.subtract).then_inc(wr_lo, 1)
            dve.wait_ge(logits_done, 1)
            for b in range(NB):
                done(nc.vector.tensor_scalar(lg[:, b], A[0][:, b * NE:(b + 1) * NE], st[:, 12 + b:13 + b], None,
                                             ALU.mult))
            settle()
            done(nc.vector.tensor_reduce(lmax[:], lg[:], AX, ALU.max))
            settle()
            nc.vector.tensor_scalar(lmax[:], lmax[:], -1.0, None, ALU.mult).then_inc(lmax_ready, 1)
            for b in range(NB):
                nc.vector.tensor_scalar(xn[:, b, :], xs[:, b, :], st[:, 12 + b:13 + b], None, ALU.mult
                                        ).then_inc(rows_ready, 1)
            for b in range(NB):
                other = lg[:, b].unsqueeze(1).broadcast_to([P, NE, NE])
                this = lg[:, b].unsqueeze(2).broadcast_to([P, NE, NE])
                done(nc.vector.tensor_tensor(above[:, b], other, this, ALU.is_gt))
                done(nc.vector.tensor_tensor(ties[:, b], other, this, ALU.is_equal))
            settle()
            lower = cst[:, K_LOWER:K_ALL].rearrange("p (e f) -> p e f", e=NE)
            for b in range(NB):
                done(nc.vector.tensor_tensor(ties[:, b], ties[:, b], lower, ALU.mult))
            settle()
            done(nc.vector.tensor_tensor(above[:], above[:], ties[:], ALU.add))
            settle()
            done(nc.vector.tensor_reduce(rank[:], above[:], AX, ALU.add))
            settle()
            nc.vector.tensor_scalar(mask[:], rank[:], 2.0, None, ALU.is_lt).then_inc(mask_ready, 1)
            dve.wait_ge(mask_ready, 1)
            dve.wait_ge(lexp_done, NB)
            done(nc.vector.tensor_tensor(pe8[:], pe8[:], mask[:], ALU.mult))
            settle()
            done(nc.vector.tensor_reduce(psum8[:], pe8[:], AX, ALU.add))
            settle()
            done(nc.vector.reciprocal(psum8[:], psum8[:]))
            settle()
            done(nc.vector.tensor_tensor(comb[:], pe8[:], psum8[:].unsqueeze(2).broadcast_to([P, NB, NE]), ALU.mult))
            dve.wait_ge(counted, 1)
            cnt = A[1][:, :NB * NE].rearrange("p (b e) -> p b e", b=NB)
            done(nc.vector.scalar_tensor_tensor(pos[:], cnt, 1.0, mask[:], ALU.add, ALU.mult))
            done(nc.vector.tensor_reduce(most[:], A[1][:, NB * NE:NB * NE + NE], AX, ALU.max))
            settle()
            done(nc.vector.tensor_scalar(pos[:], pos[:], -1.0, None, ALU.add))
            nc.vector.tensor_scalar(flag[:], most[:], float(P), None, ALU.is_gt).then_inc(routed, 1)
            settle()

            def select(turn, n, e, col):
                nc.vector.tensor_copy(posc[:], pos[:, :, bass.ds(col, 1)].rearrange("p b a -> p (b a)")
                                      ).then_inc(selected, 1)
                nc.vector.tensor_copy(combc[:], comb[:, :, bass.ds(col, 1)].rearrange("p b a -> p (b a)")
                                      ).then_inc(selected, 1)
                dve.wait_ge(selected, 2 * n + 2 + e * 2)
                rank_of = cst[:, K_IOTA + turn * P:K_IOTA + (turn + 1) * P]
                for b in range(NB):
                    nc.vector.tensor_scalar(pick[:, b], rank_of, posc[:, b:b + 1], None, ALU.is_equal
                                            ).then_inc(picked, 1)
                    nc.vector.tensor_scalar(cw[:, b], rank_of, posc[:, b:b + 1], combc[:, b:b + 1], ALU.is_equal,
                                            ALU.mult).then_inc(picked, 1)

            def tokens_low(i, n, e):
                dve.wait_ge(he_hi, 8 * n + 4 * i + 4 + e * 8)
                for kk in range(4):
                    k = 4 * i + kk
                    c = G_LAYER + G_FFN + k
                    nc.vector.scalar_tensor_tensor(
                        heTl[:, k, :], T[i][:, kk * P:(kk + 1) * P], gcol[:, c:c + 1],
                        heTh[:, k, :].bitcast(F32), ALU.mult, ALU.subtract).then_inc(he_lo, 1)

            def add_spread(b, full, value, added):
                for h in range(2):
                    dve.wait_ge(full, value + h)
                    c = xs[:, b, h * N:(h + 1) * N]
                    nc.vector.tensor_tensor(c, DN[h][:], c, ALU.add).then_inc(added, 1)

            def expert(base, n, e, following):
                ahead = Lead(dve, split_lo, base, base + EU + (S if following else 0), e)
                ahead.next += S
                for j in range(EG + 1):
                    u = base + group_at(j)
                    ahead.to(u + (4 if j < EG else 2))
                    if j == 0:
                        add_spread(0, oe_full, 4 * n + 1 + e * 4, x_added[1])
                    if j:
                        dve.wait_ge(ff_hi[1], EG * n + j + e * EG)
                        nc.vector.tensor_tensor(aTl[:, (j - 1) % 2], T[(j - 1) % 2][:].rearrange("p (k t) -> p k t", k=4),
                                                aTh[:, (j - 1) % 2].bitcast(F32), ALU.subtract).then_inc(ff_lo[1], 1)
                    if following and j == EG - 2:
                        select(0, n + 1, e, e + 1)
                    if j < EG:
                        ahead.to(u + 6)
                        dve.wait_ge(unit_used, u + 4 + e * EU)
                        dve.wait_ge(silu_done[1], EG * n + j + 1 + e * EG)
                        nc.vector.tensor_tensor(av[:, j % 2], A[2 + j % 2][:], sg[:, j % 2], ALU.mult
                                                ).then_inc(ff_ready[1], 1)
                    if j == 0:
                        add_spread(1, oe_full, 4 * n + 3 + e * 4, x_added[1])
                    if following and j >= EG - 1:
                        tokens_low(j - EG + 1, n + 1, e)
                ahead.to(base + EU + S)
                dve.wait_ge(unit_used, base + EU + e * EU)
                nc.vector.tensor_copy(oe[:, N:], DN[1][:]).then_inc(oe_dve, 1)

            def head(turn, base, n, e):
                select(turn, n, e, e)
                Lead(dve, split_lo, base, base + S, e).to(base + S)
                for i in range(2):
                    tokens_low(i, n, e)

            nc.vector.memset(oe[:], 0.0).then_inc(oe_act, 1)
            nc.vector.memset(cwT[:], 0.0).then_inc(oe_dve, 1)
            head(0, UM, 0, 0)
            with dve.Fori(0, NE - 1) as e:
                expert(UM, 0, e, True)
            expert(UM + (NE - 1) * EU, NE - 1, 0, False)
            more = dve.value_load(flag[0:1, 0:1], min_val=0, max_val=1)
            with dve.If(more > 0):
                with dve.Fori(0, NE) as e:
                    head(1, UM + NE * EU, NE, e)
                    expert(UM + NE * EU, NE, e, False)
            for b in range(NB):
                add_spread(b, last_full, 2 * b + 1, last_added)
            dve.wait_ge(last_added, 2 * NB)
            nc.vector.tensor_copy(st[:, 14:15], eps[:]).then_inc(scattered, 1)
            dve.wait_ge(norm_root[4], 1)
            nc.vector.reciprocal(st[:, 12:14], st[:, 2:4]).then_inc(norm_inv[4], 1)
            dve.wait_ge(norm_inv[4], 1)
            dve.wait_ge(gfin_landed, 16)
            for b in range(NB):
                nc.vector.scalar_tensor_tensor(gout[:, b, :], xs[:, b, :], st[:, 12 + b:13 + b], gfin[:],
                                               ALU.mult, ALU.mult).then_inc(rows_ready, 1)

        @block.tensor
        def _(pe):
            def turn_x(n, x_there, halves):
                for i in range(4):
                    if i % 2 == 0:
                        pe.wait_ge(x_there, halves[i // 2])
                    for kk in range(2):
                        for b in range(NB):
                            k = 2 * i + kk
                            last = nc.tensor.transpose(TB[i][:, (kk * NB + b) * P:(kk * NB + b + 1) * P],
                                                       xs[:, b, k * P:(k + 1) * P], ident)
                    last.then_inc(norm_T[n], 1)

            def block_of(u, b, kt0, kt, total, n, hi, lo, bank):
                if b == 0:
                    pe.wait_ge(lo_done, u + 1)
                for kk in range(kt):
                    k = kt0 + kk
                    wh, wl = split_tile(u, kk, n)
                    last = product(bank[:, :n], hi[:, k, b * P:(b + 1) * P], lo[:, k, b * P:(b + 1) * P],
                                   wh, wl, k == 0, k == total - 1)
                if b == NB - 1:
                    last.then_inc(unit_used, 1)

            def columns(u, kt0, kt, total, n, hi, lo, banks):
                for b in range(NB):
                    block_of(u, b, kt0, kt, total, n, hi, lo, banks[b])

            pe.wait_ge(const_landed, 16)
            pe.wait_ge(gain_landed, 16 * 8)
            nc.tensor.transpose(T[0][:, 0:DEPTH * G_LAYER], grow[0:DEPTH * G_LAYER, :],
                                ident[0:DEPTH * G_LAYER, 0:DEPTH * G_LAYER]).then_inc(gain_T, 1)
            for l in range(DEPTH):
                if l == 0:
                    pe.wait_ge(gain_done, 1)
                    turn_x(0, x_landed, (16, 16))
                else:
                    turn_x(1, x_added[0], (X_DENSE - 2, X_DENSE))
                for g, (c0, n) in enumerate(PROJ):
                    u = at[l, "in"] + 2 * g
                    if g == 2:
                        pe.wait_ge(proj_act[l], 1)
                        pe.wait_ge(proj_dve[l], 1)
                    for h in range(2):
                        pe.wait_ge(norm_lo[l], 4 * (h + 1))
                        columns(u + h, 4 * h, 4, KD, n, hTh, hTl, A[2 * (g % 2):])
                pe.wait_ge(proj_act[l], 2)
                pe.wait_ge(proj_dve[l], 2)
                for i in range(3):
                    for kk in range(2 if i < 2 else 1):
                        k = 2 * i + kk
                        for b in range(NB):
                            last = nc.tensor.transpose(TB[i][:, (kk * NB + b) * P:(kk * NB + b + 1) * P],
                                                       pj[:, b, k * P:(k + 1) * P], ident)
                    last.then_inc(lat_T[l], 1)
                for h in range(2):
                    columns(at[l, "gate0"] + h, 4 * h, 4, KD, N, hTh, hTl, A[2:])
                pe.wait_ge(lat_lo[l], KQ + KKV)
                pe.wait_ge(proj_act[l], 3)
                pe.wait_ge(proj_dve[l], 3)
                pe.wait_ge(kdup_done[l], 2)
                for i in range(3):
                    for s in range(2):
                        for b in range(NB):
                            c = C_QS + (2 * i + s) * P
                            src = pj[:, b, c:c + P] if i < 2 else kdup[:, b, s].rearrange("p r d -> p (r d)")
                            last = nc.tensor.transpose([T[0], T[1], DN[1]][i][:, (s * NB + b) * P:(s * NB + b + 1) * P],
                                                       src, ident)
                    last.then_inc(win_T[l], 1)
                for i in range(2):
                    if i:
                        pe.wait_ge(win_act[l], 2)
                    columns(at[l, "q"] + i, 0, KQ, KQ, 4 * QK, latTh, latTl, [A, DN][i])
                u = at[l, "kv"]
                pe.wait_ge(lo_done, u + 1)
                pe.wait_ge(up_act[l], 1)
                pe.wait_ge(up_dve[l], 1)
                pe.wait_ge(gate_added[l], 2)
                for b in range(NB):
                    for n in range(2):
                        for k in range(KKV):
                            wh, wl = split_tile(u, k, D, n * N, N)
                            last = product(A[2 * b + n][:], latTh[:, KQ + k, b * P:(b + 1) * P],
                                           latTl[:, KQ + k, b * P:(b + 1) * P], wh, wl, k == 0, k == KKV - 1)
                last.then_inc(unit_used, 1)
                for i in range(QT_FILLS):
                    bank = T[i % 2]
                    if i == 0:
                        pe.wait_ge(rope_done[l], 4)
                        pe.wait_ge(win_act[l], 1)
                        pe.wait_ge(win_dve[l], 1)
                    if i == 4:
                        pe.wait_ge(up_act[l], 6)
                        pe.wait_ge(up_dve[l], 6)
                    if i >= 2:
                        pe.wait_ge([qk_act, qk_dve][i % 2][l], i // 2)
                    for s in range(2):
                        for b in range(NB):
                            o = (s * NB + b) * P
                            src = (qn if i < 4 else kn)[:, b, 2 * (i % 4) + s, :]
                            last = nc.tensor.transpose(bank[0:QK, o:o + P], src, ident)
                    last.then_inc(qk_T[l], 1)

                def scores(f):
                    kind, b, heads = FILLS[f]
                    w = P * (b + 1)
                    if f >= 2:
                        if FILLS[f - 2][0] == 0:
                            pe.wait_ge(exp_done[l], EXPS[f - 2])
                        else:
                            pe.wait_ge(masked[l], f - 1 - MLA_FILLS)
                    for i, h in enumerate(heads):
                        o = A[f % 2][:, i * w:(i + 1) * w]
                        q = slice(b * P, (b + 1) * P)
                        if kind == 0:
                            last = nc.tensor.matmul(o, qT[0:AUG, h, q], kT[0:AUG, h, 0:w], start=True, stop=True)
                        else:
                            r = slice(SW_D * (h % 2), SW_D * (h % 2) + SW_D)
                            last = nc.tensor.matmul(o, sqT[r, h // 2, q], skT[r, h // 4, 0:w], start=True, stop=True)
                    last.then_inc(scored[l], 1)

                def turn_probs(f):
                    kind, b, heads = FILLS[f]
                    pe.wait_ge(probs_ready[l], f + 1)
                    if f >= 2:
                        pe.wait_ge(probs_T_out[l], f - 1)
                    for i in range(4):
                        last = nc.tensor.transpose(T[f % 2][:, i * P:(i + 1) * P], sx[:, f % 2, i * P:(i + 1) * P],
                                                   ident)
                    last.then_inc(probs_T[l], 1)

                def values(f):
                    kind, b, heads = FILLS[f]
                    pe.wait_ge(probs_T_out[l], f + 1)
                    if kind and heads[0] == 0:
                        pe.wait_ge(o_lo[l], b + 1)
                    for i, h in enumerate(heads):
                        r = slice(VD * (h % 2), VD * (h % 2) + VD)
                        o = DN[b][r, (h // 2) * P:(h // 2 + 1) * P]
                        for kb in range(b + 1):
                            v = pj[:, kb, h * VD:(h + 1) * VD] if kind == 0 else \
                                pj[:, kb, C_VS + SW_D * (h // 4):C_VS + SW_D * (h // 4) + SW_D]
                            c = (i * (b + 1) + kb) * P
                            last = nc.tensor.matmul(o, v, pT[:, f % 2, c:c + P], start=kb == 0, stop=kb == b)
                    last.then_inc(pv_done[l], 1)

                pe.wait_ge(qk_act[l], QT_FILLS - QT_FILLS // 2)
                pe.wait_ge(qk_dve[l], QT_FILLS // 2)

                def half_unit(i):
                    u, b = at[l, "gate"] + i // 2, i % 2
                    if u < at[l, "br"]:
                        if i % 4 == 0:
                            pe.wait_ge(gate_added[l], 2 + i // 2)
                        if i == 0:
                            pe.wait_ge(up_dve[l], 6)
                        block_of(u, b, 4 * (u - at[l, "gate"]) % KD, 4, KD, N, hTh, hTl, A[2 + b])
                    else:
                        if b == 0:
                            pe.wait_ge(masked[l], NF - MLA_FILLS)
                            pe.wait_ge(o_lo[l], 2)
                        block_of(u, b, 0, 4, 4, N, oTh[:, 0], oTl[:, 0], BR[0][0][b])

                if l == 0:
                    pe.wait_ge(rows_landed, 32)
                scores(0)
                scores(1)
                half_unit(0)
                half_unit(1)
                for f in range(NF):
                    turn_probs(f)
                    if f + 2 < NF:
                        scores(f + 2)
                    half_unit(f + 2)
                    if f:
                        values(f - 1)
                values(NF - 1)
                def branch(kind, n):
                    columns(at[l, "br"] + 2 * kind + n, 0, 4, 4, N, oTh[:, kind], oTl[:, kind], BR[kind][n])

                def turn_merged(half):
                    pe.wait_ge(merged[l], NB * (1 + half))
                    for i in range(2 * half, 2 * half + 2):
                        for kk in range(2):
                            for b in range(NB):
                                k = 2 * i + kk
                                last = nc.tensor.transpose(MB[i][:, (kk * NB + b) * P:(kk * NB + b + 1) * P],
                                                           mg[:, b, k * P:(k + 1) * P], ident)
                        last.then_inc(mg_T[l], 1)

                def projected(n, half):
                    pe.wait_ge(mg_lo[l], 2 * half + 2)
                    columns(at[l, "out"] + 2 * half + n, 4 * half, 4, KD, N, hTh, hTl, OUT[n])

                pe.wait_ge(gate_added[l], 8)
                branch(0, 1)
                pe.wait_ge(o_lo[l], 4)
                branch(1, 0)
                branch(1, 1)
                turn_merged(0)
                projected(0, 0)
                turn_merged(1)
                projected(1, 0)
                projected(0, 1)
                projected(1, 1)
                turn_x(2 + l, x_added[l], (2, 4))
                pe.wait_ge(norm_lo[2 + l], 4)
                if l == 0:
                    u0 = at[0, "ffn"]
                    pe.wait_ge(x_added[0], 4)
                    for j in range(DG + 1):
                        n = min(N, FF - j * N)
                        u = u0 + group_at(j)
                        if j < DG:
                            if j:
                                pe.wait_ge(silu_done[0], NB * j)
                            for h in range(2):
                                pe.wait_ge(norm_lo[2], 4 * (h + 1))
                                columns(u + h, 4 * h, 4, KD, n, hTh, hTl, A)
                        if j:
                            m = min(N, FF - (j - 1) * N)
                            if j > 1:
                                pe.wait_ge(x_added[0], 4 + 4 * (j - 1))
                            for b in range(NB):
                                pe.wait_ge(ff_ready[0], NB * (j - 1) + b + 1)
                                for k in range(m // P):
                                    last = nc.tensor.transpose(T[b][:, k * P:(k + 1) * P], av[:, b, k * P:(k + 1) * P],
                                                               ident)
                                last.then_inc(ff_T[0], 1)
                        if j < DG:
                            if j:
                                pe.wait_ge(ff_ready[0], NB * j)
                            for h in range(2):
                                columns(u + 2 + h, 4 * h, 4, KD, n, hTh, hTl, A[2:])
                        if j:
                            pe.wait_ge(ff_lo[0], NB * j)
                            ud = u0 + down_at(j - 1, DG)
                            kt = m // P
                            pe.wait_ge(lo_done, ud + kt // 2)
                            for i, (b, h, bank) in enumerate(down_order(j)):
                                for k in range(kt):
                                    wh, wl = split_tile(ud + k // 2, k % 2, D, h * N, N)
                                    last = product(bank[:], aTh[:, b, k, :], aTl[:, b, k, :], wh, wl,
                                                   k == 0, k == kt - 1)
                                    if i == 3 and k % 2 == 1:
                                        last.then_inc(unit_used, 1)
                                    elif k == kt - 1:
                                        last.then_inc(down_done, 1)

            pe.wait_ge(norm_lo[3], KD)
            pe.wait_ge(wr_lo, 1)
            for b in range(NB):
                for k in range(KD):
                    last = product(A[0][:, b * NE:(b + 1) * NE], hTh[:, k, b * P:(b + 1) * P],
                                   hTl[:, k, b * P:(b + 1) * P], wrh[:, k, :], wrl[:, k, :], k == 0, k == KD - 1)
            last.then_inc(logits_done, 1)
            pe.wait_ge(mask_ready, 1)
            nc.tensor.matmul(A[1][:, 0:NE], before, mask[:, 0, :], start=True, stop=True)
            nc.tensor.matmul(A[1][:, NE:2 * NE], ones[:], mask[:, 0, :], start=True, stop=False)
            nc.tensor.matmul(A[1][:, NE:2 * NE], before, mask[:, 1, :], start=False, stop=True)
            nc.tensor.matmul(A[1][:, 2 * NE:3 * NE], ones[:], mask[:, 0, :], start=True, stop=False)
            nc.tensor.matmul(A[1][:, 2 * NE:3 * NE], ones[:], mask[:, 1, :], start=False, stop=True
                             ).then_inc(counted, 1)
            pe.wait_ge(routed, 1)

            def gather(i, n, e):
                pe.wait_ge(picked, 4 * n + 4 + e * 4)
                for kk in range(4):
                    k = 4 * i + kk
                    for b in range(NB):
                        last = nc.tensor.matmul(T[i][:, kk * P:(kk + 1) * P], xn[:, b, k * P:(k + 1) * P],
                                                pick[:, b], start=b == 0, stop=b == NB - 1)
                last.then_inc(gathered, 1)

            def spread(b, full):
                for h in range(2):
                    nc.tensor.matmul(DN[h][:], cwT[:, b * P:(b + 1) * P], oe[:, h * N:(h + 1) * N],
                                     start=True, stop=True).then_inc(full, 1)

            def expert(base, n, e, following):
                def products(u, h, bank):
                    pe.wait_ge(lo_done, u + 1 + e * EU)
                    for kk in range(4):
                        k = 4 * h + kk
                        wh, wl = split_tile(u, kk, N)
                        last = product(bank[:], heTh[:, k, :], heTl[:, k, :], wh, wl, k == 0, k == KD - 1)
                    last.then_inc(unit_used, 1)

                pe.wait_ge(he_lo, 8 * n + 8 + e * 8)
                for j in range(EG + 1):
                    u = base + group_at(j)
                    if j < EG:
                        if j >= 2:
                            pe.wait_ge(silu_done[1], EG * n + j - 1 + e * EG)
                        for h in range(2):
                            products(u + h, h, A[j % 2])
                    if j == 0:
                        pe.wait_ge(oe_act, n + 1 + e)
                        pe.wait_ge(oe_dve, n + 1 + e)
                        spread(0, oe_full)
                    else:
                        q = (j - 1) % 2
                        pe.wait_ge(ff_ready[1], EG * n + j + e * EG)
                        if j == 2:
                            pe.wait_ge(cw_out, n + 1 + e)
                        if j > 2:
                            pe.wait_ge(ff_lo[1], EG * n + j - 2 + e * EG)
                        if following and j == EG:
                            pe.wait_ge(he_lo, 8 * n + 12 + e * 8)
                        for k in range(4):
                            last = nc.tensor.transpose(T[q][:, k * P:(k + 1) * P], av[:, q, k * P:(k + 1) * P], ident)
                        last.then_inc(ff_T[1], 1)
                    if j == 1:
                        for b in range(NB):
                            last = nc.tensor.transpose(T[1][:, b * P:(b + 1) * P], cw[:, b], ident)
                        last.then_inc(cw_T, 1)
                    if following and j == EG:
                        gather(1, n + 1, e)
                    if j < EG:
                        if j >= 2:
                            pe.wait_ge(ff_ready[1], EG * n + j - 1 + e * EG)
                        for h in range(2):
                            products(u + 2 + h, h, A[2 + j % 2])
                    if j == 0:
                        pe.wait_ge(x_added[1], 4 + 4 * n + 2 + e * 4)
                        spread(1, oe_full)
                    if following and j == EG - 1:
                        pe.wait_ge(ff_lo[1], EG * n + EG - 2 + e * EG)
                        gather(0, n + 1, e)
                    if j:
                        if j == 1:
                            pe.wait_ge(x_added[1], 4 + 4 * n + 4 + e * 4)
                        pe.wait_ge(ff_lo[1], EG * n + j + e * EG)
                        ud = base + down_at(j - 1, EG)
                        for i in range(2):
                            pe.wait_ge(lo_done, ud + i + 1 + e * EU)
                            for kk in range(2):
                                k = 2 * i + kk
                                for h in range(2):
                                    wh, wl = split_tile(ud + i, kk, D, h * N, N)
                                    last = product(DN[h][:], aTh[:, q, k, :], aTl[:, q, k, :], wh, wl,
                                                   j == 1 and k == 0, j == EG and k == 3)
                            last.then_inc(unit_used, 1)

            def head(n, e):
                for i in range(2):
                    gather(i, n, e)

            def output_out(n, e):
                pe.wait_ge(oe_act, n + 1 + e)
                pe.wait_ge(oe_dve, n + 1 + e)

            pe.wait_ge(oe_act, 1)
            pe.wait_ge(oe_dve, 1)
            head(0, 0)
            with pe.Fori(0, NE - 1) as e:
                expert(UM, 0, e, True)
            expert(UM + (NE - 1) * EU, NE - 1, 0, False)
            output_out(NE, 0)
            more = pe.value_load(flag[0:1, 0:1], min_val=0, max_val=1)
            with pe.If(more > 0):
                with pe.Fori(0, NE) as e:
                    head(NE, e)
                    expert(UM + NE * EU, NE, e, False)
                    output_out(NE + 1, e)
            for b in range(NB):
                if b:
                    pe.wait_ge(last_added, 2)
                spread(b, last_full)

        @block.gpsimd
        def _(pool):
            pool.wait_ge(o_lo[1], 4)
            pool.dma_start(wr[:], w_router[0].rearrange("(k p) e -> p k e", p=P)).then_inc(router_landed, 16)
            pool.dma_start(gfin[:], g_final.rearrange("(a d) -> a d", a=1).broadcast_to([P, D])
                           ).then_inc(gfin_landed, 16)
            pool.wait_ge(gfin_landed, 16)


_INS = ["x", "g_attn_norm", "w_in", "b_gate", "g_q_norm", "w_q_up", "g_kv_norm", "w_kv_up", "sinks", "w_br_mla",
        "w_br_swa", "w_out", "g_ffn_norm", "dense_w_gate", "dense_w_up", "dense_w_down", "w_router",
        "moe_w_gate", "moe_w_up", "moe_w_down", "g_final"]


def shape_constants():
    import numpy as np

    c = np.zeros((P, K_ALL), np.float32)
    inv = 1.0 / (10000.0 ** (np.arange(0, ROPE, 2, dtype=np.float32) / ROPE))
    ang = np.arange(SEQ, dtype=np.float32)[:, None] * inv[None, :]
    for b in range(NB):
        c[:, K_COS + b * HALF:K_COS + (b + 1) * HALF] = np.cos(ang[b * P:(b + 1) * P])
        c[:, K_SIN + b * HALF:K_SIN + (b + 1) * HALF] = np.sin(ang[b * P:(b + 1) * P])
    q, k = np.arange(P, SEQ)[:, None], np.arange(SEQ)[None, :]
    ahead = k // CHUNK > q // CHUNK
    outside = ahead | (k // CHUNK < q // CHUNK - 1)
    c[:, K_DIST:K_IDENT] = np.where(outside, 1e33, np.abs(q - k))
    c[:, K_IDENT:K_BEFORE] = np.eye(P)
    c[:, K_BEFORE:K_IOTA] = np.triu(np.ones((P, P)), 1)
    c[:, K_IOTA:K_LOWER] = np.arange(SEQ)[None, :]
    c[:, K_LOWER:K_ALL] = np.tril(np.ones((NE, NE)), -1).reshape(1, -1)
    return c


def shape_mask_rows():
    import numpy as np

    chunk = np.arange(SEQ) // CHUNK
    r = np.zeros((NB, 2, SEQ), np.float32)
    for b in range(NB):
        r[b, 0] = chunk == 2 * b
        r[b, 1] = np.where(chunk == 2 * b + 1, -1e30, 0.0)
    return r


def kernel(**inputs):
    import numpy as np
    import concourse.bacc as bacc
    from concourse.bass_utils import run_bass_kernel_spmd

    nc = bacc.Bacc("TRN2", target_bir_lowering=False, num_devices=1)
    arrays, args = {}, []
    for name in _INS:
        a = np.ascontiguousarray(inputs[name])
        arrays[f"in_{name}"] = a
        args.append(nc.dram_tensor(f"in_{name}", a.shape, F32, kind="ExternalInput").ap())
    arrays["shape_constants"] = shape_constants()
    args.append(nc.dram_tensor("shape_constants", (P, K_ALL), F32, kind="ExternalInput").ap())
    arrays["shape_mask_rows"] = shape_mask_rows()
    args.append(nc.dram_tensor("shape_mask_rows", (NB, 2, SEQ), F32, kind="ExternalInput").ap())
    args.append(nc.dram_tensor("out", (1, SEQ, D), F32, kind="ExternalOutput").ap())
    trunk(nc, *args)
    r = run_bass_kernel_spmd(nc, [arrays], core_ids=[0])
    return r.results[0]["out"]
```

```python
from contextlib import ExitStack

import concourse.bass as bass
from concourse import mybir

F32 = mybir.dt.float32
F32R = mybir.dt.float32r
I32 = mybir.dt.int32
ALU = mybir.AluOpType
ACT = mybir.ActivationFunctionType
AX = mybir.AxisListType.X

P = 128
D = 1024
SEQ = 256
NB = SEQ // P
KD = D // P
DEPTH = 2
CHUNK = 64
HEADS = 8
NOPE, ROPE, VD = 64, 32, 64
QK = NOPE + ROPE
HALF = ROPE // 2
Q_LORA, KV_LORA = 384, 256
KQ, KKV = Q_LORA // P, KV_LORA // P
SW_KV, SW_D = 2, 64
FF = 2816
NE = 8
EFF = 3584
EPS = 1e-6
MLA_SCALE = float(QK) ** -0.5
SWA_SCALE = float(SW_D) ** -0.5
SLOPES = [2.0 ** (-8.0 * (h + 1.0) / HEADS) for h in range(HEADS)]

C_KV = Q_LORA
C_KR = C_KV + KV_LORA
C_QS = C_KR + ROPE
C_KS = C_QS + HEADS * SW_D
C_VS = C_KS + SW_KV * SW_D
C_GATE = C_VS + SW_KV * SW_D
PROJ = [(0, 512), (512, 512), (1024, C_GATE - 1024)]

UNIT = 2048
R = 6
S = 3
N = 512

def group_at(j):
    return 0 if j == 0 else 4 + 6 * (j - 1)


def down_at(j, groups):
    return 8 + 6 * j if j < groups - 1 else 4 + 6 * (groups - 1)


EG = EFF // N
EU = 6 * EG
DG = -(-FF // N)
assert EU % R == 0 and EU % S == 0

K_COS = 0
K_SIN = K_COS + NB * HALF
K_DIST = K_SIN + NB * HALF
K_IDENT = K_DIST + SEQ
K_BEFORE = K_IDENT + P
K_IOTA = K_BEFORE + P
K_LOWER = K_IOTA + SEQ
K_ALL = K_LOWER + NE * NE

G_LAYER = KD + KQ + KKV + KD
G_ATTN, G_Q, G_KV, G_FFN = 0, KD, KD + KQ, KD + KQ + KKV

FILLS = []
for kind in range(2):
    for b in range(NB):
        per = 4 // (b + 1)
        order = list(range(HEADS)) if kind == 0 else list(range(0, HEADS, 2)) + list(range(1, HEADS, 2))
        FILLS += [(kind, b, order[h:h + per]) for h in range(0, HEADS, per)]
NF = len(FILLS)
LAST = [max(f for f, x in enumerate(FILLS) if x[:2] == (kind, b)) for kind in range(2) for b in range(NB)]
MLA_FILLS = sum(x[0] == 0 for x in FILLS)
EXPS = [sum(len(x[2]) for x in FILLS[:f + 1]) for f in range(NF)]
AUG = QK + NB
QT_FILLS = 8


def trunk(nc, x, g_attn_norm, w_in, b_gate, g_q_norm, w_q_up, g_kv_norm, w_kv_up, sinks, w_br_mla,
          w_br_swa, w_out, g_ffn_norm, dense_w_gate, dense_w_up, dense_w_down, w_router, moe_w_gate,
          moe_w_up, moe_w_down, g_final, consts, mask_rows, out):
    units = []
    at = {}

    def rows(w, k0, kt, c0, n):
        units.append((w[k0 * P:(k0 + kt) * P, c0:c0 + n].rearrange("(k p) n -> p k n", p=P), kt, n))

    for l in range(DEPTH):
        at[l, "in"] = len(units)
        for c0, n in PROJ:
            rows(w_in[l], 0, 4, c0, n)
            rows(w_in[l], 4, 4, c0, n)
        at[l, "gate0"] = len(units)
        rows(w_in[l], 0, 4, C_GATE, N)
        rows(w_in[l], 4, 4, C_GATE, N)
        at[l, "q"] = len(units)
        for i in range(2):
            rows(w_q_up[l], 0, KQ, i * 4 * QK, 4 * QK)
        at[l, "kv"] = len(units)
        rows(w_kv_up[l], 0, KKV, 0, D)
        at[l, "gate"] = len(units)
        for g in range(1, 4):
            rows(w_in[l], 0, 4, C_GATE + g * N, N)
            rows(w_in[l], 4, 4, C_GATE + g * N, N)
        at[l, "br"] = len(units)
        for w in (w_br_mla, w_br_swa):
            for n in range(2):
                rows(w[l], 0, 4, n * N, N)
        at[l, "out"] = len(units)
        for h in range(2):
            for n in range(2):
                rows(w_out[l], 4 * h, 4, n * N, N)
        at[l, "ffn"] = len(units)
        if l == 0:
            def down(j):
                for k in range(4 * j, min(4 * j + 4, FF // P), 2):
                    rows(dense_w_down[0], k, 2, 0, D)

            for j in range(DG):
                n = min(N, FF - j * N)
                for w in (dense_w_gate, dense_w_up):
                    rows(w[0], 0, 4, j * N, n)
                    rows(w[0], 4, 4, j * N, n)
                if j:
                    down(j - 1)
            down(DG - 1)
    UM = len(units)
    assert UM == at[1, "ffn"]

    with ExitStack() as ctx:
        used = [(nc.sbuf_base + 31) // 32 * 32]

        def place(name, shape, dt, offset=None):
            size = 4
            for s in shape[1:]:
                size *= s
            if offset is None:
                offset = used[0]
                used[0] += (size + 31) // 32 * 32
            assert offset + size <= nc.sbuf_usable_end, (name, offset + size)
            return nc.alloc_sbuf_tensor_at(name, shape, dt, offset=offset)

        def sem(name):
            return ctx.enter_context(nc.semaphore(name))

        raw = place("raw", [P, R, UNIT], F32)
        whi = place("whi", [P, S, UNIT], F32R)
        wlo = place("wlo", [P, S, UNIT], F32R)
        xs = place("xs", [P, NB, D], F32)
        o_xn = used[0]
        xn = place("xn", [P, NB, D], F32)
        sqT = place("sqT", [P, 4, SEQ], F32, o_xn)
        skT = place("skT", [P, SW_KV, SEQ], F32, o_xn + 4096)
        kdup = place("kdup", [P, NB, SW_KV, 2, SW_D], F32, o_xn + 6144)
        hTh = place("hTh", [P, KD, SEQ], F32R)
        hTl = place("hTl", [P, KD, SEQ], F32R)
        o_o = used[0]
        oTh = place("oTh", [P, 2, 4, SEQ], F32R)
        oTl = place("oTl", [P, 2, 4, SEQ], F32R)
        latTh = place("latTh", [P, KQ + KKV, SEQ], F32R, o_o)
        latTl = place("latTl", [P, KQ + KKV, SEQ], F32R, o_o + 8192)
        sg = place("sg", [P, 2, N], F32, o_o)
        av = place("av", [P, 2, N], F32, o_o + 4096)
        aTh = place("aTh", [P, 2, 4, P], F32R, o_o + 8192)
        aTl = place("aTl", [P, 2, 4, P], F32R, o_o + 12288)
        o_pj = used[0]
        pj = place("pj", [P, NB, C_GATE], F32)
        mg = place("mg", [P, NB, D], F32, o_pj)
        o_g = used[0]
        gates = place("gates", [P, 4, NB, N], F32)
        qn = place("qn", [P, NB, HEADS, QK], F32, o_g + 4096)
        kn = place("kn", [P, NB, HEADS, QK], F32, o_g + 4096 + 6144)
        heTh = place("heTh", [P, KD, P], F32R, o_g)
        heTl = place("heTl", [P, KD, P], F32R, o_g + 4096)
        oe = place("oe", [P, D], F32, o_g + 8192)
        pick = place("pick", [P, NB, P], F32, o_g + 12288)
        cw = place("cw", [P, NB, P], F32, o_g + 13312)
        cwT = place("cwT", [P, SEQ], F32, o_g + 14336)
        gout = place("gout", [P, NB, D], F32, o_g)
        qT = place("qT", [P, HEADS, SEQ], F32)
        o_kT = used[0]
        kT = place("kT", [P, HEADS, SEQ], F32)
        gfin = place("gfin", [P, D], F32, o_kT)
        bg = place("bg", [P, 2, N], F32)
        o_sx = used[0]
        sx = place("sx", [P, 2, N], F32)
        rt = place("rt", [P, 4, NB * HEADS * HALF], F32, o_sx)
        pT = place("pT", [P, 2, N], F32)
        cst = place("cst", [P, K_ALL], F32)
        gcol = place("gcol", [P, DEPTH * G_LAYER], F32)
        sk = place("sk", [P, DEPTH, HEADS], F32)
        sk_neg = place("sk_neg", [P, DEPTH, HEADS], F32)
        ones = place("ones", [P, P], F32)
        krt = place("krt", [P, 4, NB * HALF], F32)
        st = place("st", [P, 16], F32)
        eps = place("eps", [P, 1], F32)
        nm = place("nm", [P, 2, 4], F32)
        sink_d = place("sink_d", [P, NB, HEADS], F32)
        sink_e = place("sink_e", [P, NB, HEADS], F32)
        sums = place("sums", [P, 2, NB, HEADS], F32)
        rsum = place("rsum", [P, HEADS], F32)
        on = place("on", [P, N], F32)
        wr = place("wr", [P, KD, NE], F32)
        wrh = place("wrh", [P, KD, NE], F32R)
        wrl = place("wrl", [P, KD, NE], F32R)
        lgT = place("lgT", [P, SEQ], F32, o_kT + 4096)
        lg = place("lg", [P, NB, NE], F32, o_sx)
        above = place("above", [P, NB, NE, NE], F32, o_sx + 64)
        ties = place("ties", [P, NB, NE, NE], F32, o_sx + 576)
        rank = place("rank", [P, NB, NE], F32, o_sx + 1088)
        mask = place("mask", [P, NB, NE], F32, o_sx + 1152)
        lmax = place("lmax", [P, NB], F32, o_sx + 1216)
        pe8 = place("pe8", [P, NB, NE], F32, o_sx + 1248)
        psum8 = place("psum8", [P, NB], F32, o_sx + 1312)
        comb = place("comb", [P, NB, NE], F32, o_sx + 1344)
        pos = place("pos", [P, NB, NE], F32, o_sx + 1408)
        most = place("most", [P, 1], F32, o_sx + 1472)
        flag = place("flag", [P, 1], I32, o_sx + 1504)
        posc = place("posc", [P, NB], F32, o_sx + 1536)
        combc = place("combc", [P, NB], F32, o_sx + 1568)
        grow = place("grow", [P, P], F32, o_sx + 2048)

        A = [ctx.enter_context(nc.psum_tensor(f"A{i}", [P, N], F32)) for i in range(4)]
        T = [ctx.enter_context(nc.psum_tensor(f"T{i}", [P, N], F32)) for i in range(2)]
        DN = [ctx.enter_context(nc.psum_tensor(f"DN{i}", [P, N], F32)) for i in range(2)]

        TB = T + DN
        ident = cst[:, K_IDENT:K_IDENT + P]
        before = cst[:, K_BEFORE:K_BEFORE + P]

        raw_landed = [sem(f"raw_landed{i}") for i in range(R)]
        hi_done = sem("hi_done")
        lo_done = sem("lo_done")
        unit_used = sem("unit_used")
        const_landed = sem("const_landed")
        gain_landed = sem("gain_landed")
        x_landed = sem("x_landed")
        sink_landed = sem("sink_landed")
        rows_landed = sem("rows_landed")
        sink_negated = sem("sink_negated")
        router_landed = sem("router_landed")
        gfin_landed = sem("gfin_landed")
        bg_landed = [sem(f"bg_landed{i}") for i in range(2)]
        out_landed = sem("out_landed")
        ones_set = sem("ones_set")
        gain_T = sem("gain_T")
        gain_done = sem("gain_done")
        act_own = sem("act_own")
        dve_own = sem("dve_own")

        def layered(name):
            return [sem(f"{name}{l}") for l in range(DEPTH)]

        norm_root = [sem(f"norm_root{n}") for n in range(5)]
        norm_inv = [sem(f"norm_inv{n}") for n in range(5)]
        rows_ready = sem("rows_ready")
        norm_T = [sem(f"norm_T{n}") for n in range(4)]
        norm_hi = [sem(f"norm_hi{n}") for n in range(4)]
        norm_lo = [sem(f"norm_lo{n}") for n in range(4)]
        proj_act, proj_dve = layered("proj_act"), layered("proj_dve")
        gate_added, gate_ready = layered("gate_added"), layered("gate_ready")
        lat_root, lat_inv = layered("lat_root"), layered("lat_inv")
        win_T, win_act, win_dve = layered("win_T"), layered("win_act"), layered("win_dve")
        lat_T, lat_hi, lat_lo = layered("lat_T"), layered("lat_hi"), layered("lat_lo")
        up_act, up_dve = layered("up_act"), layered("up_dve")
        rope_done, kdup_done = layered("rope_done"), layered("kdup_done")
        qk_T, qk_act, qk_dve = layered("qk_T"), layered("qk_act"), layered("qk_dve")
        scored, masked, max_ready = layered("scored"), layered("masked"), layered("max_ready")
        exp_done, sink_done = layered("exp_done"), layered("sink_done")
        o_scaled, o_T = layered("o_scaled"), layered("o_T")
        probs_T, probs_T_out = layered("probs_T"), layered("probs_T_out")
        pv_done, o_hi, o_lo = layered("pv_done"), layered("o_hi"), layered("o_lo")
        gated, merged = layered("gated"), layered("merged")
        mg_T, mg_hi, mg_lo = layered("mg_T"), layered("mg_hi"), layered("mg_lo")
        x_added = layered("x_added")
        silu_done, ff_ready = layered("silu_done"), layered("ff_ready")
        ff_T, ff_hi, ff_lo = layered("ff_T"), layered("ff_hi"), layered("ff_lo")
        down_done = sem("down_done")
        wr_hi, wr_lo = sem("wr_hi"), sem("wr_lo")
        logits_done, logits_out, logits_T = sem("logits_done"), sem("logits_out"), sem("logits_T")
        mask_ready, counted = sem("mask_ready"), sem("counted")
        lmax_ready, lexp_done = sem("lmax_ready"), sem("lexp_done")
        routed, selected = sem("routed"), sem("selected")
        picked, gathered = sem("picked"), sem("gathered")
        he_hi, he_lo = sem("he_hi"), sem("he_lo")
        cw_T, cw_out = sem("cw_T"), sem("cw_out")
        oe_full, oe_act, oe_dve = sem("oe_full"), sem("oe_act"), sem("oe_dve")
        last_full, last_added = sem("last_full"), sem("last_added")

        X_DENSE = 4 + 4 * DG

        def times(e, per):
            return 0 if e is None else e * per

        def load_gains(eng, l):
            for g, k, o in ((g_attn_norm, KD, G_ATTN), (g_q_norm, KQ, G_Q), (g_kv_norm, KKV, G_KV),
                            (g_ffn_norm, KD, G_FFN)):
                r = l * G_LAYER + o
                eng.dma_start(grow[r:r + k, :], g[l].rearrange("(k p) -> k p", p=P)).then_inc(gain_landed, 16)

        def split_hi(act, u, e=None):
            n = UNIT if u >= UM else units[u][1] * units[u][2]
            act.wait_ge(raw_landed[u % R], 16 * (u // R + 1) + times(e, 16 * EU // R))
            if u >= S:
                act.wait_ge(unit_used, u - S + 1 + times(e, EU))
            nc.scalar.activation(whi[:, u % S, :n], raw[:, u % R, :n], ACT.Copy).then_inc(hi_done, 1)

        def split_lo(dve, u, e=None):
            n = UNIT if u >= UM else units[u][1] * units[u][2]
            dve.wait_ge(hi_done, u + 1 + times(e, EU))
            nc.vector.tensor_tensor(wlo[:, u % S, :n], raw[:, u % R, :n],
                                    whi[:, u % S, :n].bitcast(F32), ALU.subtract).then_inc(lo_done, 1)

        class Lead:

            def __init__(self, eng, split, first, last, e=None):
                self.eng, self.split, self.next, self.last, self.e = eng, split, first, last, e

            def to(self, u):
                while self.next < min(u, self.last):
                    self.split(self.eng, self.next, self.e)
                    self.next += 1

        def split_tile(u, kk, n, c0=0, width=None):
            a = kk * n + c0
            b = a + (n if width is None else width)
            return whi[:, u % S, a:b], wlo[:, u % S, a:b]

        def product(o, hi, lo, wh, wl, start, stop):
            nc.tensor.matmul(o, hi, wh, start=start, stop=False)
            nc.tensor.matmul(o, hi, wl, start=False, stop=False)
            return nc.tensor.matmul(o, lo, wh, start=False, stop=stop)

        def vm(b, n):
            return pj[:, b, n * 4 * VD:(n + 1) * 4 * VD].rearrange("p (h d) -> p h d", h=4)

        def qk_target(i):
            if i < 4:
                return qT[0:QK, 2 * i:2 * i + 2, :].rearrange("p h t -> p (h t)"), QK, N, MLA_SCALE
            return kT[0:QK, 2 * i - 8:2 * i - 6, :].rearrange("p h t -> p (h t)"), QK, N, 1.0

        BR = [[A[:2], A[2:]], [DN, T]]
        MB = A[:2] + T
        KV = [A[:2], DN]
        QB = T + A[:2]
        OUT = [DN, A[2:]]

        def turned(j, b):
            return T[b] if j < DG else A[2 + b]

        def down_order(j):
            if j < DG:
                return [(b, h, [DN, T][b][h]) for b in range(NB) for h in range(2)]
            return [(b, h, A[2 * b + h]) for h in range(2) for b in range(NB)]

        block = ctx.enter_context(nc.Block())

        @block.sync
        def _(sp):
            sp.dma_start(xs[:], x[0].rearrange("(b p) d -> p b d", p=P)).then_inc(x_landed, 16)
            load_gains(sp, 0)
            sp.dma_start(cst[:], consts).then_inc(const_landed, 16)

            def load(u, dst_u, src, kt, n, e=None):
                if u >= R:
                    sp.wait_ge(lo_done, u - R + 1 + times(e, EU))
                sp.dma_start(raw[:, dst_u, :kt * n].rearrange("p (k n) -> p k n", k=kt), src
                             ).then_inc(raw_landed[dst_u], 16)

            for u, (src, kt, n) in enumerate(units):
                load(u, u % R, src, kt, n)

            def expert_loads(base, e):
                gate = moe_w_gate[0, bass.ds(e, 1)].rearrange("a (k p) n -> p (a k) n", p=P)
                up = moe_w_up[0, bass.ds(e, 1)].rearrange("a (k p) n -> p (a k) n", p=P)
                dn = moe_w_down[0, bass.ds(e, 1)].rearrange("a (k p) n -> p (a k) n", p=P)
                i = 0

                def take(src, kt, n):
                    nonlocal i
                    load(base + i, (base + i) % R, src, kt, n, e)
                    i += 1

                for j in range(EG + 1):
                    if j < EG:
                        for w in (gate, up):
                            take(w[:, 0:4, j * N:(j + 1) * N], 4, N)
                            take(w[:, 4:8, j * N:(j + 1) * N], 4, N)
                    if j:
                        take(dn[:, 4 * j - 4:4 * j - 2, :], 2, D)
                        take(dn[:, 4 * j - 2:4 * j, :], 2, D)

            with sp.Fori(0, NE) as e:
                expert_loads(UM, e)
            sp.wait_ge(routed, 1)
            more = sp.value_load(flag[0:1, 0:1], min_val=0, max_val=1)
            with sp.If(more > 0):
                with sp.Fori(0, NE) as e:
                    expert_loads(UM + NE * EU, e)
            for b in range(NB):
                sp.wait_ge(rows_ready, NB + b + 1)
                sp.dma_start(out[0, b * P:(b + 1) * P, :], gout[:, b, :]).then_inc(out_landed, 16)
            sp.wait_ge(out_landed, 16 * NB)

        @block.scalar
        def _(act):
            own = [0]

            def done(ins):
                own[0] += 1
                ins.then_inc(act_own, 1)
                return own[0]

            lead = Lead(act, split_hi, 0, UM)

            def bias_chunk(l, g):
                act.dma_start(bg[:, g % 2, :], b_gate[l:l + 1, g * N:(g + 1) * N].broadcast_to([P, N])
                              ).then_inc(bg_landed[g % 2], 16)

            def root(n):
                for b in range(NB):
                    v = done(nc.scalar.activation(xn[:, b, :], xs[:, b, :], ACT.Square, accum_out=st[:, b:b + 1]))
                act.wait_ge(act_own, v)
                nc.scalar.activation(st[:, 2:4], st[:, 0:2], ACT.Sqrt, scale=1.0 / D, bias=eps[:]
                                     ).then_inc(norm_root[n], 1)

            def norm_high(n, gains, fills=range(4)):
                for i in fills:
                    act.wait_ge(norm_T[n], i + 1)
                    for kk in range(2):
                        k = 2 * i + kk
                        nc.scalar.activation(hTh[:, k, :], TB[i][:, kk * SEQ:(kk + 1) * SEQ], ACT.Copy,
                                             scale=gcol[:, gains + k:gains + k + 1]).then_inc(norm_hi[n], 1)

            load_gains(act, 1)
            def split_head(base, e):
                Lead(act, split_hi, base, base + S, e).to(base + S)

            act.wait_ge(ones_set, 2)
            nc.scalar.activation(st[:, 14:15], eps[:], ACT.Square)
            act.wait_ge(x_landed, 16)
            for l in range(DEPTH):
                if l == 0:
                    act.wait_ge(gain_T, 1)
                    nc.scalar.activation(gcol[:], A[0][:, 0:DEPTH * G_LAYER], ACT.Copy).then_inc(gain_done, 1)
                    act.wait_ge(gain_done, 1)
                if l:
                    lead.to(at[l, "in"] + 2)
                    norm_high(1, G_LAYER + G_ATTN)
                else:
                    norm_high(0, G_ATTN, range(2))
                    lead.to(1)
                    norm_high(0, G_ATTN, range(2, 4))
                lead.to(at[l, "in"] + 2)
                bias_chunk(l, 0)
                bias_chunk(l, 1)
                root(l)
                for g, (c0, n) in enumerate(PROJ):
                    u = at[l, "in"] + 2 * g + 1
                    lead.to(u + 3)
                    act.wait_ge(unit_used, u + 1)
                    act.wait_ge(norm_inv[l], 1)
                    nc.scalar.activation(pj[:, 0, c0:c0 + n], A[2 * (g % 2)][:, :n], ACT.Copy,
                                         scale=st[:, 12:13]).then_inc(proj_act[l], 1)
                for i in range(3):
                    act.wait_ge(lat_T[l], i + 1)
                    for kk in range(2 if i < 2 else 1):
                        k = 2 * i + kk
                        c = l * G_LAYER + G_Q + k
                        nc.scalar.activation(latTh[:, k, :], TB[i][:, kk * SEQ:(kk + 1) * SEQ], ACT.Copy,
                                             scale=gcol[:, c:c + 1]).then_inc(lat_hi[l], 1)
                act.wait_ge(proj_act[l], 3)
                act.wait_ge(proj_dve[l], 3)
                for b in range(NB):
                    done(nc.scalar.activation(xn[:, b, 0:Q_LORA], pj[:, b, 0:Q_LORA], ACT.Square,
                                              accum_out=st[:, 4 + b:5 + b]))
                    done(nc.scalar.activation(xn[:, b, Q_LORA:C_KR], pj[:, b, C_KV:C_KR], ACT.Square,
                                              accum_out=st[:, 6 + b:7 + b]))
                act.wait_ge(act_own, own[0])
                nc.scalar.activation(st[:, 8:10], st[:, 4:6], ACT.Sqrt, scale=1.0 / Q_LORA, bias=eps[:]
                                     ).then_inc(lat_root[l], 1)
                nc.scalar.activation(st[:, 10:12], st[:, 6:8], ACT.Sqrt, scale=1.0 / KV_LORA, bias=eps[:]
                                     ).then_inc(lat_root[l], 1)
                for r in range(2):
                    nc.scalar.activation(kdup[:, :, :, r, :],
                                         pj[:, :, C_KS:C_VS].rearrange("p b (k d) -> p b k d", k=SW_KV),
                                         ACT.Copy).then_inc(kdup_done[l], 1)
                lead.to(at[l, "gate0"] + 4)
                act.wait_ge(win_T[l], 1)
                nc.scalar.activation(sqT[:, 0:2, :].rearrange("p h t -> p (h t)"), T[0][:], ACT.Copy,
                                     scale=SWA_SCALE).then_inc(win_act[l], 1)
                act.wait_ge(win_T[l], 3)
                nc.scalar.activation(skT[:].rearrange("p h t -> p (h t)"), DN[1][:], ACT.Copy
                                     ).then_inc(win_act[l], 1)
                act.wait_ge(lat_inv[l], 1)
                for i in range(2):
                    u = at[l, "q"] + i
                    lead.to(u + 3)
                    act.wait_ge(unit_used, u + 1)
                    nc.scalar.activation(qn[:, 0, 4 * i:4 * i + 4, :], [A, DN][i][0][:, :4 * QK], ACT.Copy,
                                         scale=st[:, 4:5]).then_inc(up_act[l], 1)
                lead.to(at[l, "kv"] + 3)
                act.wait_ge(unit_used, at[l, "kv"] + 1)
                for n in range(2):
                    kv = A[n][:].rearrange("p (h c) -> p h c", h=4)
                    nc.scalar.activation(kn[:, 0, 4 * n:4 * n + 4, 0:NOPE], kv[:, :, 0:NOPE], ACT.Copy,
                                         scale=st[:, 6:7]).then_inc(up_act[l], 1)
                    nc.scalar.activation(vm(0, n), kv[:, :, NOPE:], ACT.Copy, scale=st[:, 6:7]
                                         ).then_inc(up_act[l], 1)
                for i in range(0, QT_FILLS, 2):
                    act.wait_ge(qk_T[l], i + 1)
                    dst, p, w, scale = qk_target(i)
                    nc.scalar.activation(dst, QB[i % 4][0:p, 0:w], ACT.Copy, scale=scale).then_inc(qk_act[l], 1)

                def exps(f):
                    kind, b, heads = FILLS[f]
                    w = P * (b + 1)
                    act.wait_ge(max_ready[l], f + 1)
                    if f >= 2 and kind == 0:
                        act.wait_ge(probs_T[l], f - 1)
                    for i, h in enumerate(heads):
                        s = sx[:, f % 2, i * w:(i + 1) * w]
                        scores = s if kind else A[f % 2][:, i * w:(i + 1) * w]
                        nc.scalar.activation(s, scores, ACT.Exp, bias=nm[:, f % 2, i:i + 1],
                                             accum_out=sums[:, kind, b, h:h + 1]).then_inc(exp_done[l], 1)
                    if kind and f in LAST:
                        nc.scalar.activation(sink_e[:, b, :], sink_d[:, b, :], ACT.Exp).then_inc(sink_done[l], 1)

                def probs_out(f):
                    act.wait_ge(probs_T[l], f + 1)
                    if f >= 2:
                        act.wait_ge(pv_done[l], f - 1)
                    nc.scalar.activation(pT[:, f % 2, :], T[f % 2][:], ACT.Copy).then_inc(probs_T_out[l], 1)

                def o_high(i):
                    kind, b = i // NB, i % NB
                    act.wait_ge(o_T[l], i + 1)
                    nc.scalar.activation(oTh[:, kind, :, b * P:(b + 1) * P],
                                         DN[b][:].rearrange("p (j t) -> p j t", j=4), ACT.Copy
                                         ).then_inc(o_hi[l], 1)

                for f in range(NF):
                    exps(f)
                    if f:
                        probs_out(f - 1)
                    lead.to(at[l, "gate"] + f // 2 + 3)
                    if f - 3 in LAST:
                        o_high(LAST.index(f - 3))
                    if f == 0:
                        act.wait_ge(gate_added[l], 2)
                        bias_chunk(l, 2)
                    if f == 4:
                        act.wait_ge(gate_added[l], 4)
                        bias_chunk(l, 3)
                lead.to(at[l, "br"] + 3)
                probs_out(NF - 1)
                if l == 1:
                    act.wait_ge(router_landed, 16)
                    nc.scalar.activation(wrh[:], wr[:], ACT.Copy).then_inc(wr_hi, 1)
                for n in range(2):
                    if n:
                        o_high(3)
                    act.wait_ge(gate_added[l], 6 + 2 * n)
                    for b in range(NB):
                        for h in range(2):
                            g = gates[:, 2 * h + n, b, :]
                            nc.scalar.activation(g, g, ACT.Sigmoid).then_inc(gate_ready[l], 1)
                for i in range(4):
                    lead.to(at[l, "out"] + (1 if i < 2 else 3))
                    act.wait_ge(mg_T[l], i + 1)
                    nc.scalar.activation(hTh[:, 2 * i:2 * i + 2, :], MB[i][:].rearrange("p (k t) -> p k t", k=2),
                                         ACT.Copy).then_inc(mg_hi[l], 1)
                lead.to(at[l, "ffn"] + 2)
                norm_high(2 + l, l * G_LAYER + G_FFN)
                root(2 + l)
                if l == 0:
                    lead.to(at[0, "ffn"] + 4)
                    act.wait_ge(norm_inv[2], 1)
                if l == 0:
                    u0 = at[0, "ffn"]
                    for j in range(DG + 1):
                        n = min(N, FF - j * N)
                        u = u0 + group_at(j)
                        lead.to(u + (4 if j < DG else 1))
                        if j < DG:
                            act.wait_ge(unit_used, u + 2)
                            for b in range(NB):
                                if j:
                                    act.wait_ge(ff_ready[0], NB * (j - 1) + b + 1)
                                nc.scalar.activation(sg[:, b, :n], A[b][:, :n], ACT.Silu, scale=st[:, 12 + b:13 + b]
                                                     ).then_inc(silu_done[0], 1)
                        if j:
                            m = min(N, FF - (j - 1) * N)
                            for b in range(NB):
                                q = NB * (j - 1) + b
                                act.wait_ge(ff_T[0], q + 1)
                                nc.scalar.activation(aTh[:, b, :m // P, :],
                                                     turned(j, b)[:, :m].rearrange("p (k t) -> p k t", t=P),
                                                     ACT.Copy).then_inc(ff_hi[0], 1)

            first = Lead(act, split_hi, UM, UM + S)
            first.to(UM + 1)
            act.wait_ge(logits_done, 1)
            nc.scalar.activation(lgT[0:NE, :], A[0][0:NE, :SEQ], ACT.Copy).then_inc(logits_out, 1)
            act.wait_ge(lmax_ready, 1)
            for b in range(NB):
                nc.scalar.activation(pe8[:, b, :], lg[:, b, :], ACT.Exp, bias=lmax[:, b:b + 1]
                                     ).then_inc(lexp_done, 1)
            first.to(UM + S)

            def tokens_high(i, n, e):
                act.wait_ge(gathered, 2 * n + i + 1 + e * 2)
                for kk in range(4):
                    k = 4 * i + kk
                    c = G_LAYER + G_FFN + k
                    nc.scalar.activation(heTh[:, k, :], T[i][:, kk * P:(kk + 1) * P], ACT.Copy,
                                         scale=gcol[:, c:c + 1]).then_inc(he_hi, 1)

            def expert(base, n, e, following):
                ahead = Lead(act, split_hi, base, base + EU + (S if following else 0), e)
                ahead.next += S
                for j in range(EG + 1):
                    u = base + group_at(j)
                    ahead.to(u + (4 if j < EG else 2))
                    if j < EG:
                        act.wait_ge(unit_used, u + 2 + e * EU)
                        if j >= 2:
                            act.wait_ge(ff_ready[1], EG * n + j - 1 + e * EG)
                        nc.scalar.activation(sg[:, j % 2, :], A[j % 2][:], ACT.Silu).then_inc(silu_done[1], 1)
                    ahead.to(u + (5 if j < EG else 2))
                    if j:
                        act.wait_ge(ff_T[1], EG * n + j + e * EG)
                        nc.scalar.activation(aTh[:, (j - 1) % 2], T[(j - 1) % 2][:].rearrange("p (k t) -> p k t", k=4),
                                             ACT.Copy).then_inc(ff_hi[1], 1)
                    if j == 1:
                        act.wait_ge(cw_T, n + 1 + e)
                        nc.scalar.activation(cwT[:], T[1][:, :SEQ], ACT.Copy).then_inc(cw_out, 1)
                    if following and j >= EG - 1:
                        if j < EG:
                            ahead.to(u + 6)
                        tokens_high(j - EG + 1, n + 1, e)
                ahead.to(base + EU + S)
                act.wait_ge(unit_used, base + EU + e * EU)
                nc.scalar.activation(oe[:, 0:N], DN[0][:], ACT.Copy).then_inc(oe_act, 1)

            def head(n, e):
                for i in range(2):
                    tokens_high(i, n, e)

            head(0, 0)
            with act.Fori(0, NE - 1) as e:
                expert(UM, 0, e, True)
            act.wait_ge(routed, 1)
            more = act.value_load(flag[0:1, 0:1], min_val=0, max_val=1)
            expert(UM + (NE - 1) * EU, NE - 1, 0, False)
            with act.If(more > 0):
                with act.Fori(0, NE) as e:
                    split_head(UM + NE * EU, e)
                    head(NE, e)
                    expert(UM + NE * EU, NE, e, False)
            nc.scalar.activation(st[:, 14:15], eps[:], ACT.Sqrt)
            for b in range(NB):
                act.wait_ge(last_added, 2 * b + 2)
                v = done(nc.scalar.activation(xn[:, b, :], xs[:, b, :], ACT.Square, accum_out=st[:, b:b + 1]))
                act.wait_ge(act_own, v)
                nc.scalar.activation(st[:, 2 + b:3 + b], st[:, b:b + 1], ACT.Sqrt, scale=1.0 / D, bias=eps[:]
                                     ).then_inc(norm_root[4], 1)

        @block.vector
        def _(dve):
            own = [0]

            def done(ins):
                own[0] += 1
                ins.then_inc(dve_own, 1)
                return own[0]

            def settle():
                dve.wait_ge(dve_own, own[0])

            lead = Lead(dve, split_lo, 0, UM)

            def invert(n):
                dve.wait_ge(norm_root[n], 1)
                nc.vector.reciprocal(st[:, 12:14], st[:, 2:4]).then_inc(norm_inv[n], 1)
                dve.wait_ge(norm_inv[n], 1)

            def norm_low(n, gains, fills=range(4)):
                for i in fills:
                    dve.wait_ge(norm_hi[n], 2 * i + 2)
                    for kk in range(2):
                        k = 2 * i + kk
                        nc.vector.scalar_tensor_tensor(
                            hTl[:, k, :], TB[i][:, kk * SEQ:(kk + 1) * SEQ], gcol[:, gains + k:gains + k + 1],
                            hTh[:, k, :].bitcast(F32), ALU.mult, ALU.subtract).then_inc(norm_lo[n], 1)

            nc.vector.memset(ones[:], 1.0).then_inc(ones_set, 1)
            nc.vector.memset(eps[:], EPS).then_inc(ones_set, 1)
            for l in range(DEPTH):
                if l == 0:
                    dve.wait_ge(gain_done, 1)
                if l:
                    norm_low(1, G_LAYER + G_ATTN)
                else:
                    norm_low(0, G_ATTN, range(2))
                    lead.to(1)
                    norm_low(0, G_ATTN, range(2, 4))
                lead.to(at[l, "in"] + 2)
                invert(l)
                for g, (c0, n) in enumerate(PROJ):
                    u = at[l, "in"] + 2 * g + 1
                    lead.to(u + 3)
                    dve.wait_ge(unit_used, u + 1)
                    nc.vector.tensor_scalar(pj[:, 1, c0:c0 + n], A[2 * (g % 2) + 1][:, :n], st[:, 13:14], None,
                                            ALU.mult).then_inc(proj_dve[l], 1)
                for i in range(3):
                    dve.wait_ge(lat_hi[l], min(2 * i + 2, KQ + KKV))
                    for kk in range(2 if i < 2 else 1):
                        k = 2 * i + kk
                        c = l * G_LAYER + G_Q + k
                        nc.vector.scalar_tensor_tensor(
                            latTl[:, k, :], TB[i][:, kk * SEQ:(kk + 1) * SEQ], gcol[:, c:c + 1],
                            latTh[:, k, :].bitcast(F32), ALU.mult, ALU.subtract).then_inc(lat_lo[l], 1)
                dve.wait_ge(proj_act[l], 3)
                dve.wait_ge(proj_dve[l], 3)

                def rope(x1, x2, cos, sin, t, o1, o2, outs):
                    done(nc.vector.tensor_tensor(t[0], x1, cos, ALU.mult))
                    done(nc.vector.tensor_tensor(t[1], x2, sin, ALU.mult))
                    done(nc.vector.tensor_tensor(t[2], x1, sin, ALU.mult))
                    done(nc.vector.tensor_tensor(t[3], x2, cos, ALU.mult))
                    settle()
                    nc.vector.tensor_tensor(o1, outs(t[0]), outs(t[1]), ALU.subtract).then_inc(rope_done[l], 1)
                    nc.vector.tensor_tensor(o2, outs(t[2]), outs(t[3]), ALU.add).then_inc(rope_done[l], 1)

                cos = cst[:, K_COS:K_SIN].rearrange("p (b r) -> p b r", b=NB)
                sin = cst[:, K_SIN:K_DIST].rearrange("p (b r) -> p b r", b=NB)
                kr = pj[:, :, C_KR:C_QS]
                tk = [krt[:, i].rearrange("p (b r) -> p b r", b=NB) for i in range(4)]

                def heads_of(a):
                    return a.unsqueeze(2).broadcast_to([P, NB, HEADS, HALF])

                rope(kr[:, :, :HALF], kr[:, :, HALF:], cos, sin, tk, kn[:, :, :, NOPE:NOPE + HALF],
                     kn[:, :, :, NOPE + HALF:], heads_of)
                dve.wait_ge(lat_root[l], 2)
                nc.vector.reciprocal(st[:, 4:8], st[:, 8:12]).then_inc(lat_inv[l], 1)
                dve.wait_ge(lat_inv[l], 1)

                def gate_add(g):
                    u = at[l, "gate0"] + 1 if g == 0 else at[l, "gate"] + 2 * g - 1
                    dve.wait_ge(unit_used, u + 1)
                    dve.wait_ge(bg_landed[g % 2], 16 * (2 * l + g // 2 + 1))
                    for b in range(NB):
                        nc.vector.scalar_tensor_tensor(gates[:, g, b, :], A[2 + b][:], st[:, 12 + b:13 + b],
                                                       bg[:, g % 2, :], ALU.mult, ALU.add
                                                       ).then_inc(gate_added[l], 1)

                lead.to(at[l, "gate0"] + 4)
                gate_add(0)
                dve.wait_ge(win_T[l], 2)
                nc.vector.tensor_scalar(sqT[:, 2:4, :].rearrange("p h t -> p (h t)"), T[1][:], SWA_SCALE, None,
                                        ALU.mult).then_inc(win_dve[l], 1)
                for i in range(2):
                    u = at[l, "q"] + i
                    lead.to(u + 3)
                    dve.wait_ge(unit_used, u + 1)
                    nc.vector.tensor_scalar(qn[:, 1, 4 * i:4 * i + 4, :], [A, DN][i][1][:, :4 * QK].rearrange(
                        "p (h c) -> p h c", h=4), st[:, 5:6], None, ALU.mult).then_inc(up_dve[l], 1)
                dve.wait_ge(up_act[l], 2)
                dve.wait_ge(up_dve[l], 2)
                tq = [rt[:, i].rearrange("p (b h r) -> p b h r", b=NB, h=HEADS) for i in range(4)]
                x1, x2 = qn[:, :, :, NOPE:NOPE + HALF], qn[:, :, :, NOPE + HALF:]
                rope(x1, x2, heads_of(cos), heads_of(sin), tq, x1, x2, lambda a: a)
                lead.to(at[l, "kv"] + 3)
                dve.wait_ge(unit_used, at[l, "kv"] + 1)
                for n in range(2):
                    kv = KV[1][n][:].rearrange("p (h c) -> p h c", h=4)
                    nc.vector.tensor_scalar(kn[:, 1, 4 * n:4 * n + 4, 0:NOPE], kv[:, :, 0:NOPE], st[:, 7:8], None,
                                            ALU.mult).then_inc(up_dve[l], 1)
                    nc.vector.tensor_scalar(vm(1, n), kv[:, :, NOPE:], st[:, 7:8], None, ALU.mult
                                            ).then_inc(up_dve[l], 1)
                for i in range(1, QT_FILLS, 2):
                    dve.wait_ge(qk_T[l], i + 1)
                    dst, p, w, scale = qk_target(i)
                    nc.vector.tensor_scalar(dst, QB[i % 4][0:p, 0:w], scale, None, ALU.mult).then_inc(qk_dve[l], 1)

                def mask_max(f):
                    kind, b, heads = FILLS[f]
                    nh, w, off = len(heads), P * (b + 1), P * (1 - b)
                    dve.wait_ge(scored[l], f + 1)
                    s = sx[:, f % 2, :].rearrange("p (h k) -> p h k", h=nh)
                    sc = A[f % 2][:].rearrange("p (h k) -> p h k", h=nh)
                    neg = nm[:, f % 2, :nh]
                    if kind == 0:
                        nc.vector.tensor_reduce(neg, sc, AX, ALU.max, negate=True).then_inc(max_ready[l], 1)
                    else:
                        dve.wait_ge(probs_T[l], f - 1)
                        tab = cst[:, K_DIST + off:K_DIST + SEQ]
                        for i, h in enumerate(heads):
                            last = nc.vector.scalar_tensor_tensor(s[:, i], tab, -SLOPES[h], sc[:, i], ALU.mult, ALU.add)
                            if i < nh - 1:
                                done(last)
                        last.then_inc(masked[l], 1)
                        dve.wait_ge(masked[l], f + 1 - MLA_FILLS)
                        settle()
                        done(nc.vector.tensor_reduce(neg, s, AX, ALU.max, negate=True))
                        settle()
                        sink = slice(heads[0], heads[-1] + 1, 2)
                        done(nc.vector.tensor_tensor(neg, neg, sk_neg[:, l, sink], ALU.min))
                        settle()
                        nc.vector.tensor_tensor(sink_d[:, b, sink], sk[:, l, sink], neg, ALU.add
                                                ).then_inc(max_ready[l], 1)

                def o_scale(i):
                    kind, b = i // NB, i % NB
                    sm = sums[:, kind, b, :]
                    dve.wait_ge(exp_done[l], EXPS[LAST[i]])
                    if kind:
                        dve.wait_ge(sink_done[l], b + 1)
                        done(nc.vector.tensor_tensor(sm, sm, sink_e[:, b, :], ALU.add))
                        settle()
                    done(nc.vector.reciprocal(rsum[:], sm))
                    settle()
                    dve.wait_ge(pv_done[l], LAST[i] + 1)
                    nc.vector.tensor_tensor(on[:].rearrange("p (h d) -> p h d", h=HEADS),
                                            DN[b][:].rearrange("p (h d) -> p h d", h=HEADS),
                                            rsum[:].unsqueeze(2).broadcast_to([P, HEADS, VD]), ALU.mult
                                            ).then_inc(o_scaled[l], 1)

                def o_low(i):
                    kind, b = i // NB, i % NB
                    dve.wait_ge(o_hi[l], i + 1)
                    o = slice(b * P, (b + 1) * P)
                    nc.vector.tensor_tensor(oTl[:, kind, :, o], DN[b][:].rearrange("p (j t) -> p j t", j=4),
                                            oTh[:, kind, :, o].bitcast(F32), ALU.subtract).then_inc(o_lo[l], 1)

                if l == 0:
                    dve.wait_ge(sink_landed, 16)
                    nc.vector.tensor_scalar(sk_neg[:], sk[:], -1.0, None, ALU.mult).then_inc(sink_negated, 1)
                    dve.wait_ge(sink_negated, 1)
                mask_max(0)
                for f in range(NF):
                    if f + 1 < NF:
                        mask_max(f + 1)
                    if f - 2 in LAST:
                        o_scale(LAST.index(f - 2))
                    lead.to(at[l, "gate"] + f // 2 + 3)
                    if f in (2, 6, 10):
                        gate_add((f + 2) // 4)
                    if f - 3 in LAST:
                        o_low(LAST.index(f - 3))
                lead.to(at[l, "br"] + 3)
                o_scale(3)
                def merged_low(half):
                    for i in range(2 * half, 2 * half + 2):
                        lead.to(at[l, "out"] + (1 if i < 2 else 3))
                        dve.wait_ge(mg_hi[l], i + 1)
                        nc.vector.tensor_tensor(hTl[:, 2 * i:2 * i + 2, :],
                                                MB[i][:].rearrange("p (k t) -> p k t", k=2),
                                                hTh[:, 2 * i:2 * i + 2, :].bitcast(F32), ALU.subtract
                                                ).then_inc(mg_lo[l], 1)

                for kind in range(2):
                    for n in range(2):
                        if kind == 0 and n == 1:
                            o_low(3)
                        if l == 1 and kind == n == 0:
                            dve.wait_ge(wr_hi, 1)
                            nc.vector.tensor_tensor(wrl[:], wr[:], wrh[:].bitcast(F32), ALU.subtract
                                                    ).then_inc(wr_lo, 1)
                        u = at[l, "br"] + 2 * kind + n
                        lead.to(u + (2 if kind else 3))
                        dve.wait_ge(unit_used, u + 1)
                        dve.wait_ge(gate_ready[l], 4 * n + 4)
                        c = slice(n * N, (n + 1) * N)
                        for b in range(NB):
                            g = gates[:, 2 * kind + n, b, :]
                            nc.vector.tensor_tensor(g if kind else mg[:, b, c], BR[kind][n][b][:], g, ALU.mult
                                                    ).then_inc(gated[l], 1)
                        if kind:
                            dve.wait_ge(gated[l], 4 + 2 * (n + 1))
                            for b in range(NB):
                                nc.vector.tensor_tensor(mg[:, b, c], mg[:, b, c], gates[:, 2 + n, b, :], ALU.add
                                                        ).then_inc(merged[l], 1)
                            merged_low(n)
                for n in range(2):
                    u = at[l, "out"] + 2 + n
                    lead.to(u + 3)
                    dve.wait_ge(unit_used, u + 1)
                    for b in range(NB):
                        c = xs[:, b, n * N:(n + 1) * N]
                        nc.vector.tensor_tensor(c, OUT[n][b][:], c, ALU.add).then_inc(x_added[l], 1)
                norm_low(2 + l, l * G_LAYER + G_FFN)
                invert(2 + l)
                if l == 0:
                    u0 = at[0, "ffn"]
                    for j in range(DG + 1):
                        n = min(N, FF - j * N)
                        u = u0 + group_at(j)
                        lead.to(u + (4 if j < DG else 1))
                        if j:
                            m = min(N, FF - (j - 1) * N)
                            for b in range(NB):
                                dve.wait_ge(ff_hi[0], NB * (j - 1) + b + 1)
                                nc.vector.tensor_tensor(aTl[:, b, :m // P, :],
                                                        turned(j, b)[:, :m].rearrange("p (k t) -> p k t", t=P),
                                                        aTh[:, b, :m // P, :].bitcast(F32), ALU.subtract
                                                        ).then_inc(ff_lo[0], 1)
                        if j < DG:
                            lead.to(u + 6)
                            dve.wait_ge(unit_used, u + 4)
                            for b in range(NB):
                                dve.wait_ge(silu_done[0], NB * j + b + 1)
                                if j:
                                    dve.wait_ge(ff_T[0], NB * j)
                                nc.vector.scalar_tensor_tensor(av[:, b, :n], A[2 + b][:, :n], st[:, 12 + b:13 + b],
                                                               sg[:, b, :n], ALU.mult, ALU.mult
                                                               ).then_inc(ff_ready[0], 1)
                        if 0 < j < DG:
                            lead.to(u0 + down_at(j - 1, DG) + (4 if j < DG - 1 else 3))
                        for g in {0: [], DG - 1: [], DG: [DG - 1, DG]}.get(j, [j]):
                            if g == DG:
                                lead.to(at[1, "in"] + 1)
                            for i, (b, h, bank) in enumerate(down_order(g)):
                                if i == 3:
                                    dve.wait_ge(unit_used, u0 + down_at(g - 1, DG) + (2 if g < DG else m // SEQ))
                                else:
                                    dve.wait_ge(down_done, 3 * (g - 1) + i + 1)
                                c = xs[:, b, h * N:(h + 1) * N]
                                dve.wait_ge(x_added[0], 4 * g)
                                nc.vector.tensor_tensor(c, bank[:], c, ALU.add).then_inc(x_added[0], 1)
                    dve.wait_ge(x_added[0], X_DENSE)

            for b in range(NB):
                nc.vector.tensor_scalar(xn[:, b, :], xs[:, b, :], st[:, 12 + b:13 + b], None, ALU.mult
                                        ).then_inc(rows_ready, 1)
            first = Lead(dve, split_lo, UM, UM + S)
            first.to(UM + 1)
            dve.wait_ge(logits_T, 1)
            for b in range(NB):
                done(nc.vector.tensor_scalar(lg[:, b], A[1][:, b * NE:(b + 1) * NE], st[:, 12 + b:13 + b], None,
                                             ALU.mult))
            settle()
            done(nc.vector.tensor_reduce(lmax[:], lg[:], AX, ALU.max))
            settle()
            nc.vector.tensor_scalar(lmax[:], lmax[:], -1.0, None, ALU.mult).then_inc(lmax_ready, 1)
            for b in range(NB):
                other = lg[:, b].unsqueeze(1).broadcast_to([P, NE, NE])
                this = lg[:, b].unsqueeze(2).broadcast_to([P, NE, NE])
                done(nc.vector.tensor_tensor(above[:, b], other, this, ALU.is_gt))
                done(nc.vector.tensor_tensor(ties[:, b], other, this, ALU.is_equal))
            settle()
            lower = cst[:, K_LOWER:K_ALL].rearrange("p (e f) -> p e f", e=NE)
            for b in range(NB):
                done(nc.vector.tensor_tensor(ties[:, b], ties[:, b], lower, ALU.mult))
            settle()
            done(nc.vector.tensor_tensor(above[:], above[:], ties[:], ALU.add))
            settle()
            done(nc.vector.tensor_reduce(rank[:], above[:], AX, ALU.add))
            settle()
            nc.vector.tensor_scalar(mask[:], rank[:], 2.0, None, ALU.is_lt).then_inc(mask_ready, 1)
            dve.wait_ge(mask_ready, 1)
            dve.wait_ge(lexp_done, NB)
            done(nc.vector.tensor_tensor(pe8[:], pe8[:], mask[:], ALU.mult))
            settle()
            done(nc.vector.tensor_reduce(psum8[:], pe8[:], AX, ALU.add))
            settle()
            done(nc.vector.reciprocal(psum8[:], psum8[:]))
            settle()
            done(nc.vector.tensor_tensor(comb[:], pe8[:], psum8[:].unsqueeze(2).broadcast_to([P, NB, NE]), ALU.mult))
            dve.wait_ge(counted, 1)
            cnt = A[2][:, :NB * NE].rearrange("p (b e) -> p b e", b=NB)
            done(nc.vector.scalar_tensor_tensor(pos[:], cnt, 1.0, mask[:], ALU.add, ALU.mult))
            done(nc.vector.tensor_reduce(most[:], A[2][:, NB * NE:NB * NE + NE], AX, ALU.max))
            settle()
            done(nc.vector.tensor_scalar(pos[:], pos[:], -1.0, None, ALU.add))
            nc.vector.tensor_scalar(flag[:], most[:], float(P), None, ALU.is_gt).then_inc(routed, 1)
            settle()

            def select(turn, n, e, col):
                nc.vector.tensor_copy(posc[:], pos[:, :, bass.ds(col, 1)].rearrange("p b a -> p (b a)")
                                      ).then_inc(selected, 1)
                nc.vector.tensor_copy(combc[:], comb[:, :, bass.ds(col, 1)].rearrange("p b a -> p (b a)")
                                      ).then_inc(selected, 1)
                dve.wait_ge(selected, 2 * n + 2 + e * 2)
                rank_of = cst[:, K_IOTA + turn * P:K_IOTA + (turn + 1) * P]
                for b in range(NB):
                    nc.vector.tensor_scalar(pick[:, b], rank_of, posc[:, b:b + 1], None, ALU.is_equal
                                            ).then_inc(picked, 1)
                    nc.vector.tensor_scalar(cw[:, b], rank_of, posc[:, b:b + 1], combc[:, b:b + 1], ALU.is_equal,
                                            ALU.mult).then_inc(picked, 1)

            def tokens_low(i, n, e):
                dve.wait_ge(he_hi, 8 * n + 4 * i + 4 + e * 8)
                for kk in range(4):
                    k = 4 * i + kk
                    c = G_LAYER + G_FFN + k
                    nc.vector.scalar_tensor_tensor(
                        heTl[:, k, :], T[i][:, kk * P:(kk + 1) * P], gcol[:, c:c + 1],
                        heTh[:, k, :].bitcast(F32), ALU.mult, ALU.subtract).then_inc(he_lo, 1)

            def add_spread(b, full, value, added):
                for h in range(2):
                    dve.wait_ge(full, value + h)
                    c = xs[:, b, h * N:(h + 1) * N]
                    nc.vector.tensor_tensor(c, DN[h][:], c, ALU.add).then_inc(added, 1)

            def expert(base, n, e, following):
                ahead = Lead(dve, split_lo, base, base + EU + (S if following else 0), e)
                ahead.next += S
                for j in range(EG + 1):
                    u = base + group_at(j)
                    ahead.to(u + (4 if j < EG else 2))
                    if j == 0:
                        add_spread(0, oe_full, 4 * n + 1 + e * 4, x_added[1])
                    if j:
                        dve.wait_ge(ff_hi[1], EG * n + j + e * EG)
                        nc.vector.tensor_tensor(aTl[:, (j - 1) % 2], T[(j - 1) % 2][:].rearrange("p (k t) -> p k t", k=4),
                                                aTh[:, (j - 1) % 2].bitcast(F32), ALU.subtract).then_inc(ff_lo[1], 1)
                    if following and j == EG - 2:
                        select(0, n + 1, e, e + 1)
                    if j < EG:
                        ahead.to(u + 6)
                        dve.wait_ge(unit_used, u + 4 + e * EU)
                        dve.wait_ge(silu_done[1], EG * n + j + 1 + e * EG)
                        nc.vector.tensor_tensor(av[:, j % 2], A[2 + j % 2][:], sg[:, j % 2], ALU.mult
                                                ).then_inc(ff_ready[1], 1)
                    if j == 0:
                        add_spread(1, oe_full, 4 * n + 3 + e * 4, x_added[1])
                    if following and j >= EG - 1:
                        tokens_low(j - EG + 1, n + 1, e)
                ahead.to(base + EU + S)
                dve.wait_ge(unit_used, base + EU + e * EU)
                nc.vector.tensor_copy(oe[:, N:], DN[1][:]).then_inc(oe_dve, 1)

            def head(turn, base, n, e, splits):
                select(turn, n, e, e)
                splits.to(base + S)
                for i in range(2):
                    tokens_low(i, n, e)

            head(0, UM, 0, 0, first)
            with dve.Fori(0, NE - 1) as e:
                expert(UM, 0, e, True)
            more = dve.value_load(flag[0:1, 0:1], min_val=0, max_val=1)
            expert(UM + (NE - 1) * EU, NE - 1, 0, False)
            with dve.If(more > 0):
                with dve.Fori(0, NE) as e:
                    head(1, UM + NE * EU, NE, e, Lead(dve, split_lo, UM + NE * EU, UM + NE * EU + S, e))
                    expert(UM + NE * EU, NE, e, False)
            for b in range(NB):
                add_spread(b, last_full, 2 * b + 1, last_added)
            dve.wait_ge(gfin_landed, 16)
            for b in range(NB):
                dve.wait_ge(norm_root[4], b + 1)
                nc.vector.reciprocal(st[:, 12 + b:13 + b], st[:, 2 + b:3 + b]).then_inc(norm_inv[4], 1)
                dve.wait_ge(norm_inv[4], b + 1)
                nc.vector.scalar_tensor_tensor(gout[:, b, :], xs[:, b, :], st[:, 12 + b:13 + b], gfin[:],
                                               ALU.mult, ALU.mult).then_inc(rows_ready, 1)

        @block.tensor
        def _(pe):
            def turn_x(n, x_there, halves):
                for i in range(4):
                    if i % 2 == 0:
                        pe.wait_ge(x_there, halves[i // 2])
                    for kk in range(2):
                        for b in range(NB):
                            k = 2 * i + kk
                            last = nc.tensor.transpose(TB[i][:, (kk * NB + b) * P:(kk * NB + b + 1) * P],
                                                       xs[:, b, k * P:(k + 1) * P], ident)
                    last.then_inc(norm_T[n], 1)

            def block_of(u, b, kt0, kt, total, n, hi, lo, bank):
                if b == 0:
                    pe.wait_ge(lo_done, u + 1)
                for kk in range(kt):
                    k = kt0 + kk
                    wh, wl = split_tile(u, kk, n)
                    last = product(bank[:, :n], hi[:, k, b * P:(b + 1) * P], lo[:, k, b * P:(b + 1) * P],
                                   wh, wl, k == 0, k == total - 1)
                if b == NB - 1:
                    last.then_inc(unit_used, 1)

            def columns(u, kt0, kt, total, n, hi, lo, banks):
                for b in range(NB):
                    block_of(u, b, kt0, kt, total, n, hi, lo, banks[b])

            pe.wait_ge(const_landed, 16)
            pe.wait_ge(gain_landed, 16 * 8)
            nc.tensor.transpose(A[0][:, 0:DEPTH * G_LAYER], grow[0:DEPTH * G_LAYER, :],
                                ident[0:DEPTH * G_LAYER, 0:DEPTH * G_LAYER]).then_inc(gain_T, 1)
            for l in range(DEPTH):
                if l == 0:
                    turn_x(0, x_landed, (16, 16))
                else:
                    turn_x(1, x_added[0], (X_DENSE - 2, X_DENSE))
                for g, (c0, n) in enumerate(PROJ):
                    u = at[l, "in"] + 2 * g
                    if g == 2:
                        pe.wait_ge(proj_act[l], 1)
                        pe.wait_ge(proj_dve[l], 1)
                    for h in range(2):
                        pe.wait_ge(norm_lo[l], 4 * (h + 1))
                        columns(u + h, 4 * h, 4, KD, n, hTh, hTl, A[2 * (g % 2):])
                pe.wait_ge(proj_act[l], 2)
                pe.wait_ge(proj_dve[l], 2)
                for i in range(3):
                    for kk in range(2 if i < 2 else 1):
                        k = 2 * i + kk
                        for b in range(NB):
                            last = nc.tensor.transpose(TB[i][:, (kk * NB + b) * P:(kk * NB + b + 1) * P],
                                                       pj[:, b, k * P:(k + 1) * P], ident)
                    last.then_inc(lat_T[l], 1)
                for h in range(2):
                    columns(at[l, "gate0"] + h, 4 * h, 4, KD, N, hTh, hTl, A[2:])
                pe.wait_ge(lat_lo[l], KQ + KKV)
                pe.wait_ge(proj_act[l], 3)
                pe.wait_ge(proj_dve[l], 3)
                pe.wait_ge(kdup_done[l], 2)
                for i in range(3):
                    for s in range(2):
                        for b in range(NB):
                            c = C_QS + (2 * i + s) * P
                            src = pj[:, b, c:c + P] if i < 2 else kdup[:, b, s].rearrange("p r d -> p (r d)")
                            last = nc.tensor.transpose([T[0], T[1], DN[1]][i][:, (s * NB + b) * P:(s * NB + b + 1) * P],
                                                       src, ident)
                    last.then_inc(win_T[l], 1)
                for i in range(2):
                    if i:
                        pe.wait_ge(win_act[l], 2)
                    columns(at[l, "q"] + i, 0, KQ, KQ, 4 * QK, latTh, latTl, [A, DN][i])
                def half_unit(i):
                    u, b = at[l, "gate"] + i // 2, i % 2
                    if u < at[l, "br"]:
                        if i % 4 == 0:
                            pe.wait_ge(gate_added[l], 2 + i // 2)
                        block_of(u, b, 4 * (u - at[l, "gate"]) % KD, 4, KD, N, hTh, hTl, A[2 + b])
                    else:
                        if b == 0:
                            pe.wait_ge(masked[l], NF - MLA_FILLS)
                            pe.wait_ge(o_lo[l], 2)
                        block_of(u, b, 0, 4, 4, N, oTh[:, 0], oTl[:, 0], BR[0][0][b])

                u = at[l, "kv"]
                pe.wait_ge(lo_done, u + 1)
                pe.wait_ge(up_act[l], 1)
                pe.wait_ge(up_dve[l], 1)
                for b in range(NB):
                    if b:
                        pe.wait_ge(up_act[l], 2)
                        pe.wait_ge(up_dve[l], 2)
                    for n in range(2):
                        for k in range(KKV):
                            wh, wl = split_tile(u, k, D, n * N, N)
                            last = product(KV[b][n][:], latTh[:, KQ + k, b * P:(b + 1) * P],
                                           latTl[:, KQ + k, b * P:(b + 1) * P], wh, wl, k == 0, k == KKV - 1)
                last.then_inc(unit_used, 1)
                half_unit(0)
                for i in range(QT_FILLS):
                    bank = QB[i % 4]
                    if i == 0:
                        pe.wait_ge(rope_done[l], 4)
                        pe.wait_ge(win_act[l], 1)
                        pe.wait_ge(win_dve[l], 1)
                    if i == 2:
                        pe.wait_ge(up_act[l], 6)
                        pe.wait_ge(up_dve[l], 6)
                    if i >= 4:
                        pe.wait_ge([qk_act, qk_dve][i % 2][l], i // 2 - 1)
                    for s in range(2):
                        for b in range(NB):
                            o = (s * NB + b) * P
                            src = (qn if i < 4 else kn)[:, b, 2 * (i % 4) + s, :]
                            last = nc.tensor.transpose(bank[0:QK, o:o + P], src, ident)
                    last.then_inc(qk_T[l], 1)

                def scores(f):
                    kind, b, heads = FILLS[f]
                    w = P * (b + 1)
                    if f >= 2:
                        if FILLS[f - 2][0] == 0:
                            pe.wait_ge(exp_done[l], EXPS[f - 2])
                        else:
                            pe.wait_ge(masked[l], f - 1 - MLA_FILLS)
                    for i, h in enumerate(heads):
                        o = A[f % 2][:, i * w:(i + 1) * w]
                        q = slice(b * P, (b + 1) * P)
                        if kind == 0:
                            last = nc.tensor.matmul(o, qT[0:AUG, h, q], kT[0:AUG, h, 0:w], start=True, stop=True)
                        else:
                            r = slice(SW_D * (h % 2), SW_D * (h % 2) + SW_D)
                            last = nc.tensor.matmul(o, sqT[r, h // 2, q], skT[r, h // 4, 0:w], start=True, stop=True)
                    last.then_inc(scored[l], 1)

                def turn_probs(f):
                    kind, b, heads = FILLS[f]
                    pe.wait_ge(exp_done[l], EXPS[f])
                    if f >= 2:
                        pe.wait_ge(probs_T_out[l], f - 1)
                    for i in range(4):
                        last = nc.tensor.transpose(T[f % 2][:, i * P:(i + 1) * P], sx[:, f % 2, i * P:(i + 1) * P],
                                                   ident)
                    last.then_inc(probs_T[l], 1)

                def values(f):
                    kind, b, heads = FILLS[f]
                    pe.wait_ge(probs_T_out[l], f + 1)
                    if kind and heads[0] == 0:
                        pe.wait_ge(o_lo[l], b + 1)
                    for i, h in enumerate(heads):
                        o = DN[b][:, h * VD:(h + 1) * VD]
                        for kb in range(b + 1):
                            v = pj[:, kb, h * VD:(h + 1) * VD] if kind == 0 else \
                                pj[:, kb, C_VS + SW_D * (h // 4):C_VS + SW_D * (h // 4) + SW_D]
                            c = (i * (b + 1) + kb) * P
                            last = nc.tensor.matmul(o, pT[:, f % 2, c:c + P], v, start=kb == 0, stop=kb == b)
                    last.then_inc(pv_done[l], 1)

                def turn_o(i):
                    pe.wait_ge(o_scaled[l], i + 1)
                    for j in range(4):
                        last = nc.tensor.transpose(DN[i % NB][:, j * P:(j + 1) * P], on[:, j * P:(j + 1) * P], ident)
                    last.then_inc(o_T[l], 1)

                pe.wait_ge(qk_act[l], QT_FILLS - QT_FILLS // 2)
                pe.wait_ge(qk_dve[l], QT_FILLS // 2)

                if l == 0:
                    pe.wait_ge(rows_landed, 32)
                scores(0)
                scores(1)
                half_unit(1)
                for f in range(NF):
                    turn_probs(f)
                    if f + 2 < NF:
                        scores(f + 2)
                    half_unit(f + 2)
                    if f - 2 in LAST:
                        turn_o(LAST.index(f - 2))
                    if f:
                        values(f - 1)
                values(NF - 1)
                def branch(kind, n, b):
                    block_of(at[l, "br"] + 2 * kind + n, b, 0, 4, 4, N, oTh[:, kind], oTl[:, kind], BR[kind][n][b])

                def turn_merged(half):
                    pe.wait_ge(merged[l], NB * (1 + half))
                    for i in range(2 * half, 2 * half + 2):
                        for kk in range(2):
                            for b in range(NB):
                                k = 2 * i + kk
                                last = nc.tensor.transpose(MB[i][:, (kk * NB + b) * P:(kk * NB + b + 1) * P],
                                                           mg[:, b, k * P:(k + 1) * P], ident)
                        last.then_inc(mg_T[l], 1)

                def projected(n, half):
                    pe.wait_ge(mg_lo[l], 2 * half + 2)
                    columns(at[l, "out"] + 2 * half + n, 4 * half, 4, KD, N, hTh, hTl, OUT[n])

                pe.wait_ge(gate_added[l], 8)
                branch(0, 1, 0)
                turn_o(3)
                branch(0, 1, 1)
                pe.wait_ge(o_lo[l], 4)
                branch(1, 0, 0)
                branch(1, 0, 1)
                branch(1, 1, 0)
                turn_merged(0)
                branch(1, 1, 1)
                projected(0, 0)
                turn_merged(1)
                projected(1, 0)
                projected(0, 1)
                projected(1, 1)
                turn_x(2 + l, x_added[l], (2, 4))
                pe.wait_ge(norm_lo[2 + l], 4)
                if l == 0:
                    u0 = at[0, "ffn"]
                    pe.wait_ge(x_added[0], 4)
                    for j in range(DG + 1):
                        n = min(N, FF - j * N)
                        u = u0 + group_at(j)
                        if j < DG:
                            if j:
                                pe.wait_ge(silu_done[0], NB * j)
                            for h in range(2):
                                pe.wait_ge(norm_lo[2], 4 * (h + 1))
                                columns(u + h, 4 * h, 4, KD, n, hTh, hTl, A)
                        if j:
                            m = min(N, FF - (j - 1) * N)
                            if 1 < j < DG:
                                pe.wait_ge(x_added[0], 4 + 4 * (j - 1))
                            if j == DG:
                                pe.wait_ge(ff_ready[0], NB * DG)
                            for b in range(NB):
                                pe.wait_ge(ff_ready[0], NB * (j - 1) + b + 1)
                                for k in range(m // P):
                                    last = nc.tensor.transpose(turned(j, b)[:, k * P:(k + 1) * P], av[:, b, k * P:(k + 1) * P],
                                                               ident)
                                last.then_inc(ff_T[0], 1)
                        if j < DG:
                            if j:
                                pe.wait_ge(ff_ready[0], NB * j)
                            for h in range(2):
                                columns(u + 2 + h, 4 * h, 4, KD, n, hTh, hTl, A[2:])
                        if j:
                            pe.wait_ge(ff_lo[0], NB * j)
                            ud = u0 + down_at(j - 1, DG)
                            kt = m // P
                            for r in range(kt // 2):
                                pe.wait_ge(lo_done, ud + r + 1)
                                for i, (b, h, bank) in enumerate(down_order(j)):
                                    for kk in range(2):
                                        k = 2 * r + kk
                                        wh, wl = split_tile(ud + r, kk, D, h * N, N)
                                        last = product(bank[:], aTh[:, b, k, :], aTl[:, b, k, :], wh, wl,
                                                       k == 0, k == kt - 1)
                                    if i == 3:
                                        last.then_inc(unit_used, 1)
                                    elif k == kt - 1:
                                        last.then_inc(down_done, 1)

            pe.wait_ge(norm_lo[3], KD)
            pe.wait_ge(wr_lo, 1)
            for k in range(KD):
                last = product(A[0][0:NE, :SEQ], wrh[:, k, :], wrl[:, k, :], hTh[:, k, :], hTl[:, k, :],
                               k == 0, k == KD - 1)
            last.then_inc(logits_done, 1)
            pe.wait_ge(logits_out, 1)
            for b in range(NB):
                last = nc.tensor.transpose(A[1][:, b * NE:(b + 1) * NE], lgT[0:NE, b * P:(b + 1) * P],
                                           ident[0:NE, 0:NE])
            last.then_inc(logits_T, 1)
            pe.wait_ge(mask_ready, 1)
            nc.tensor.matmul(A[2][:, 0:NE], before, mask[:, 0, :], start=True, stop=True)
            nc.tensor.matmul(A[2][:, NE:2 * NE], ones[:], mask[:, 0, :], start=True, stop=False)
            nc.tensor.matmul(A[2][:, NE:2 * NE], before, mask[:, 1, :], start=False, stop=True)
            nc.tensor.matmul(A[2][:, 2 * NE:3 * NE], ones[:], mask[:, 0, :], start=True, stop=False)
            nc.tensor.matmul(A[2][:, 2 * NE:3 * NE], ones[:], mask[:, 1, :], start=False, stop=True
                             ).then_inc(counted, 1)
            pe.wait_ge(routed, 1)

            def gather(i, n, e):
                pe.wait_ge(picked, 4 * n + 4 + e * 4)
                for kk in range(4):
                    k = 4 * i + kk
                    for b in range(NB):
                        last = nc.tensor.matmul(T[i][:, kk * P:(kk + 1) * P], xn[:, b, k * P:(k + 1) * P],
                                                pick[:, b], start=b == 0, stop=b == NB - 1)
                last.then_inc(gathered, 1)

            def spread(b, full):
                for h in range(2):
                    nc.tensor.matmul(DN[h][:], cwT[:, b * P:(b + 1) * P], oe[:, h * N:(h + 1) * N],
                                     start=True, stop=True).then_inc(full, 1)

            def expert(base, n, e, following):
                def products(u, h, bank):
                    pe.wait_ge(lo_done, u + 1 + e * EU)
                    for kk in range(4):
                        k = 4 * h + kk
                        wh, wl = split_tile(u, kk, N)
                        last = product(bank[:], heTh[:, k, :], heTl[:, k, :], wh, wl, k == 0, k == KD - 1)
                    last.then_inc(unit_used, 1)

                pe.wait_ge(he_lo, 8 * n + 8 + e * 8)
                for j in range(EG + 1):
                    u = base + group_at(j)
                    if j < EG:
                        if j >= 2:
                            pe.wait_ge(silu_done[1], EG * n + j - 1 + e * EG)
                        for h in range(2):
                            products(u + h, h, A[j % 2])
                    if j == 0:
                        pe.wait_ge(oe_act, n + 1 + e)
                        pe.wait_ge(oe_dve, n + 1 + e)
                        spread(0, oe_full)
                    else:
                        q = (j - 1) % 2
                        pe.wait_ge(ff_ready[1], EG * n + j + e * EG)
                        if j == 2:
                            pe.wait_ge(cw_out, n + 1 + e)
                        if j > 2:
                            pe.wait_ge(ff_lo[1], EG * n + j - 2 + e * EG)
                        if following and j == EG:
                            pe.wait_ge(he_lo, 8 * n + 12 + e * 8)
                        for k in range(4):
                            last = nc.tensor.transpose(T[q][:, k * P:(k + 1) * P], av[:, q, k * P:(k + 1) * P], ident)
                        last.then_inc(ff_T[1], 1)
                    if j == 1:
                        for b in range(NB):
                            last = nc.tensor.transpose(T[1][:, b * P:(b + 1) * P], cw[:, b], ident)
                        last.then_inc(cw_T, 1)
                    if following and j == EG:
                        gather(1, n + 1, e)
                    if j < EG:
                        if j >= 2:
                            pe.wait_ge(ff_ready[1], EG * n + j - 1 + e * EG)
                        for h in range(2):
                            products(u + 2 + h, h, A[2 + j % 2])
                    if j == 0:
                        pe.wait_ge(x_added[1], 4 + 4 * n + 2 + e * 4)
                        spread(1, oe_full)
                    if following and j == EG - 1:
                        pe.wait_ge(ff_lo[1], EG * n + EG - 2 + e * EG)
                        gather(0, n + 1, e)
                    if j:
                        if j == 1:
                            pe.wait_ge(x_added[1], 4 + 4 * n + 4 + e * 4)
                        pe.wait_ge(ff_lo[1], EG * n + j + e * EG)
                        ud = base + down_at(j - 1, EG)
                        for i in range(2):
                            pe.wait_ge(lo_done, ud + i + 1 + e * EU)
                            for kk in range(2):
                                k = 2 * i + kk
                                for h in range(2):
                                    wh, wl = split_tile(ud + i, kk, D, h * N, N)
                                    last = product(DN[h][:], aTh[:, q, k, :], aTl[:, q, k, :], wh, wl,
                                                   j == 1 and k == 0, j == EG and k == 3)
                            last.then_inc(unit_used, 1)

            def head(n, e):
                for i in range(2):
                    gather(i, n, e)

            def output_out(n, e):
                pe.wait_ge(oe_act, n + 1 + e)
                pe.wait_ge(oe_dve, n + 1 + e)

            pe.wait_ge(oe_act, 1)
            pe.wait_ge(oe_dve, 1)
            head(0, 0)
            with pe.Fori(0, NE - 1) as e:
                expert(UM, 0, e, True)
            more = pe.value_load(flag[0:1, 0:1], min_val=0, max_val=1)
            expert(UM + (NE - 1) * EU, NE - 1, 0, False)
            output_out(NE, 0)
            with pe.If(more > 0):
                with pe.Fori(0, NE) as e:
                    head(NE, e)
                    expert(UM + NE * EU, NE, e, False)
                    output_out(NE + 1, e)
            for b in range(NB):
                if b:
                    pe.wait_ge(last_added, 2)
                spread(b, last_full)

        @block.gpsimd
        def _(pool):
            for src, dst in enumerate((qT, kT)):
                pool.dma_start(dst[QK:AUG], mask_rows[:, src:src + 1, :].broadcast_to([NB, HEADS, SEQ])
                               ).then_inc(rows_landed, 16)
            pool.dma_start(sk[:], sinks.rearrange("(a l) h -> a l h", a=1).broadcast_to([P, DEPTH, HEADS])
                           ).then_inc(sink_landed, 16)
            pool.dma_start(wr[:], w_router[0].rearrange("(k p) e -> p k e", p=P)).then_inc(router_landed, 16)
            pool.wait_ge(o_lo[1], 4)
            pool.dma_start(gfin[:], g_final.rearrange("(a d) -> a d", a=1).broadcast_to([P, D])
                           ).then_inc(gfin_landed, 16)
            pool.wait_ge(gfin_landed, 16)
            pool.wait_ge(merged[1], 4)
            nc.gpsimd.memset(oe[:], 0.0).then_inc(oe_act, 1)
            nc.gpsimd.memset(cwT[:], 0.0).then_inc(oe_dve, 1)


_INS = ["x", "g_attn_norm", "w_in", "b_gate", "g_q_norm", "w_q_up", "g_kv_norm", "w_kv_up", "sinks", "w_br_mla",
        "w_br_swa", "w_out", "g_ffn_norm", "dense_w_gate", "dense_w_up", "dense_w_down", "w_router",
        "moe_w_gate", "moe_w_up", "moe_w_down", "g_final"]


def shape_constants():
    import numpy as np

    c = np.zeros((P, K_ALL), np.float32)
    inv = 1.0 / (10000.0 ** (np.arange(0, ROPE, 2, dtype=np.float32) / ROPE))
    ang = np.arange(SEQ, dtype=np.float32)[:, None] * inv[None, :]
    for b in range(NB):
        c[:, K_COS + b * HALF:K_COS + (b + 1) * HALF] = np.cos(ang[b * P:(b + 1) * P])
        c[:, K_SIN + b * HALF:K_SIN + (b + 1) * HALF] = np.sin(ang[b * P:(b + 1) * P])
    q, k = np.arange(P, SEQ)[:, None], np.arange(SEQ)[None, :]
    outside = (k // CHUNK > q // CHUNK) | (k // CHUNK < q // CHUNK - 1)
    c[:, K_DIST:K_IDENT] = np.where(outside, 1e33, np.abs(q - k))
    c[:, K_IDENT:K_BEFORE] = np.eye(P)
    c[:, K_BEFORE:K_IOTA] = np.triu(np.ones((P, P)), 1)
    c[:, K_IOTA:K_LOWER] = np.arange(SEQ)[None, :]
    c[:, K_LOWER:K_ALL] = np.tril(np.ones((NE, NE)), -1).reshape(1, -1)
    return c


def shape_mask_rows():
    import numpy as np

    chunk = np.arange(SEQ) // CHUNK
    r = np.zeros((NB, 2, SEQ), np.float32)
    for b in range(NB):
        r[b, 0] = chunk == 2 * b
        r[b, 1] = np.where(chunk == 2 * b + 1, -1e30, 0.0)
    return r


def kernel(**inputs):
    import numpy as np
    import concourse.bacc as bacc
    from concourse.bass_utils import run_bass_kernel_spmd

    nc = bacc.Bacc("TRN2", target_bir_lowering=False, num_devices=1)
    arrays, args = {}, []
    for name in _INS:
        a = np.ascontiguousarray(inputs[name])
        arrays[f"in_{name}"] = a
        args.append(nc.dram_tensor(f"in_{name}", a.shape, F32, kind="ExternalInput").ap())
    arrays["shape_constants"] = shape_constants()
    args.append(nc.dram_tensor("shape_constants", (P, K_ALL), F32, kind="ExternalInput").ap())
    arrays["shape_mask_rows"] = shape_mask_rows()
    args.append(nc.dram_tensor("shape_mask_rows", (NB, 2, SEQ), F32, kind="ExternalInput").ap())
    args.append(nc.dram_tensor("out", (1, SEQ, D), F32, kind="ExternalOutput").ap())
    trunk(nc, *args)
    r = run_bass_kernel_spmd(nc, [arrays], core_ids=[0])
    return r.results[0]["out"]
```
